# Optimizing a Trainium2 kernel written in Bass

```python
import math
import jax, jax.numpy as jnp
from jax import lax
import numpy as np

D_MODEL = 1024
BATCH = 1
SEQ = 1024
DEPTH = 1
DEC_BATCH = 8
DEC_SEQ = 1
PAST_LEN = 1024
PAGE_SIZE = 128

ATTN_HEADS = 16
ATTN_KV_HEADS = 4
HEAD_DIM = 64
ATTN_GROUP = ATTN_HEADS // ATTN_KV_HEADS
WINDOW = 128
ATTN_BLOCK = WINDOW
REL_BUCKETS = 32
REL_MAX_DIST = 128
RWKV_HEAD = 64
RWKV_HEADS = D_MODEL // RWKV_HEAD
RWKV_DIM = RWKV_HEADS * RWKV_HEAD
LORA_W = 64
LORA_A = 64
LORA_G = 128
RWKV_IN = 3 * RWKV_DIM + LORA_W + LORA_A + LORA_G
Q_DIM = ATTN_HEADS * HEAD_DIM
KV_DIM = ATTN_KV_HEADS * HEAD_DIM
IN_TOTAL = Q_DIM + 2 * KV_DIM + RWKV_IN + 2 * D_MODEL
PEER_HEADS = 8
N_KEYS = 128
N_EXPERTS = N_KEYS * N_KEYS
PEER_TOPK = 16
PEER_KEY_DIM = 128
PEER_HALF = PEER_KEY_DIM // 2
PEER_BLOCK = 128
LN_EPS = 1e-5
GN_EPS = 64e-5
DEEPNORM_ALPHA = (2.0 * DEPTH) ** 0.25
DEEPNORM_BETA = (8.0 * DEPTH) ** -0.25

kernel_name = "hybrid_swa_rwkv7_peer_step"

def layer_norm(x, g, b):
    xf = x.astype(jnp.float32)
    mu = xf.mean(-1, keepdims=True)
    var = jnp.square(xf - mu).mean(-1, keepdims=True)
    y = (xf - mu) * lax.rsqrt(var + LN_EPS) * g.astype(jnp.float32) + b.astype(jnp.float32)
    return y.astype(x.dtype)

def t5_bucket(rel):
    n = jnp.maximum(rel, 0)
    max_exact = REL_BUCKETS // 2
    nf = jnp.maximum(n, max_exact).astype(jnp.float32)
    large = max_exact + (jnp.log(nf / max_exact) / math.log(REL_MAX_DIST / max_exact)
                         * (REL_BUCKETS - max_exact)).astype(jnp.int32)
    large = jnp.minimum(large, REL_BUCKETS - 1)
    return jnp.where(n < max_exact, n, large)

def window_attention(q, k, v, rel, valid, sinks, rel_bias):
    b, n, nq, hk, g, dh = q.shape
    nk = k.shape[2]
    bias = rel_bias.astype(jnp.float32)[t5_bucket(rel)]
    bias = bias.transpose(2, 0, 1).reshape(hk, g, nq, nk)
    s = jnp.einsum("bnqhgd,bnkhd->bnhgqk", q, k).astype(jnp.float32) * (dh ** -0.5) + bias
    s = jnp.where(valid[None, :, None, None], s, -jnp.inf)
    sink = sinks.astype(jnp.float32).reshape(1, 1, hk, g, 1, 1)
    m = jnp.maximum(s.max(-1, keepdims=True), sink)
    p = jnp.exp(s - m)
    probs = p / (p.sum(-1, keepdims=True) + jnp.exp(sink - m))
    o = jnp.einsum("bnhgqk,bnkhd->bnqhgd", probs.astype(v.dtype), v)
    return o.reshape(b, n * nq, hk * g * dh)

def rwkv7_time_mix(feats, shift0, wkv0, mu, w0, w_up, a0, a_up, g_up, k_k, k_a, r_k, lnx_g, lnx_b):
    b, t, _ = feats.shape
    prev = jnp.concatenate([shift0[:, None].astype(feats.dtype), feats[:, :-1]], axis=1)
    f = (feats + (prev - feats) * mu).astype(jnp.float32)
    r, k, v, xw, xa, xg = jnp.split(
        f, [RWKV_DIM, 2 * RWKV_DIM, 3 * RWKV_DIM, 3 * RWKV_DIM + LORA_W, 3 * RWKV_DIM + LORA_W + LORA_A], axis=-1)
    w_log = -jax.nn.softplus(-(w0 + jnp.tanh(xw) @ w_up)) - 0.5
    decay = jnp.exp(-jnp.exp(w_log))
    a = jax.nn.sigmoid(a0 + xa @ a_up)
    g = jax.nn.sigmoid(xg) @ g_up
    hs = lambda u: u.reshape(b, t, RWKV_HEADS, RWKV_HEAD)
    kk = hs(k * k_k)
    kk = kk * lax.rsqrt(jnp.maximum(jnp.sum(kk * kk, -1, keepdims=True), 1e-24))
    k = k * (1.0 + (a - 1.0) * k_a)
    tm = lambda u: jnp.swapaxes(u, 0, 1)
    xs = (tm(hs(r)), tm(hs(decay)), tm(hs(k)), tm(hs(v)), tm(kk), tm(kk * hs(a)))

    def step(S, inp):
        r_t, w_t, k_t, v_t, kk_t, kka_t = inp
        sa = jnp.einsum("bhvk,bhk->bhv", S, kk_t)
        S = S * w_t[:, :, None, :] - sa[..., None] * kka_t[:, :, None, :] + v_t[..., None] * k_t[:, :, None, :]
        return S, jnp.einsum("bhvk,bhk->bhv", S, r_t)

    s_final, ys = lax.scan(step, wkv0.astype(jnp.float32), xs)
    y = jnp.swapaxes(ys, 0, 1)
    mu_y = y.mean(-1, keepdims=True)
    var_y = jnp.square(y - mu_y).mean(-1, keepdims=True)
    y = ((y - mu_y) * lax.rsqrt(var_y + GN_EPS)).reshape(b, t, RWKV_DIM) * lnx_g + lnx_b
    bonus = (jnp.sum(hs(r * k * r_k), -1, keepdims=True) * hs(v)).reshape(b, t, RWKV_DIM)
    out = (y + bonus) * g
    return out.astype(feats.dtype), feats[:, -1], s_final

def peer(h, peer_q, peer_keys, peer_u, peer_v):
    b, t, d = h.shape
    xf = h.reshape(b * t, d)
    n = xf.shape[0]
    pad = (-n) % PEER_BLOCK
    xf = jnp.pad(xf, ((0, pad), (0, 0)))
    blocks = xf.reshape(-1, PEER_BLOCK, d)

    def one_block(xb):
        q = (xb @ peer_q).reshape(PEER_BLOCK, PEER_HEADS, 2, PEER_HALF)
        s = jnp.einsum("bhcd,hckd->bhck", q, peer_keys).astype(jnp.float32)
        sv, si = lax.top_k(s, PEER_TOPK)
        cand = sv[:, :, 0, :, None] + sv[:, :, 1, None, :]
        cidx = si[:, :, 0, :, None] * N_KEYS + si[:, :, 1, None, :]
        fv, fi = lax.top_k(cand.reshape(PEER_BLOCK, PEER_HEADS, PEER_TOPK * PEER_TOPK), PEER_TOPK)
        eidx = jnp.take_along_axis(cidx.reshape(PEER_BLOCK, PEER_HEADS, -1), fi, axis=-1)
        gate = jax.nn.softmax(fv, axis=-1)
        act = jax.nn.gelu(jnp.einsum("bhkd,bd->bhk", peer_u[eidx], xb).astype(jnp.float32), approximate=False)
        return jnp.einsum("bhk,bhkd->bd", (gate * act).astype(xb.dtype), peer_v[eidx])

    ys = lax.map(one_block, blocks)
    return ys.reshape(-1, d)[:n].reshape(b, t, d)

def hybrid_layer(x, is_prompt, cache_k, cache_v, wkv0, shift0, rel_bias, lp):
    (w_in, sinks, w_br_attn, w_br_rwkv, w_out, mu, w0, w_up, a0, a_up, g_up, k_k, k_a, r_k,
     lnx_g, lnx_b, ln1_g, ln1_b, peer_q, peer_keys, peer_u, peer_v, ln2_g, ln2_b) = lp
    b, t, _ = x.shape
    z = x @ w_in
    cuts = [Q_DIM, Q_DIM + KV_DIM, Q_DIM + 2 * KV_DIM, Q_DIM + 2 * KV_DIM + RWKV_IN,
            Q_DIM + 2 * KV_DIM + RWKV_IN + D_MODEL]
    q, ka, va, feats, gate_a, gate_b = jnp.split(z, cuts, axis=-1)
    q = q.reshape(b, t, ATTN_KV_HEADS, ATTN_GROUP, HEAD_DIM)
    ka = ka.reshape(b, t, ATTN_KV_HEADS, HEAD_DIM)
    va = va.reshape(b, t, ATTN_KV_HEADS, HEAD_DIM)
    if is_prompt:
        nb = t // ATTN_BLOCK
        qb = q.reshape(b, nb, ATTN_BLOCK, ATTN_KV_HEADS, ATTN_GROUP, HEAD_DIM)

        def band(u):
            ub = u.reshape(b, nb, ATTN_BLOCK, ATTN_KV_HEADS, HEAD_DIM)
            prev = jnp.concatenate([jnp.zeros_like(ub[:, :1]), ub[:, :-1]], axis=1)
            return jnp.concatenate([prev, ub], axis=2)

        i = jnp.arange(ATTN_BLOCK)[:, None]
        j = jnp.arange(2 * ATTN_BLOCK)[None, :]
        rel = i + ATTN_BLOCK - j
        key_pos = jnp.arange(nb)[:, None, None] * ATTN_BLOCK - ATTN_BLOCK + j[None]
        valid = (rel >= 0) & (rel <= WINDOW) & (key_pos >= 0)
        attn = window_attention(qb, band(ka), band(va), rel, valid, sinks, rel_bias)
        nw = min(WINDOW, t)
        new_k, new_v = ka[:, t - nw:], va[:, t - nw:]
        shift_init = jnp.zeros((b, RWKV_IN), x.dtype)
        wkv_init = jnp.zeros((b, RWKV_HEADS, RWKV_HEAD, RWKV_HEAD), jnp.float32)
    else:
        wb = cache_k.shape[1]
        k_all = jnp.concatenate([cache_k.astype(x.dtype), ka], axis=1)
        v_all = jnp.concatenate([cache_v.astype(x.dtype), va], axis=1)
        rel = jnp.arange(t)[:, None] + wb - jnp.arange(wb + t)[None, :]
        valid = ((rel >= 0) & (rel <= WINDOW))[None]
        attn = window_attention(q[:, None], k_all[:, None], v_all[:, None], rel, valid, sinks, rel_bias)
        new_k, new_v = k_all[:, t:], v_all[:, t:]
        shift_init, wkv_init = shift0, wkv0
    rwkv_out, new_shift, new_wkv = rwkv7_time_mix(feats, shift_init, wkv_init, mu, w0, w_up, a0, a_up, g_up,
                                                  k_k, k_a, r_k, lnx_g, lnx_b)
    merged = jax.nn.sigmoid(gate_a) * (attn @ w_br_attn) + jax.nn.sigmoid(gate_b) * (rwkv_out @ w_br_rwkv)
    h = layer_norm(DEEPNORM_ALPHA * x + merged @ w_out, ln1_g, ln1_b)
    y = layer_norm(DEEPNORM_ALPHA * h + peer(h, peer_q, peer_keys, peer_u, peer_v), ln2_g, ln2_b)
    dt = x.dtype if is_prompt else wkv0.dtype
    return y, new_k, new_v, new_wkv.astype(dt), new_shift

def setup_inputs(seed: int = 0) -> dict:
    key = jax.random.key(seed)
    ks = iter(jax.random.split(key, 48))
    nrm = lambda shape, scale: jax.random.normal(next(ks), shape, jnp.float32) * scale
    uni = lambda shape, lo, hi: jax.random.uniform(next(ks), shape, jnp.float32, lo, hi)
    L = DEPTH
    wb = min(WINDOW, PAST_LEN)
    return {
        "x_prompt": nrm((BATCH, SEQ, D_MODEL), 1.0),
        "x_sample": nrm((DEC_BATCH, DEC_SEQ, D_MODEL), 1.0),
        "cache_win_k": nrm((L, DEC_BATCH, wb, ATTN_KV_HEADS, HEAD_DIM), 1.0),
        "cache_win_v": nrm((L, DEC_BATCH, wb, ATTN_KV_HEADS, HEAD_DIM), 1.0),
        "state_wkv": nrm((L, DEC_BATCH, RWKV_HEADS, RWKV_HEAD, RWKV_HEAD), 0.3),
        "state_shift": nrm((L, DEC_BATCH, RWKV_IN), 1.0),
        "rel_bias": nrm((REL_BUCKETS, ATTN_HEADS), 0.2),
        "w_in": nrm((L, D_MODEL, IN_TOTAL), D_MODEL ** -0.5),
        "attn_sinks": nrm((L, ATTN_HEADS), 0.5),
        "w_branch_attn": nrm((L, Q_DIM, D_MODEL), Q_DIM ** -0.5),
        "w_branch_rwkv": nrm((L, RWKV_DIM, D_MODEL), RWKV_DIM ** -0.5),
        "w_out": nrm((L, D_MODEL, D_MODEL), DEEPNORM_BETA * D_MODEL ** -0.5),
        "rwkv_mu": uni((L, RWKV_IN), 0.0, 1.0),
        "rwkv_w0": uni((L, RWKV_DIM), -4.0, 1.0),
        "rwkv_w_up": nrm((L, LORA_W, RWKV_DIM), 0.1),
        "rwkv_a0": nrm((L, RWKV_DIM), 0.1),
        "rwkv_a_up": nrm((L, LORA_A, RWKV_DIM), 0.1),
        "rwkv_g_up": nrm((L, LORA_G, RWKV_DIM), LORA_G ** -0.5),
        "rwkv_k_k": 0.85 + nrm((L, RWKV_DIM), 0.02),
        "rwkv_k_a": 1.0 + nrm((L, RWKV_DIM), 0.02),
        "rwkv_r_k": nrm((L, RWKV_DIM), 0.1),
        "rwkv_lnx_g": 1.0 + nrm((L, RWKV_DIM), 0.02),
        "rwkv_lnx_b": nrm((L, RWKV_DIM), 0.02),
        "ln1_g": 1.0 + nrm((L, D_MODEL), 0.02),
        "ln1_b": nrm((L, D_MODEL), 0.02),
        "peer_q": nrm((L, D_MODEL, PEER_HEADS * PEER_KEY_DIM), D_MODEL ** -0.5),
        "peer_keys": nrm((L, PEER_HEADS, 2, N_KEYS, PEER_HALF), PEER_HALF ** -0.5),
        "peer_u": nrm((L, N_EXPERTS, D_MODEL), D_MODEL ** -0.5),
        "peer_v": nrm((L, N_EXPERTS, D_MODEL), DEEPNORM_BETA),
        "ln2_g": 1.0 + nrm((L, D_MODEL), 0.02),
        "ln2_b": nrm((L, D_MODEL), 0.02),
    }

def reference(x_prompt, x_sample, cache_win_k, cache_win_v, state_wkv, state_shift, rel_bias,
              w_in, attn_sinks, w_branch_attn, w_branch_rwkv, w_out, rwkv_mu, rwkv_w0, rwkv_w_up,
              rwkv_a0, rwkv_a_up, rwkv_g_up, rwkv_k_k, rwkv_k_a, rwkv_r_k, rwkv_lnx_g, rwkv_lnx_b,
              ln1_g, ln1_b, peer_q, peer_keys, peer_u, peer_v, ln2_g, ln2_b):
    yp, ys = x_prompt, x_sample
    kp, vp, wp, sp = [], [], [], []
    kd, vd, wd, sd = [], [], [], []
    for l in range(DEPTH):
        lp = (w_in[l], attn_sinks[l], w_branch_attn[l], w_branch_rwkv[l], w_out[l], rwkv_mu[l], rwkv_w0[l],
              rwkv_w_up[l], rwkv_a0[l], rwkv_a_up[l], rwkv_g_up[l], rwkv_k_k[l], rwkv_k_a[l], rwkv_r_k[l],
              rwkv_lnx_g[l], rwkv_lnx_b[l], ln1_g[l], ln1_b[l], peer_q[l], peer_keys[l], peer_u[l], peer_v[l],
              ln2_g[l], ln2_b[l])
        yp, k1, v1, w1, s1 = hybrid_layer(yp, True, None, None, None, None, rel_bias, lp)
        ys, k2, v2, w2, s2 = hybrid_layer(ys, False, cache_win_k[l], cache_win_v[l], state_wkv[l],
                                          state_shift[l], rel_bias, lp)
        kp.append(k1); vp.append(v1); wp.append(w1); sp.append(s1)
        kd.append(k2); vd.append(v2); wd.append(w2); sd.append(s2)
    return (yp, ys, jnp.stack(kp), jnp.stack(vp), jnp.stack(wp), jnp.stack(sp),
            jnp.stack(kd), jnp.stack(vd), jnp.stack(wd), jnp.stack(sd))


_drawn_inputs = setup_inputs


def setup_inputs(seed=0):
    import zlib

    import numpy as np

    out = dict(_drawn_inputs(seed))
    spreads = {}
    factors = {'attn_sinks': 8.0,
     'rwkv_k_k': 16.124,
     'rwkv_k_a': 2.722,
     'rwkv_lnx_g': 3.855,
     'ln2_g': 8.514,
     'ln2_b': 8.08,
     'rwkv_lnx_b': 3.493}
    for name, (base, spread) in spreads.items():
        noise = np.random.default_rng([zlib.crc32(name.encode()), seed]).standard_normal(out[name].shape)
        drawn = base * np.exp(spread * noise) if base else spread * noise
        out[name] = __import__('jax').numpy.asarray(drawn.astype(out[name].dtype))
    for name, factor in factors.items():
        out[name] = (out[name] * factor).astype(out[name].dtype)
    return out
```

```python
import math
from contextlib import ExitStack

import numpy as np
import concourse.bass as bass
from concourse import mybir

F32 = mybir.dt.float32
U32 = mybir.dt.uint32
ALU = mybir.AluOpType
ACT = mybir.ActivationFunctionType
AX_X = mybir.AxisListType.X

P = 128
DM = 1024
KT = DM // P
NP = 1024
NS = 8
NT = NP + NS
TG = NT // 3
NH = 16
NKV = 4
NPAD = NP + P
HD = 64
WIN = 128
NB = NP // WIN
NPAIR = NH // 2
CL = 64
NC = NP // CL
LN_EPS = 1e-5
GN_EPS = 64e-5
ALPHA = 2.0 ** 0.25
REL_ROWS = 33
MASKED = -1e30
DECAY_C = float(np.exp(-0.5))

T_Q, T_K, T_V, T_XWA, T_XG, T_GA, T_GB, T_PAIR = 0, 8, 10, 12, 13, 14, 22, 30
N_PLAIN = T_PAIR
N_TILES = T_PAIR + 3 * NPAIR
Q_PAIR_K, Q_PAIR_R, Q_PAIR_V = 0, 1, 2

(C_MUK, C_MUR, C_MUV, C_W0, C_A0, C_KK, C_KA, C_RK, C_LG, C_LB) = range(10)
NPRM = 10

(R_ALPHA, R_BETA, R_KAPPA, R_RHO, R_BETAE, R_KAPPAE, R_V) = range(7)
N_RW = 7


class Steps:

    def __init__(self, *names):
        self.at = {n: i + 1 for i, n in enumerate(names)}
        self.n = len(names)
        assert len(self.at) == self.n

    def after(self, name, turn=0):
        return turn * self.n + self.at[name]


def stand_alone(engine, A):
    engine.sem_inc(A["passed"], 1)


def grouped(ap):
    return ap.rearrange("p (a b) -> p a b", a=3)


def project_plain(nc, A, S):
    PE = Steps("z0", "z1", "t0", "t1")
    AC = Steps("z0", "z1", "t0", "t1")
    with ExitStack() as ctx:
        xT, ident = A["sb_xT"], A["sb_ident"]
        w = [ctx.enter_context(nc.sbuf_tensor(f"pw{j}", [P, KT, P], F32)) for j in range(2)]
        z = [ctx.enter_context(nc.sbuf_tensor(f"pz{j}", [P, NT], F32)) for j in range(2)]
        zn = [ctx.enter_context(nc.sbuf_tensor(f"pzn{j}", [NS + 1, P], F32)) for j in range(2)]
        zp = [ctx.enter_context(nc.psum_tensor(f"pzp{j}", [P, 3, 512], F32)) for j in range(2)]
        tp = [ctx.enter_context(nc.psum_tensor(f"ptp{j}", [P, 512], F32)) for j in range(2)]
        sem = lambda n: ctx.enter_context(nc.semaphore(n))
        const_in = sem("p_const_in")
        w_in = [sem(f"p_w_in{j}") for j in range(2)]
        z_out = [sem(f"p_z_out{j}") for j in range(2)]
        zn_out = [sem(f"p_zn_out{j}") for j in range(2)]
        pe_done, act_done = sem("p_pe_done"), sem("p_act_done")
        block = ctx.enter_context(nc.Block())

        @block.sync
        def _(sp):
            sp.dma_start(ident[:, :], A["ident"]).then_inc(const_in, 16)
            sp.dma_start(A["sb_bd"][:, :], A["bd"]).then_inc(const_in, 16)
            sp.dma_start(A["sb_eye2"][:, :], A["eye2"]).then_inc(const_in, 16)
            for k in range(KT):
                sp.dma_start(xT[:, k, :], A["xT"][:, k, :]).then_inc(const_in, 16)
            with sp.Fori(0, N_PLAIN // 2) as i:
                for j in range(2):
                    sp.wait_ge(pe_done, PE.n * i)
                    sp.dma_start(w[j][:, :, :], A["w_tiles"][2 * i + j]).then_inc(w_in[j], 16)

        @block.tensor
        def _(pe):
            pe.wait_ge(const_in, 16 * (KT + 3))
            with pe.Fori(0, N_PLAIN // 2) as i:
                for j in range(2):
                    pe.wait_ge(w_in[j], 16 * i + 16)
                    pe.wait_ge(act_done, AC.n * i)
                    for g in range(3):
                        for k in range(KT):
                            mm = pe.matmul(zp[j][:, g, 0:TG], w[j][:, k, :], xT[:, k, g * TG:(g + 1) * TG],
                                           start=(k == 0), stop=(k == KT - 1))
                    mm.then_inc(pe_done, 1)
                for j in range(2):
                    pe.wait_ge(act_done, AC.after(f"z{j}", i))
                    pe.transpose(tp[j][0:NS + 1, 0:P], z[j][:, NP - 1:NT], ident[:, :]).then_inc(pe_done, 1)

        @block.scalar
        def _(act):
            with act.Fori(0, N_PLAIN // 2) as i:
                for j in range(2):
                    act.wait_ge(pe_done, PE.after(f"z{j}", i))
                    act.wait_ge(z_out[j], 16 * i)
                    act.activation(grouped(z[j][:, :]), zp[j][:, :, 0:TG], ACT.Copy).then_inc(act_done, 1)
                    act.wait_ge(act_done, AC.after(f"z{j}", i))
                    act.dma_start(A["zT"][2 * i + j], z[j][:, :]).then_inc(z_out[j], 16)
                for j in range(2):
                    act.wait_ge(pe_done, PE.after(f"t{j}", i))
                    act.wait_ge(zn_out[j], 16 * i)
                    act.activation(zn[j][:, :], tp[j][0:NS + 1, 0:P], ACT.Copy).then_inc(act_done, 1)
                    act.wait_ge(act_done, AC.after(f"t{j}", i))
                    act.dma_start(A["zn"][:, 2 * i + j, :], zn[j][:, :]).then_inc(zn_out[j], 16)
            for j in range(2):
                act.wait_ge(z_out[j], 16 * (N_PLAIN // 2))
                act.wait_ge(zn_out[j], 16 * (N_PLAIN // 2))


def project_pairs(nc, A, S):
    PE = Steps("k", "w", "a", "g", "r", "v", "ss", "bonus", "raw_t", "dec_t")
    AC = Steps("k", "w", "a", "g", "r", "v", "D", "Dprev", "Dinv", "wdec", "norm", "raw_t", "dec_t0", "dec_t1")
    DV = Steps("prm", "half", "k_d", "k_ds", "k_f", "kkr", "sq", "lw", "scan", "lprev", "a", "ka1", "kp",
               "r_d", "r_ds", "r_f", "rkr", "rk", "v_d", "v_ds", "v_f", "ssm", "rinv", "kk", "kka", "bonus",
               "alpha", "beta", "kappa", "rho", "dend", "betae", "kappae")
    N_PRE = 13
    with ExitStack() as ctx:
        xT, ident, bd = A["sb_xT"], A["sb_ident"], A["sb_bd"]
        sb = lambda n, s: ctx.enter_context(nc.sbuf_tensor(n, s, F32))
        sem = lambda n: ctx.enter_context(nc.semaphore(n))
        w = [sb(f"qw{j}", [P, KT, P]) for j in range(3)]
        up = sb("q_up", [P, 2, P])
        z = [sb(f"qz{q}", [P, 1 + NT]) for q in range(3)]
        lora = [sb(f"q_lora{j}", [P, NT]) for j in range(2)]
        prm = sb("q_prm", [P, NPAIR, NPRM])
        sh = sb("q_sh", [P, 2 + 3 * NPAIR, NS])
        mul_ = sb("q_mulora", [P, 2])
        pc = sb("q_pc", [P, NPRM])
        hc = sb("q_hc", [P, 2])
        tmp = sb("q_tmp", [P, NT])
        fk, fr, fv = sb("q_fk", [P, NT]), sb("q_fr", [P, NT]), sb("q_fv", [P, NT])
        kkr, sq, tw, ta = sb("q_kkr", [P, NT]), sb("q_sq", [P, NT]), sb("q_tw", [P, NT]), sb("q_ta", [P, NT])
        kk, kka, kp, rk = sb("q_kk", [P, NT]), sb("q_kka", [P, NT]), sb("q_kp", [P, NT]), sb("q_rk", [P, NT])
        lcum, lprev = sb("q_lcum", [P, NP]), sb("q_lprev", [P, NP])
        D, Dp, Di = sb("q_D", [P, NP]), sb("q_Dp", [P, NP]), sb("q_Di", [P, NP])
        wdec = sb("q_wdec", [P, NS])
        dend = sb("q_dend", [P, NC])
        reset = sb("q_reset", [P, NP])
        gate, bonus = sb("q_gate", [P, NT]), sb("q_bonus", [P, NT])
        out = [sb(f"q_out{n}", [P, NP]) for n in range(6)]
        rawn = sb("q_rawn", [NS + 1, 3 * P])
        decn = sb("q_decn", [NS, 6 * P])
        zp = [ctx.enter_context(nc.psum_tensor(f"qzp{j}", [P, 3, 512], F32)) for j in range(2)]
        tp = [ctx.enter_context(nc.psum_tensor(f"qtp{j}", [P, 512], F32)) for j in range(2)]
        const_in, lora_in = sem("q_const_in"), sem("q_lora_in")
        w_in = [sem(f"q_w_in{j}") for j in range(3)]
        up_in = sem("q_up_in")
        pe_done, act_done, dve_done = sem("q_pe_done"), sem("q_act_done"), sem("q_dve_done")
        pre_dve, pre_act = sem("q_pre_dve"), sem("q_pre_act")
        rw_out = [sem(f"q_rw_out{n}") for n in range(N_RW)]
        g_out, b_out, d_out = sem("q_g_out"), sem("q_b_out"), sem("q_d_out")
        raw_out, dec_out = sem("q_raw_out"), sem("q_dec_out")
        block = ctx.enter_context(nc.Block())
        PROMPT, DEC = slice(0, NP), slice(NP, NT)
        chunks = lambda ap: ap.rearrange("p (c l) -> p c l", l=CL)
        each = lambda ap: ap.unsqueeze(2).broadcast_to([P, NC, CL])

        @block.sync
        def _(sp):
            for d, s in ((z[0][:, 1:], A["zT"][T_XWA]), (z[1][:, 1:], A["zT"][T_XG])):
                sp.dma_start(d, s).then_inc(lora_in, 16)
            for d, s in ((prm[:, :, :], A["prm"]), (sh[:, :, :], A["shT"]), (mul_[:, :], A["mu_lora"])):
                sp.dma_start(d, s).then_inc(const_in, 16)
            with sp.Fori(0, NPAIR) as p:
                sp.wait_ge(pe_done, PE.n * p)
                for q in range(3):
                    if q == 1:
                        sp.dma_start(up[:, :, :], A["up"][p]).then_inc(up_in, 16)
                    sp.dma_start(w[q][:, :, :], A["w_tiles"][T_PAIR + 3 * p + q]).then_inc(w_in[q], 16)

        @block.tensor
        def _(pe):
            def project(q, s):
                for g in range(3):
                    for k in range(KT):
                        mm = pe.matmul(zp[s][:, g, 0:TG], w[q][:, k, :], xT[:, k, g * TG:(g + 1) * TG],
                                       start=(k == 0), stop=(k == KT - 1))
                mm.then_inc(pe_done, 1)

            def small(s, lhsT, rhs):
                for g in range(3):
                    mm = pe.matmul(zp[s][:, g, 0:TG], lhsT, rhs[:, g * TG:(g + 1) * TG], start=True, stop=True)
                mm.then_inc(pe_done, 1)

            pe.wait_ge(pre_act, 2)
            pe.wait_ge(pre_dve, N_PRE)
            with pe.Fori(0, NPAIR) as p:
                pe.wait_ge(dve_done, DV.n * p)
                pe.wait_ge(act_done, AC.n * p)
                pe.wait_ge(w_in[0], 16 * p + 16)
                project(Q_PAIR_K, 0)
                pe.wait_ge(up_in, 16 * p + 16)
                small(1, up[0:HD, 0, :], lora[0][0:HD, :])
                pe.wait_ge(act_done, AC.after("k", p))
                small(0, up[HD:P, 0, :], lora[0][HD:P, :])
                pe.wait_ge(act_done, AC.after("w", p))
                small(1, up[:, 1, :], lora[1][:, :])
                pe.wait_ge(w_in[1], 16 * p + 16)
                pe.wait_ge(act_done, AC.after("a", p))
                project(Q_PAIR_R, 0)
                pe.wait_ge(w_in[2], 16 * p + 16)
                pe.wait_ge(act_done, AC.after("g", p))
                project(Q_PAIR_V, 1)
                pe.wait_ge(act_done, AC.after("r", p))
                pe.wait_ge(dve_done, DV.after("sq", p))
                small(0, bd[:, :], sq[:, :])
                pe.wait_ge(act_done, AC.after("v", p))
                pe.wait_ge(dve_done, DV.after("rk", p))
                small(1, bd[:, :], rk[:, :])
                for q in range(3):
                    t = pe.transpose(tp[0][0:NS + 1, q * P:(q + 1) * P], z[q][:, NP:1 + NT], ident[:, :])
                t.then_inc(pe_done, 1)
                pe.wait_ge(act_done, AC.after("raw_t", p))
                pe.wait_ge(act_done, AC.after("wdec", p))
                pe.wait_ge(dve_done, DV.after("kka", p))
                for n, src in enumerate((fr[:, DEC], wdec[:, :], kp[:, DEC], fv[:, DEC], kk[:, DEC], kka[:, DEC])):
                    t = pe.transpose(tp[n // 4][0:NS, (n % 4) * P:(n % 4 + 1) * P], src, ident[:, :])
                t.then_inc(pe_done, 1)

        @block.scalar
        def _(act):
            act.wait_ge(pre_dve, N_PRE - 2)
            act.activation(lora[0][0:HD, :], z[0][0:HD, 1:], ACT.Tanh).then_inc(pre_act, 1)
            act.activation(lora[1][:, :], z[1][:, 1:], ACT.Tanh, scale=0.5).then_inc(pre_act, 1)
            act.wait_ge(pre_dve, N_PRE)
            with act.Fori(0, NPAIR) as p:
                act.wait_ge(dve_done, DV.n * p)
                act.wait_ge(pe_done, PE.after("k", p))
                act.activation(grouped(z[0][:, 1:]), zp[0][:, :, 0:TG], ACT.Copy).then_inc(act_done, 1)
                act.wait_ge(dve_done, DV.after("half", p))
                act.wait_ge(pe_done, PE.after("w", p))
                act.activation(grouped(tw[:, :]), zp[1][:, :, 0:TG], ACT.Tanh, bias=hc[:, 0:1], scale=0.5).then_inc(act_done, 1)
                act.wait_ge(pe_done, PE.after("a", p))
                act.activation(grouped(ta[:, :]), zp[0][:, :, 0:TG], ACT.Tanh, bias=hc[:, 1:2], scale=0.5).then_inc(act_done, 1)
                act.wait_ge(pe_done, PE.after("g", p))
                act.wait_ge(g_out, 16 * p)
                act.activation(grouped(gate[:, :]), zp[1][:, :, 0:TG], ACT.Copy).then_inc(act_done, 1)
                act.wait_ge(pe_done, PE.after("r", p))
                act.activation(grouped(z[1][:, 1:]), zp[0][:, :, 0:TG], ACT.Copy).then_inc(act_done, 1)
                act.wait_ge(pe_done, PE.after("v", p))
                act.activation(grouped(z[2][:, 1:]), zp[1][:, :, 0:TG], ACT.Copy).then_inc(act_done, 1)
                act.wait_ge(dve_done, DV.after("lprev", p))
                act.activation(D[:, :], lcum[:, :], ACT.Exp).then_inc(act_done, 1)
                act.activation(Dp[:, :], lprev[:, :], ACT.Exp).then_inc(act_done, 1)
                act.activation(Di[:, :], lcum[:, :], ACT.Exp, scale=-1.0).then_inc(act_done, 1)
                act.activation(wdec[:, :], tw[:, DEC], ACT.Exp).then_inc(act_done, 1)
                act.wait_ge(dve_done, DV.after("ssm", p))
                act.activation(sq[:, :], sq[:, :], ACT.Sqrt).then_inc(act_done, 1)
                act.wait_ge(pe_done, PE.after("raw_t", p))
                act.wait_ge(raw_out, 16 * p)
                act.activation(rawn[:, :], tp[0][0:NS + 1, 0:3 * P], ACT.Copy).then_inc(act_done, 1)
                act.wait_ge(act_done, AC.after("raw_t", p))
                act.dma_start(A["zn"][:, bass.ds(T_PAIR + 3 * p, 3), :],
                              rawn[:, :].rearrange("b (q f) -> b q f", q=3)).then_inc(raw_out, 16)
                act.wait_ge(pe_done, PE.after("dec_t", p))
                act.wait_ge(dec_out, 32 * p)
                act.activation(decn[:, 0:4 * P], tp[0][0:NS, :], ACT.Copy).then_inc(act_done, 1)
                act.activation(decn[:, 4 * P:], tp[1][0:NS, 0:2 * P], ACT.Copy).then_inc(act_done, 1)
                act.wait_ge(act_done, AC.after("dec_t1", p))
                for h in range(2):
                    act.dma_start(A["decn"][:, p, h],
                                  decn[:, :].rearrange("b (q h d) -> b q h d", h=2, d=HD)[:, :, h, :]).then_inc(dec_out, 16)
            act.wait_ge(raw_out, 16 * NPAIR)
            act.wait_ge(dec_out, 32 * NPAIR)

        @block.vector
        def _(dve):
            steps = iter(range(1, N_PRE + 1))

            def pre(ins):
                ins.then_inc(pre_dve, 1)
                dve.wait_ge(pre_dve, next(steps))

            for q in range(3):
                pre(nc.vector.memset(z[q][:, 0:1], 0.0))
            pre(nc.vector.memset(reset[:, :], 1.0))
            pre(nc.vector.memset(reset[:, 0:NP:CL], 0.0))
            dve.wait_ge(lora_in, 32)
            dve.wait_ge(const_in, 48)
            for j, t in ((0, tmp), (1, fk)):
                pre(nc.vector.tensor_tensor(t[:, PROMPT], z[j][:, 0:NP], z[j][:, 1:1 + NP], ALU.subtract))
                pre(nc.vector.tensor_tensor(t[:, DEC], sh[:, j, :], z[j][:, 1 + NP:], ALU.subtract))
                pre(nc.vector.scalar_tensor_tensor(z[j][:, 1:], t[:, :], mul_[:, j:j + 1], z[j][:, 1:], ALU.mult, ALU.add))
            dve.wait_ge(pre_act, 2)
            pre(nc.vector.tensor_copy(lora[0][HD:P, :], z[0][HD:P, 1:]))
            pre(nc.vector.tensor_scalar(lora[1][:, :], lora[1][:, :], 0.5, 0.5, ALU.mult, ALU.add))

            with dve.Fori(0, NPAIR) as p:
                def do(name, ins):
                    ins.then_inc(dve_done, 1)
                    dve.wait_ge(dve_done, DV.after(name, p))

                def mixed(q, f, n, mu):
                    do(n + "_d", nc.vector.tensor_tensor(tmp[:, PROMPT], z[q][:, 0:NP], z[q][:, 1:1 + NP], ALU.subtract))
                    do(n + "_ds", nc.vector.tensor_tensor(tmp[:, DEC], sh[:, bass.ds(2 + 3 * p + q, 1), :].rearrange("p a b -> p (a b)"),
                                                          z[q][:, 1 + NP:], ALU.subtract))
                    do(n + "_f", nc.vector.scalar_tensor_tensor(f[:, :], tmp[:, :], pc[:, mu:mu + 1], z[q][:, 1:], ALU.mult, ALU.add))

                do("prm", nc.vector.tensor_copy(pc[:, :], prm[:, bass.ds(p, 1), :].rearrange("p a b -> p (a b)")))
                do("half", nc.vector.tensor_scalar(hc[:, :], pc[:, C_W0:C_A0 + 1], 0.5, None, ALU.mult))
                dve.wait_ge(act_done, AC.after("k", p))
                mixed(0, fk, "k", C_MUK)
                do("kkr", nc.vector.tensor_scalar(kkr[:, :], fk[:, :], pc[:, C_KK:C_KK + 1], None, ALU.mult))
                do("sq", nc.vector.tensor_tensor(sq[:, :], kkr[:, :], kkr[:, :], ALU.mult))
                dve.wait_ge(act_done, AC.after("w", p))
                do("lw", nc.vector.tensor_scalar(tw[:, :], tw[:, :], -0.5 * DECAY_C, -0.5 * DECAY_C, ALU.mult, ALU.add))
                do("scan", nc.vector.tensor_tensor_scan(lcum[:, :], reset[:, :], tw[:, PROMPT], 0.0, ALU.mult, ALU.add))
                do("lprev", nc.vector.tensor_tensor(lprev[:, :], lcum[:, :], tw[:, PROMPT], ALU.subtract))
                dve.wait_ge(act_done, AC.after("a", p))
                do("a", nc.vector.tensor_scalar(ta[:, :], ta[:, :], 0.5, 0.5, ALU.mult, ALU.add))
                do("ka1", nc.vector.tensor_scalar(kp[:, :], ta[:, :], -1.0, pc[:, C_KA:C_KA + 1], ALU.add, ALU.mult))
                do("kp", nc.vector.scalar_tensor_tensor(kp[:, :], kp[:, :], 1.0, fk[:, :], ALU.add, ALU.mult))
                dve.wait_ge(act_done, AC.after("r", p))
                mixed(1, fr, "r", C_MUR)
                do("rkr", nc.vector.tensor_scalar(rk[:, :], kp[:, :], pc[:, C_RK:C_RK + 1], None, ALU.mult))
                do("rk", nc.vector.tensor_tensor(rk[:, :], rk[:, :], fr[:, :], ALU.mult))
                dve.wait_ge(act_done, AC.after("v", p))
                for n in range(N_RW):
                    dve.wait_ge(rw_out[n], 16 * p)
                dve.wait_ge(b_out, 16 * p)
                dve.wait_ge(d_out, 16 * p)
                mixed(2, fv, "v", C_MUV)
                dve.wait_ge(pe_done, PE.after("ss", p))
                do("ssm", nc.vector.tensor_scalar(grouped(sq[:, :]), zp[0][:, :, 0:TG], 1e-24, None, ALU.max))
                dve.wait_ge(act_done, AC.after("norm", p))
                do("rinv", nc.vector.reciprocal(sq[:, :], sq[:, :]))
                do("kk", nc.vector.tensor_tensor(kk[:, :], kkr[:, :], sq[:, :], ALU.mult))
                do("kka", nc.vector.tensor_tensor(kka[:, :], kk[:, :], ta[:, :], ALU.mult))
                dve.wait_ge(pe_done, PE.after("bonus", p))
                do("bonus", nc.vector.tensor_tensor(grouped(bonus[:, :]), zp[1][:, :, 0:TG], grouped(fv[:, :]), ALU.mult))
                for name, n, x, d in (("alpha", R_ALPHA, kk, Dp), ("beta", R_BETA, kka, Di),
                                      ("kappa", R_KAPPA, kp, Di), ("rho", R_RHO, fr, D)):
                    do(name, nc.vector.tensor_tensor(out[n][:, :], x[:, PROMPT], d[:, :], ALU.mult))
                do("dend", nc.vector.tensor_copy(dend[:, :], D[:, CL - 1:NP:CL]))
                for name, n, x in (("betae", R_BETAE, R_BETA), ("kappae", R_KAPPAE, R_KAPPA)):
                    do(name, nc.vector.tensor_tensor(chunks(out[n][:, :]), chunks(out[x][:, :]), each(dend[:, :]), ALU.mult))

        @block.gpsimd
        def _(pool):
            with pool.Fori(0, NPAIR) as p:
                pool.wait_ge(act_done, AC.after("g", p))
                stand_alone(pool, A)
                pool.dma_start(A["gate"][p], gate[:, :]).then_inc(g_out, 16)
                pool.wait_ge(dve_done, DV.after("v_f", p))
                stand_alone(pool, A)
                pool.dma_start(A["rw"][p, R_V], fv[:, PROMPT]).then_inc(rw_out[R_V], 16)
                pool.wait_ge(dve_done, DV.after("bonus", p))
                stand_alone(pool, A)
                pool.dma_start(A["bonus"][p], bonus[:, :]).then_inc(b_out, 16)
                for name, n in (("alpha", R_ALPHA), ("beta", R_BETA), ("kappa", R_KAPPA), ("rho", R_RHO),
                                ("betae", R_BETAE), ("kappae", R_KAPPAE)):
                    pool.wait_ge(dve_done, DV.after(name, p))
                    stand_alone(pool, A)
                    pool.dma_start(A["rw"][p, n], out[n][:, :]).then_inc(rw_out[n], 16)
                    if name == "rho":
                        pool.wait_ge(dve_done, DV.after("dend", p))
                        stand_alone(pool, A)
                        pool.dma_start(A["dend"][p], dend[:, :]).then_inc(d_out, 16)
            for s in (*rw_out, g_out, b_out, d_out):
                pool.wait_ge(s, 16 * NPAIR)


def scan_pairs(nc, A):
    LEVELS = 5
    batches = [("ab", "D"), ("abT", "D"), ("akT", "D")]
    fill = {1: "vn", 2: "bn", 3: "kn", 4: "an", 5: "rbT"}
    for l in range(1, LEVELS + 1):
        batches.append((f"P{l}", "A"))
        if l < LEVELS:
            batches.append((f"PT{l}", "A"))
        batches += [(fill[l], "D" if fill[l] == "rbT" else "A"), (f"X{l}", "D")]
    batches += [("rkT", "D"), ("Z", "A"), ("GT", "A"), ("H", "A"), ("U", "D"), ("S", "D"), ("Y", "A"),
                ("fin", "A"), ("mean", "D"), ("var", "D")]
    order = [n for n, _ in batches]
    evac_on = dict(batches)
    slot_of = {n: i % 4 for i, n in enumerate(order)}
    assert len(order) % 4 == 0
    chain = [f"{x}{c}" for c in range(NC) for x in ("u", "s")]
    PE = Steps(*order[:order.index("U")], *chain, "Y", "fin", "mean", "var")
    AC = Steps(*[n for n in order if evac_on[n] == "A"], "std")
    DV = Steps("ab", "abT", "X0", "akT", "X1", "X2", "X3", "X4", "rbT", "X5", "rkT", *chain,
               "yc", "sqy", "tv", "ri", "yn", "ya", "yb")
    with ExitStack() as ctx:
        ident, bd = A["sb_ident"], A["sb_bd"]
        sb = lambda n, s: ctx.enter_context(nc.sbuf_tensor(n, s, F32))
        sem = lambda n: ctx.enter_context(nc.semaphore(n))
        rw = [sb(f"r_in{j}", [P, N_RW, NP]) for j in range(2)]
        dend = [sb(f"r_dend{j}", [P, NC]) for j in range(2)]
        gate, bonus = sb("r_gate", [P, NP]), sb("r_bonus", [P, NP])
        prm = sb("r_prm", [P, NPAIR, NPRM])
        masks = sb("r_masks", [P, 5, CL])
        Pn, Pt = [sb(f"r_P{j}", [P, NP]) for j in range(2)], [sb(f"r_PT{j}", [P, NP]) for j in range(2)]
        X = sb("r_X", [P, NP])
        akT, rbT, rkT = sb("r_akT", [P, NP]), sb("r_rbT", [P, NP]), sb("r_rkT", [P, NP])
        vn, bn, kn, an = (sb("r_" + n, [P, NP]) for n in ("vn", "bn", "kn", "an"))
        GT, Z, H, U = (sb("r_" + n, [P, NP]) for n in ("GT", "Z", "H", "U"))
        ST = sb("r_ST", [P, (NC + 1) * HD])
        ysb, sqy = sb("r_y", [P, NP]), sb("r_sqy", [P, NP])
        fin = sb("r_fin", [P, HD])
        ps = [ctx.enter_context(nc.psum_tensor(f"r_ps{j}", [P, NP], F32)) for j in range(4)]
        const_in = sem("r_const_in")
        rw_in = [sem(f"r_rw_in{j}") for j in range(2)]
        gb_in = sem("r_gb_in")
        pe_done, act_done, dve_done, zeroed = sem("r_pe_done"), sem("r_act_done"), sem("r_dve_done"), sem("r_zeroed")
        fin_out, y_out = sem("r_fin_out"), sem("r_y_out")
        block = ctx.enter_context(nc.Block())
        chunks = lambda ap: ap.rearrange("p (c l) -> p c l", l=CL)
        col = lambda c: slice(c * CL, (c + 1) * CL)
        half = lambda h: slice(h * HD, (h + 1) * HD)

        @block.sync
        def _(sp):
            for d, s in ((prm[:, :, :], A["prm"]), (masks[:, :, :], A["masks"])):
                sp.dma_start(d, s).then_inc(const_in, 16)
            with sp.Fori(0, NPAIR // 2) as i:
                for j in range(2):
                    p = 2 * i + j
                    sp.wait_ge(pe_done, 2 * PE.n * i)
                    stand_alone(sp, A)
                    sp.wait_ge(dve_done, 2 * DV.n * i)
                    stand_alone(sp, A)
                    for n in range(N_RW):
                        sp.dma_start(rw[j][:, n, :], A["rw"][p, n]).then_inc(rw_in[j], 16)
                    sp.dma_start(dend[j][:, :], A["dend"][p]).then_inc(rw_in[j], 16)
                for j in range(2):
                    p = 2 * i + j
                    sp.wait_ge(dve_done, DV.n * p)
                    sp.dma_start(gate[:, :], A["gate"][p, :, 0:NP]).then_inc(gb_in, 16)
                    sp.dma_start(bonus[:, :], A["bonus"][p, :, 0:NP]).then_inc(gb_in, 16)

        @block.tensor
        def _(pe):
            def quads(name, lhsT, rhs, cs=range(NC)):
                for c in cs:
                    for h in range(2):
                        mm = pe.matmul(ps[slot_of[name]][half(h), col(c)], lhsT[half(h), col(c)],
                                       ident[half(h), half(h)] if rhs is None else rhs[half(h), col(c)],
                                       start=True, stop=True)
                return mm

            with pe.Fori(0, NPAIR // 2) as i:
                for j in range(2):
                    p = 2 * i + j
                    r = [rw[j][:, n, :] for n in range(N_RW)]

                    def need(*names):
                        for done, S in ((act_done, AC), (dve_done, DV)):
                            mine = [n for n in names if n in S.at]
                            if mine:
                                pe.wait_ge(done, S.after(max(mine, key=S.at.get), p))
                        stand_alone(pe, A)

                    def batch(name, lhsT, rhs, *inputs):
                        before = order.index(name) - 4
                        need(*([order[before]] if before >= 0 else []), *inputs)
                        quads(name, lhsT, rhs).then_inc(pe_done, 1)

                    pe.wait_ge(rw_in[j], 16 * (N_RW + 1) * (i + 1))
                    pe.wait_ge(act_done, AC.n * p)
                    pe.wait_ge(dve_done, DV.n * p)
                    batch("ab", r[R_ALPHA], r[R_BETA])
                    batch("abT", r[R_BETA], r[R_ALPHA])
                    batch("akT", r[R_KAPPA], r[R_ALPHA])
                    for l in range(1, LEVELS + 1):
                        a, b = (l - 1) % 2, l % 2
                        got = ("ab", "abT") if l == 1 else (f"P{l - 1}", f"PT{l - 1}")
                        batch(f"P{l}", Pt[a], Pn[a], *got)
                        if l < LEVELS:
                            batch(f"PT{l}", Pn[a], Pt[a])
                        if l == 5:
                            batch("rbT", r[R_BETA], r[R_RHO])
                        else:
                            batch(fill[l], r[(R_V, R_BETAE, R_KAPPAE, R_ALPHA)[l - 1]], None)
                        batch(f"X{l}", Pn[b], X, f"P{l}", f"X{l - 1}")
                    batch("rkT", r[R_KAPPA], r[R_RHO])
                    batch("Z", akT, vn, "akT", "vn")
                    batch("GT", an, X, "an", "X5")
                    batch("H", X, Z, "Z")

                    def y_chunk(c):
                        for h in range(2):
                            out = ps[slot_of["Y"]][half(h), col(c)]
                            pe.matmul(out, ST[half(h), col(c)], r[R_RHO][half(h), col(c)], start=True, stop=False)
                            pe.matmul(out, U[half(h), col(c)], rbT[half(h), col(c)], start=False, stop=False)
                            mm = pe.matmul(out, vn[half(h), col(c)], rkT[half(h), col(c)], start=False, stop=True)
                        return mm

                    need("GT", "H", "kn", "bn", "rbT", "rkT", "X5")
                    for c in range(NC):
                        if c:
                            need(f"s{c - 1}")
                        for h in range(2):
                            mm = pe.matmul(ps[slot_of["U"]][half(h), col(c)], GT[half(h), col(c)], ST[half(h), col(c)],
                                           start=True, stop=True)
                        mm.then_inc(pe_done, 1)
                        for h in range(2):
                            pe.matmul(ps[slot_of["S"]][half(h), col(c)], kn[half(h), col(c)], vn[half(h), col(c)],
                                      start=True, stop=False)
                        if c:
                            y_chunk(c - 1)
                        need(f"u{c}")
                        for h in range(2):
                            mm = pe.matmul(ps[slot_of["S"]][half(h), col(c)], bn[half(h), col(c)], U[half(h), col(c)],
                                           start=False, stop=True)
                        mm.then_inc(pe_done, 1)
                    y_chunk(NC - 1).then_inc(pe_done, 1)
                    need(f"s{NC - 1}")
                    for h in range(2):
                        mm = pe.matmul(ps[slot_of["fin"]][half(h), 0:HD], ST[half(h), col(NC)], ident[half(h), half(h)],
                                       start=True, stop=True)
                    mm.then_inc(pe_done, 1)
                    need("Y")
                    for g in range(2):
                        mm = pe.matmul(ps[slot_of["mean"]][:, g * 512:(g + 1) * 512], bd[:, :],
                                       ysb[:, g * 512:(g + 1) * 512], start=True, stop=True)
                    mm.then_inc(pe_done, 1)
                    need("sqy")
                    for g in range(2):
                        mm = pe.matmul(ps[slot_of["var"]][:, g * 512:(g + 1) * 512], bd[:, :],
                                       sqy[:, g * 512:(g + 1) * 512], start=True, stop=True)
                    mm.then_inc(pe_done, 1)

        @block.scalar
        def _(act):
            to = {"vn": vn, "bn": bn, "kn": kn, "an": an, "Z": Z, "GT": GT, "H": H, "Y": ysb, "fin": fin}
            with act.Fori(0, NPAIR // 2) as i:
                for j in range(2):
                    p = 2 * i + j
                    act.wait_ge(dve_done, DV.n * p)
                    for name in order:
                        if evac_on[name] != "A":
                            continue
                        act.wait_ge(pe_done, PE.after(name, p))
                        if name[0] == "P":
                            l = int(name[-1])
                            dst = (Pt if name[1] == "T" else Pn)[l % 2]
                        else:
                            dst = to[name]
                        if name == "fin":
                            act.wait_ge(fin_out, 16 * p)
                        if name == "Y":
                            act.wait_ge(y_out, 16 * p)
                        n = HD if name == "fin" else NP
                        act.activation(dst[:, :], ps[slot_of[name]][:, 0:n], ACT.Copy,
                                       scale=-1.0 if name == "bn" else 1.0).then_inc(act_done, 1)
                        if name == "fin":
                            act.wait_ge(act_done, AC.after("fin", p))
                            act.dma_start(A["wkv_p"][bass.ds(p, 1)].rearrange("a p k -> (a p) k"), fin[:, :]).then_inc(fin_out, 16)
                    act.wait_ge(dve_done, DV.after("tv", p))
                    act.activation(sqy[:, :], sqy[:, :], ACT.Sqrt).then_inc(act_done, 1)
            act.wait_ge(fin_out, 16 * NPAIR)

        @block.vector
        def _(dve):
            dve.wait_ge(const_in, 32)
            nc.vector.memset(ST[:, 0:HD], 0.0).then_inc(zeroed, 1)
            dve.wait_ge(zeroed, 1)
            mask = lambda n: masks[:, n, :].unsqueeze(1).broadcast_to([P, NC, CL])
            with dve.Fori(0, NPAIR // 2) as i:
                for j in range(2):
                    p = 2 * i + j

                    def do(name, ins):
                        ins.then_inc(dve_done, 1)
                        dve.wait_ge(dve_done, DV.after(name, p))

                    def masked(name, dst, m):
                        dve.wait_ge(pe_done, PE.after(name, p))
                        do(name, nc.vector.tensor_tensor(chunks(dst[:, :]), chunks(ps[slot_of[name]][:, :]), mask(m), ALU.mult))

                    def grow(l):
                        name = f"X{l}"
                        dve.wait_ge(pe_done, PE.after(name, p))
                        do(name, nc.vector.tensor_tensor(X[:, :], ps[slot_of[name]][:, :], X[:, :], ALU.add))

                    masked("ab", Pn[0], 0)
                    masked("abT", Pt[0], 1)
                    do("X0", nc.vector.tensor_tensor(chunks(X[:, :]), chunks(Pt[0][:, :]),
                                                     A["sb_eye2"][:, :].unsqueeze(1).broadcast_to([P, NC, CL]), ALU.add))
                    masked("akT", akT, 2)
                    for l in range(1, 5):
                        grow(l)
                    masked("rbT", rbT, 3)
                    grow(5)
                    masked("rkT", rkT, 4)
                    for n in ("GT", "H"):
                        dve.wait_ge(act_done, AC.after(n, p))
                    dve.wait_ge(rw_in[j], 16 * (N_RW + 1) * (i + 1))
                    for c in range(NC):
                        dve.wait_ge(pe_done, PE.after(f"u{c}", p))
                        do(f"u{c}", nc.vector.tensor_tensor(U[:, col(c)], ps[slot_of["U"]][:, col(c)], H[:, col(c)], ALU.add))
                        dve.wait_ge(pe_done, PE.after(f"s{c}", p))
                        do(f"s{c}", nc.vector.scalar_tensor_tensor(ST[:, col(c + 1)], ST[:, col(c)], dend[j][:, c:c + 1],
                                                                   ps[slot_of["S"]][:, col(c)], ALU.mult, ALU.add))
                    dve.wait_ge(act_done, AC.after("Y", p))
                    dve.wait_ge(pe_done, PE.after("mean", p))
                    dve.wait_ge(gb_in, 32 * (p + 1))
                    do("yc", nc.vector.scalar_tensor_tensor(ysb[:, :], ps[slot_of["mean"]][:, :], -1.0 / HD, ysb[:, :], ALU.mult, ALU.add))
                    do("sqy", nc.vector.tensor_tensor(sqy[:, :], ysb[:, :], ysb[:, :], ALU.mult))
                    dve.wait_ge(pe_done, PE.after("var", p))
                    do("tv", nc.vector.tensor_scalar(sqy[:, :], ps[slot_of["var"]][:, :], 1.0 / HD, GN_EPS, ALU.mult, ALU.add))
                    dve.wait_ge(act_done, AC.after("std", p))
                    do("ri", nc.vector.reciprocal(sqy[:, :], sqy[:, :]))
                    do("yn", nc.vector.scalar_tensor_tensor(ysb[:, :], ysb[:, :], prm[:, bass.ds(p, 1), C_LG:C_LG + 1].rearrange("p a b -> p (a b)"),
                                                            sqy[:, :], ALU.mult, ALU.mult))
                    do("ya", nc.vector.scalar_tensor_tensor(ysb[:, :], ysb[:, :], prm[:, bass.ds(p, 1), C_LB:C_LB + 1].rearrange("p a b -> p (a b)"),
                                                            bonus[:, :], ALU.add, ALU.add))
                    do("yb", nc.vector.tensor_tensor(ysb[:, :], ysb[:, :], gate[:, :], ALU.mult))

        @block.gpsimd
        def _(pool):
            with pool.Fori(0, NPAIR // 2) as i:
                for j in range(2):
                    p = 2 * i + j
                    pool.wait_ge(dve_done, DV.after("yb", p))
                    pool.dma_start(A["bT"][p, :, 0:NP], ysb[:, :]).then_inc(y_out, 16)
            pool.wait_ge(y_out, 16 * NPAIR)


def attend(nc, A):
    UN = 4
    UNITS = NH // UN
    NBUF = 2
    STEPS_ = NBUF * UNITS
    names = lambda *n: [x + str(s) for s in range(STEPS_) for x in n]

    def staged(front, mid, tail):
        out = []
        for s in range(STEPS_ + 2):
            for stage, d in ((front, 0), (mid, 1), (tail, 2)):
                if 0 <= s - d < STEPS_:
                    out += [x + str(s - d) for x in stage]
        return out

    PE = Steps(*staged(("sc",), ("pt", "pv"), ("at",)))
    DV = Steps(*staged(("s1_", "s2_", "mx", "ms", "nm", "sd"), ("den", "rec", "on"), ()))
    ac = []
    for s in range(STEPS_ + 2):
        if 0 <= s - 1 < STEPS_:
            ac.append(f"cp{s - 1}")
        if s < STEPS_:
            ac += [f"e{x}_{s}" for x in range(UN)] + [f"es{s}"]
        if 0 <= s - 2:
            ac.append(f"ac{s - 2}")
    AC = Steps(*ac)
    with ExitStack() as ctx:
        ident = A["sb_ident"]
        sb = lambda n, s: ctx.enter_context(nc.sbuf_tensor(n, s, F32))
        sem = lambda n: ctx.enter_context(nc.semaphore(n))
        relb, oneh = sb("a_relb", [REL_ROWS, NH]), sb("a_oneh", [REL_ROWS, 3 * WIN])
        tab = sb("a_tab", [NH, 3 * WIN])
        bias = sb("a_bias", [P, NH, 2 * WIN])
        sinks, sink8 = sb("a_sinks", [P, NH]), sb("a_sink8", [P, NH])
        pen = sb("a_pen", [P, NB])
        q = [sb(f"a_q{j}", [P, KT, WIN]) for j in range(NBUF)]
        kT, vT = sb("a_kT", [P, 2, WIN + NP]), sb("a_vT", [P, 2, NP])
        kb = [sb(f"a_kb{j}", [P, 2, 2 * WIN]) for j in range(NBUF)]
        vnat = sb("a_vnat", [P, NB + 1, NKV * HD])
        knat = sb("a_knat", [P, NKV * HD])
        Sx = [sb(f"a_S{j}", [P, UN, 2 * WIN]) for j in range(2)]
        PTs = [sb(f"a_PT{j}", [P, UN, 2, WIN]) for j in range(2)]
        on = [sb(f"a_on{j}", [P, UN * HD]) for j in range(2)]
        aT = [sb(f"a_aT{j}", [P, KT, WIN]) for j in range(NBUF)]
        mx, ms, nm, sd, es, sums, den = (sb("a_" + n, [P, STEPS_, UN]) for n in ("mx", "ms", "nm", "sd", "es", "sums", "den"))
        scp = [ctx.enter_context(nc.psum_tensor(f"a_scp{j}", [P, UN, 2 * WIN], F32)) for j in range(2)]
        ptp = ctx.enter_context(nc.psum_tensor("a_ptp", [P, UN, 2, WIN], F32))
        outp = ctx.enter_context(nc.psum_tensor("a_outp", [P, 1, UN * HD], F32))
        atp = ctx.enter_context(nc.psum_tensor("a_atp", [P, 1, 2, WIN], F32))
        const_in, tab_out, bias_in, kv_in = sem("a_const_in"), sem("a_tab_out"), sem("a_bias_in"), sem("a_kv_in")
        q_in = [sem(f"a_q_in{j}") for j in range(NBUF)]
        a_out = [sem(f"a_a_out{j}") for j in range(NBUF)]
        win_out, kb_ready = sem("a_win_out"), sem("a_kb_ready")
        pre_pe, pre_act, pre_dve = sem("a_pre_pe"), sem("a_pre_act"), sem("a_pre_dve")
        pe_done, act_done, dve_done = sem("a_pe_done"), sem("a_act_done"), sem("a_dve_done")
        block = ctx.enter_context(nc.Block())

        @block.sync
        def _(sp):
            for d, s in ((relb[0:REL_ROWS - 1, :], A["rel_bias"]), (oneh[:, :], A["onehot"]), (sinks[:, :], A["sinks"]), (pen[:, :], A["pen"])):
                sp.dma_start(d, s).then_inc(const_in, 16)
            for t in range(2):
                sp.dma_start(kT[:, t, WIN:], A["zT"][T_K + t, :, 0:NP]).then_inc(kv_in, 16)
                sp.dma_start(vT[:, t, :], A["zT"][T_V + t, :, 0:NP]).then_inc(kv_in, 16)
            sp.wait_ge(pre_act, 1)
            sp.dma_start(A["tab"], tab[:, :].unsqueeze(1).broadcast_to([NH, P, 3 * WIN])).then_inc(tab_out, 16)
            sp.wait_ge(tab_out, 16)
            for h in range(NH):
                src = bass.AP(A["tab"].tensor, h * P * 3 * WIN + WIN - 1, [[3 * WIN - 1, P], [1, 2 * WIN]])
                sp.dma_start(bias[:, h, :], src).then_inc(bias_in, 16)
            with sp.Fori(0, NB // NBUF) as i:
                for j in range(NBUF):
                    sp.wait_ge(pe_done, PE.n * i)
                    sp.dma_start(q[j][:, :, :], A["zT"][T_Q:T_Q + KT, :, bass.ds((NBUF * i + j) * WIN, WIN)]
                                 .rearrange("t p c -> p t c")).then_inc(q_in[j], 16)
            sp.wait_ge(pre_act, 2 + NB)
            sp.dma_start(A["win_k_p"], knat[:, :]).then_inc(win_out, 16)
            sp.dma_start(A["win_v_p"], vnat[:, NB, :]).then_inc(win_out, 16)
            sp.wait_ge(win_out, 32)

        @block.tensor
        def _(pe):
            pe.wait_ge(const_in, 64)
            pe.wait_ge(pre_dve, 1)
            pe.matmul(scp[0][0:NH, :, :].rearrange("p a b -> p (a b)")[:, 0:3 * WIN],
                      relb[:, :], oneh[:, :], start=True, stop=True).then_inc(pre_pe, 1)
            pe.wait_ge(kv_in, 64)
            for b in range(NB):
                if b >= 2:
                    pe.wait_ge(pre_act, b)
                for t in range(2):
                    mm = pe.transpose(ptp[:, 2 * (b % 2), t, :], vT[:, t, b * WIN:(b + 1) * WIN], ident[:, :])
                mm.then_inc(pre_pe, 1)
            pe.wait_ge(pre_act, NB)
            for t in range(2):
                mm = pe.transpose(ptp[:, 0, t, :], kT[:, t, NP:], ident[:, :])
            mm.then_inc(pre_pe, 1)
            pe.wait_ge(pre_act, 2 + NB)
            pe.wait_ge(pre_dve, 4)
            with pe.Fori(0, NB // NBUF) as i:
                for s in range(STEPS_ + 2):
                    if s < STEPS_:
                        j, u = s // UNITS, s % UNITS
                        if u == 0:
                            pe.wait_ge(q_in[j], 16 * i + 16)
                            pe.wait_ge(kb_ready, NBUF * i + j + 1)
                        if s >= 2:
                            pe.wait_ge(dve_done, DV.after(f"s2_{s - 2}", i))
                        else:
                            pe.wait_ge(dve_done, DV.n * i)
                            pe.wait_ge(act_done, AC.n * i)
                        for x in range(UN):
                            t, h = 2 * u + x % 2, x // 2
                            o = slice(h * HD, (h + 1) * HD)
                            mm = pe.matmul(scp[s % 2][:, x, :], q[j][o, t, :],
                                           kb[j][o, u // 2, :], start=True, stop=True)
                        mm.then_inc(pe_done, 1)
                    m = s - 1
                    if 0 <= m < STEPS_:
                        j, u = m // UNITS, m % UNITS
                        pe.wait_ge(act_done, AC.after(f"e{UN - 1}_{m}", i))
                        if m:
                            pe.wait_ge(act_done, AC.after(f"cp{m - 1}", i))
                        for x in range(UN):
                            for b in range(2):
                                mm = pe.transpose(ptp[:, x, b, :], Sx[m % 2][:, x, b * WIN:(b + 1) * WIN], ident[:, :])
                        mm.then_inc(pe_done, 1)
                        pe.wait_ge(act_done, AC.after(f"cp{m}", i))
                        if m >= 1:
                            pe.wait_ge(dve_done, DV.after(f"on{m - 1}", i))
                        for x in range(UN):
                            kv = 2 * (u // 2) + x // 2
                            c = 2 * (x % 2) + x // 2
                            for b in range(2):
                                mm = pe.matmul(outp[:, 0, c * HD:(c + 1) * HD], PTs[m % 2][:, x, b, :],
                                               vnat[:, bass.ds(NBUF * i + j + b, 1), kv * HD:(kv + 1) * HD].rearrange("p a b -> p (a b)"),
                                               start=(b == 0), stop=(b == 1))
                        mm.then_inc(pe_done, 1)
                    m = s - 2
                    if m >= 0:
                        pe.wait_ge(dve_done, DV.after(f"on{m}", i))
                        if m >= 1:
                            pe.wait_ge(act_done, AC.after(f"ac{m - 1}", i))
                        for x in range(2):
                            mm = pe.transpose(atp[:, 0, x, :], on[m % 2][:, x * P:(x + 1) * P], ident[:, :])
                        mm.then_inc(pe_done, 1)

        @block.scalar
        def _(act):
            act.wait_ge(pre_pe, 1)
            act.activation(tab[:, :], scp[0][0:NH, :, :].rearrange("p a b -> p (a b)")[:, 0:3 * WIN], ACT.Copy).then_inc(pre_act, 1)
            for b in range(NB):
                act.wait_ge(pre_pe, 2 + b)
                act.activation(vnat[:, b + 1, :], ptp[:, 2 * (b % 2), :, :].rearrange("p a b -> p (a b)"), ACT.Copy).then_inc(pre_act, 1)
            act.wait_ge(pre_pe, 2 + NB)
            act.activation(knat[:, :], ptp[:, 0, :, :].rearrange("p a b -> p (a b)"), ACT.Copy).then_inc(pre_act, 1)
            with act.Fori(0, NB // NBUF) as i:
                for s in range(STEPS_ + 2):
                    m = s - 1
                    if 0 <= m < STEPS_:
                        act.wait_ge(pe_done, PE.after(f"pt{m}", i))
                        if m >= 2:
                            act.wait_ge(pe_done, PE.after(f"pv{m - 2}", i))
                        act.activation(PTs[m % 2][:, :, :, :], ptp[:, :, :, :], ACT.Copy).then_inc(act_done, 1)
                    if s < STEPS_:
                        act.wait_ge(dve_done, DV.after(f"sd{s}", i))
                        for x in range(UN):
                            act.activation(Sx[s % 2][:, x, :], Sx[s % 2][:, x, :], ACT.Exp, bias=nm[:, s, x:x + 1],
                                           scale=HD ** -0.5, accum_out=sums[:, s, x:x + 1]).then_inc(act_done, 1)
                        act.activation(es[:, s, :], sd[:, s, :], ACT.Exp).then_inc(act_done, 1)
                    m = s - 2
                    if m >= 0:
                        j, u = m // UNITS, m % UNITS
                        act.wait_ge(pe_done, PE.after(f"at{m}", i))
                        if u == 0:
                            act.wait_ge(a_out[j], 16 * i)
                        act.activation(aT[j][:, 2 * u:2 * u + 2, :], atp[:, 0, :, :], ACT.Copy).then_inc(act_done, 1)

        @block.vector
        def _(dve):
            nc.vector.memset(relb[REL_ROWS - 1:REL_ROWS, :], 1.0).then_inc(pre_dve, 1)
            nc.vector.memset(kT[:, :, 0:WIN], 0.0).then_inc(pre_dve, 1)
            nc.vector.memset(vnat[:, 0, :], 0.0).then_inc(pre_dve, 1)
            dve.wait_ge(const_in, 64)
            nc.vector.tensor_scalar(sink8[:, :], sinks[:, :], HD ** 0.5, None, ALU.mult).then_inc(pre_dve, 1)
            dve.wait_ge(pre_dve, 4)
            dve.wait_ge(bias_in, 16 * NH)
            with dve.Fori(0, NB // NBUF) as i:
                def do(name, ins):
                    ins.then_inc(dve_done, 1)
                    dve.wait_ge(dve_done, DV.after(name, i))

                for s in range(STEPS_ + 1):
                    if s < STEPS_:
                        j, u = s // UNITS, s % UNITS
                        hs = slice(u * UN, (u + 1) * UN)
                        dve.wait_ge(pe_done, PE.after(f"sc{s}", i))
                        if s >= 2:
                            dve.wait_ge(pe_done, PE.after(f"pt{s - 2}", i))
                        do(f"s1_{s}", nc.vector.scalar_tensor_tensor(Sx[s % 2][:, :, 0:WIN], scp[s % 2][:, :, 0:WIN], pen[:, bass.ds(NBUF * i + j, 1)],
                                                                     bias[:, hs, 0:WIN], ALU.add, ALU.add))
                        do(f"s2_{s}", nc.vector.tensor_tensor(Sx[s % 2][:, :, WIN:], scp[s % 2][:, :, WIN:], bias[:, hs, WIN:], ALU.add))
                        do(f"mx{s}", nc.vector.tensor_reduce(mx[:, s, :], Sx[s % 2][:, :, :], AX_X, ALU.max))
                        do(f"ms{s}", nc.vector.tensor_tensor(ms[:, s, :], mx[:, s, :], sink8[:, hs], ALU.max))
                        do(f"nm{s}", nc.vector.tensor_scalar(nm[:, s, :], ms[:, s, :], -(HD ** -0.5), None, ALU.mult))
                        do(f"sd{s}", nc.vector.tensor_tensor(sd[:, s, :], sinks[:, hs], nm[:, s, :], ALU.add))
                    m = s - 1
                    if 0 <= m:
                        dve.wait_ge(act_done, AC.after(f"es{m}", i))
                        do(f"den{m}", nc.vector.tensor_tensor(den[:, m, :], sums[:, m, :], es[:, m, :], ALU.add))
                        do(f"rec{m}", nc.vector.reciprocal(den[:, m, :], den[:, m, :]))
                        dve.wait_ge(pe_done, PE.after(f"pv{m}", i))
                        if m >= 2:
                            dve.wait_ge(pe_done, PE.after(f"at{m - 2}", i))
                        do(f"on{m}", nc.vector.tensor_tensor(on[m % 2][:, :].rearrange("p (t h d) -> p t h d", t=2, h=2),
                                                             outp[:, 0, :].rearrange("p (t h d) -> p t h d", t=2, h=2),
                                                             den[:, m, :].rearrange("p (h t) -> p t h", h=2).unsqueeze(3).broadcast_to([P, 2, 2, HD]),
                                                             ALU.mult))

        @block.gpsimd
        def _(pool):
            pool.wait_ge(kv_in, 64)
            pool.wait_ge(pre_dve, 4)
            with pool.Fori(0, NB // NBUF) as i:
                pool.wait_ge(pe_done, PE.n * i)
                for j in range(NBUF):
                    nc.gpsimd.tensor_copy(kb[j][:, :, :], kT[:, :, bass.ds((NBUF * i + j) * WIN, 2 * WIN)]).then_inc(kb_ready, 1)
                for j in range(NBUF):
                    pool.wait_ge(act_done, AC.after(f"ac{UNITS * (j + 1) - 1}", i))
                    stand_alone(pool, A)
                    pool.dma_start(A["aT"][:, :, bass.ds((NBUF * i + j) * WIN, WIN)].rearrange("t p c -> p t c"),
                                   aT[j][:, :, :]).then_inc(a_out[j], 16)
            for j in range(NBUF):
                pool.wait_ge(a_out[j], 16 * (NB // NBUF))


def decode(nc, A):
    BH = NS * NH
    J = WIN + 1
    R_, W_, K_, V_, KK_, KKA_ = range(6)
    DV = Steps("ones", "sink8", "sT0", "sT1", "qk", "self", "s_own", "s_raw", "s", "mx", "ms", "nm", "sd", "den", "rec", "p",
               "t0", "sa", "Sw", "t1", "S1", "t2", "S2", "t3", "y",
               "mu", "mun", "yc", "y2", "var", "tv", "ri", "yn", "b0", "b1", "b2", "b3")
    with ExitStack() as ctx:
        ident = A["sb_ident"]
        sb = lambda n, s: ctx.enter_context(nc.sbuf_tensor(n, s, F32))
        sem = lambda n: ctx.enter_context(nc.semaphore(n))
        bank = lambda n: ctx.enter_context(nc.psum_tensor(n, [P, 512], F32))
        relb, oneh = sb("d_relb", [REL_ROWS, BH]), sb("d_oneh", [REL_ROWS, 3 * WIN])
        sinks, sink8 = sb("d_sinks", [P, 1]), sb("d_sink8", [P, 1])
        qT = sb("d_qT", [P, KT, NS])
        kc, vc = sb("d_kc", [P, NS, 2, WIN]), sb("d_vc", [P, NS, NKV * HD])
        qn, kn = sb("d_qn", [P, HD]), sb("d_kn", [P, HD])
        vrow, prow = sb("d_vrow", [1, NS, NKV * HD]), sb("d_prow", [1, BH])
        sT, s = sb("d_sT", [P, BH]), sb("d_s", [P, J])
        pT, oT = sb("d_pT", [P, BH]), sb("d_oT", [P, KT, NS])
        small = sb("d_small", [P, 16])
        vec = sb("d_vec", [P, 6, HD])
        S, tmp = sb("d_S", [P, HD, HD]), sb("d_tmp", [P, HD, HD])
        sa, y, y2 = sb("d_sa", [P, HD]), sb("d_y", [P, HD]), sb("d_y2", [P, HD])
        yrow = sb("d_yrow", [NS, DM])
        prm = sb("d_prm", [P, NPAIR, NPRM])
        gate, bonus, b_ = sb("d_gate", [P, NPAIR, NS]), sb("d_bonus", [P, NPAIR, NS]), sb("d_b", [P, NPAIR, NS])
        sc0, sc1, bp, tp, pp, op, rp, yp = (bank("d_ps" + n) for n in ("sc0", "sc1", "bp", "tp", "pp", "op", "rp", "yp"))
        att_in, own_in, rwkv_in, y_out, y_in, state_in = (sem("d_" + n) for n in ("att_in", "own_in", "rwkv_in", "y_out", "y_in", "state_in"))
        out_done, caches_out = sem("d_out_done"), sem("d_caches_out")
        pe_done, act_done, dve_done = sem("d_pe_done"), sem("d_act_done"), sem("d_dve_done")
        PE = Steps("bias", "sc", "tp", "pT", "prow", "o", "yT")
        AC = Steps("p", "es", "pT", "prow", "oT", "std")
        block = ctx.enter_context(nc.Block())
        mx, ms, nm, sd, es, sums, den, own, mu, var = (small[:, i:i + 1] for i in range(10))

        @block.sync
        def _(sp):
            for d, s_ in ((relb[:, :], A["rel_bias_d"]), (oneh[:, :], A["onehot"]), (sinks[:, :], A["sinks_d"]),
                          (kc[:, :, :, :], A["kc"]), (vc[:, :, :], A["vc"]),
                          (qT[:, :, :], A["zT"][T_Q:T_Q + KT, :, NP:].rearrange("t p b -> p t b"))):
                sp.dma_start(d, s_).then_inc(att_in, 16)
            zn = A["zn"]
            for b in range(NS):
                rows = slice(b * NH, (b + 1) * NH)
                sp.dma_start(qn[rows, :], zn[1 + b, T_Q:T_Q + KT, :].rearrange("t (h d) -> (t h) d", h=2)).then_inc(own_in, 16)
                for g in range(2):
                    for t in range(4):
                        r = b * NH + g * 8 + t * 2
                        sp.dma_start(kn[r:r + 2, :], zn[1 + b, T_K + g, :].rearrange("(h d) -> h d", h=2)).then_inc(own_in, 16)
                sp.dma_start(vrow[0:1, b, :], zn[1 + b:2 + b, T_V:T_V + 2, :].rearrange("a t f -> a (t f)")).then_inc(own_in, 16)
            sp.wait_ge(act_done, AC.after("oT"))
            sp.dma_start(A["aT"][:, :, NP:].rearrange("t p b -> p t b"), oT[:, :, :]).then_inc(out_done, 16)
            sp.wait_ge(dve_done, DV.after("yn"))
            sp.dma_start(A["yd"].rearrange("b (h d) -> (b h) d", d=HD), y[:, :]).then_inc(y_out, 16)
            sp.wait_ge(y_out, 16)
            sp.dma_start(yrow[:, :], A["yd"]).then_inc(y_in, 16)
            sp.wait_ge(dve_done, DV.after("b3"))
            sp.dma_start(A["bT"][:, :, NP:].rearrange("t p b -> p t b"), b_[:, :, :]).then_inc(out_done, 16)
            sp.wait_ge(out_done, 32)

        @block.gpsimd
        def _(pool):
            zn = A["zn"]
            for cache, out, t in ((A["cache_k"], A["win_k_s"], T_K), (A["cache_v"], A["win_v_s"], T_V)):
                pool.dma_start(out[:, 0:WIN - 1, :], cache[:, 1:, :]).then_inc(caches_out, 16)
                pool.dma_start(out[:, WIN - 1, :], zn[1:, t:t + 2, :].rearrange("b t f -> b (t f)")).then_inc(caches_out, 16)
            for n, q in enumerate((Q_PAIR_R, Q_PAIR_K, Q_PAIR_V)):
                pool.dma_start(A["shift"][:, n * DM:(n + 1) * DM].rearrange("b (p f) -> b p f", f=P),
                               zn[:, T_PAIR + q:N_TILES:3, :]).then_inc(caches_out, 16)
            pool.dma_start(A["shift"][:, 3 * DM:].rearrange("b (t f) -> b t f", f=P), zn[:, T_XWA:T_XG + 1, :]).then_inc(caches_out, 16)
            pool.wait_ge(dve_done, DV.after("S2"))
            pool.dma_start(A["wkv_s"], S[:, :, :].rearrange("p v k -> p (v k)")).then_inc(caches_out, 16)
            pool.wait_ge(caches_out, 16 * 9)

        @block.tensor
        def _(pe):
            pe.wait_ge(att_in, 16 * 6)
            pe.matmul(bp[:, 0:J], relb[:, :], oneh[:, WIN - 1:2 * WIN], start=True, stop=True).then_inc(pe_done, 1)
            for b in range(NS):
                for g in range(2):
                    for h, dst in ((0, sc0), (1, sc1)):
                        o = slice(h * HD, (h + 1) * HD)
                        mm = pe.matmul(dst[:, b * KT + 4 * g:b * KT + 4 * g + 4], kc[o, b, g, :],
                                       qT[o, 4 * g:4 * g + 4, b], start=True, stop=True)
            mm.then_inc(pe_done, 1)
            pe.wait_ge(dve_done, DV.after("sT1"))
            pe.transpose(tp[:, 0:WIN], sT[:, :], ident[:, :]).then_inc(pe_done, 1)
            pe.wait_ge(dve_done, DV.after("p"))
            pe.transpose(pp[:, 0:BH], s[:, 0:WIN], ident[:, :]).then_inc(pe_done, 1)
            pe.transpose(rp[0:1, 0:BH], s[:, WIN:J], ident[:, :]).then_inc(pe_done, 1)
            pe.wait_ge(act_done, AC.after("prow"))
            pe.wait_ge(own_in, 16 * 10 * NS)
            for b in range(NS):
                for g in range(2):
                    for h in range(2):
                        kv = 2 * g + h
                        dst = op[h * HD:(h + 1) * HD, 0:KT * NS].rearrange("p (t b) -> p t b", b=NS)[:, 4 * g:4 * g + 4, b]
                        c = b * NH + 8 * g + h
                        pe.matmul(dst, vc[:, b, kv * HD:(kv + 1) * HD], pT[:, c:c + 7:2], start=True, stop=False)
                        mm = pe.matmul(dst, vrow[0:1, b, kv * HD:(kv + 1) * HD], prow[0:1, c:c + 7:2], start=False, stop=True)
            mm.then_inc(pe_done, 1)
            pe.wait_ge(y_in, 16)
            for t in range(NPAIR):
                mm = pe.transpose(yp[:, t * NS:(t + 1) * NS], yrow[:, t * P:(t + 1) * P], ident[0:NS, 0:NS])
            mm.then_inc(pe_done, 1)

        @block.scalar
        def _(act):
            act.dma_start(vec[:, :, :], A["decn"].rearrange("b p h q d -> (b p h) q d")).then_inc(rwkv_in, 16)
            act.dma_start(S[:, :, :].rearrange("p v k -> p (v k)"), A["state"]).then_inc(state_in, 16)
            for d, s_ in ((prm[:, :, :], A["prm"]), (gate[:, :, :], A["gate"][:, :, NP:].rearrange("t p b -> p t b")),
                          (bonus[:, :, :], A["bonus"][:, :, NP:].rearrange("t p b -> p t b"))):
                act.dma_start(d, s_).then_inc(rwkv_in, 16)
            act.wait_ge(dve_done, DV.after("sd"))
            act.activation(s[:, :], s[:, :], ACT.Exp, bias=nm, scale=HD ** -0.5, accum_out=sums).then_inc(act_done, 1)
            act.activation(es, sd, ACT.Exp).then_inc(act_done, 1)
            act.wait_ge(pe_done, PE.after("pT"))
            act.activation(pT[:, :], pp[:, 0:BH], ACT.Copy).then_inc(act_done, 1)
            act.wait_ge(pe_done, PE.after("prow"))
            act.activation(prow[:, :], rp[0:1, 0:BH], ACT.Copy).then_inc(act_done, 1)
            act.wait_ge(pe_done, PE.after("o"))
            act.activation(oT[:, :, :].rearrange("p t b -> p (t b)"), op[:, 0:KT * NS], ACT.Copy).then_inc(act_done, 1)
            act.wait_ge(dve_done, DV.after("tv"))
            act.activation(var, var, ACT.Sqrt).then_inc(act_done, 1)

        @block.vector
        def _(dve):
            V = nc.vector

            def do(name, ins):
                ins.then_inc(dve_done, 1)
                dve.wait_ge(dve_done, DV.after(name))

            over_v = lambda n: vec[:, n, :].unsqueeze(1).broadcast_to([P, HD, HD])
            over_k = lambda ap: ap.unsqueeze(2).broadcast_to([P, HD, HD])
            dve.wait_ge(att_in, 16 * 6)
            do("ones", V.memset(small[:, :], 0.0))
            do("sink8", V.tensor_scalar(sink8[:, :], sinks[:, :], HD ** 0.5, None, ALU.mult))
            dve.wait_ge(pe_done, PE.after("sc"))
            for h, src in ((0, sc0), (1, sc1)):
                do(f"sT{h}", V.tensor_copy(sT[:, h:BH:2], src[:, 0:BH // 2]))
            dve.wait_ge(own_in, 16 * 10 * NS)
            do("qk", V.tensor_tensor(qn[:, :], qn[:, :], kn[:, :], ALU.mult))
            do("self", V.tensor_reduce(own, qn[:, :], AX_X, ALU.add))
            dve.wait_ge(pe_done, PE.after("tp"))
            do("s_own", V.tensor_copy(s[:, WIN:J], own))
            do("s_raw", V.tensor_copy(s[:, 0:WIN], tp[:, 0:WIN]))
            do("s", V.tensor_tensor(s[:, :], s[:, :], bp[:, 0:J], ALU.add))
            do("mx", V.tensor_reduce(mx, s[:, :], AX_X, ALU.max))
            do("ms", V.tensor_tensor(ms, mx, sink8[:, :], ALU.max))
            do("nm", V.tensor_scalar(nm, ms, -(HD ** -0.5), None, ALU.mult))
            do("sd", V.tensor_tensor(sd, sinks[:, :], nm, ALU.add))
            dve.wait_ge(act_done, AC.after("es"))
            do("den", V.tensor_tensor(den, sums, es, ALU.add))
            do("rec", V.reciprocal(den, den))
            do("p", V.tensor_scalar(s[:, :], s[:, :], den, None, ALU.mult))
            dve.wait_ge(rwkv_in, 64)
            dve.wait_ge(state_in, 16)
            do("t0", V.tensor_tensor(tmp[:, :, :], S[:, :, :], over_v(KK_), ALU.mult))
            do("sa", V.tensor_reduce(sa[:, :], tmp[:, :, :], AX_X, ALU.add))
            do("Sw", V.tensor_tensor(S[:, :, :], S[:, :, :], over_v(W_), ALU.mult))
            do("t1", V.tensor_tensor(tmp[:, :, :], over_k(sa[:, :]), over_v(KKA_), ALU.mult))
            do("S1", V.tensor_tensor(S[:, :, :], S[:, :, :], tmp[:, :, :], ALU.subtract))
            do("t2", V.tensor_tensor(tmp[:, :, :], over_k(vec[:, V_, :]), over_v(K_), ALU.mult))
            do("S2", V.tensor_tensor(S[:, :, :], S[:, :, :], tmp[:, :, :], ALU.add))
            do("t3", V.tensor_tensor(tmp[:, :, :], S[:, :, :], over_v(R_), ALU.mult))
            do("y", V.tensor_reduce(y[:, :], tmp[:, :, :], AX_X, ALU.add))
            do("mu", V.tensor_reduce(mu, y[:, :], AX_X, ALU.add))
            do("mun", V.tensor_scalar(mu, mu, -1.0 / HD, None, ALU.mult))
            do("yc", V.tensor_scalar(y[:, :], y[:, :], mu, None, ALU.add))
            do("y2", V.tensor_tensor(y2[:, :], y[:, :], y[:, :], ALU.mult))
            do("var", V.tensor_reduce(var, y2[:, :], AX_X, ALU.add))
            do("tv", V.tensor_scalar(var, var, 1.0 / HD, GN_EPS, ALU.mult, ALU.add))
            dve.wait_ge(act_done, AC.after("std"))
            do("ri", V.reciprocal(var, var))
            do("yn", V.tensor_scalar(y[:, :], y[:, :], var, None, ALU.mult))
            dve.wait_ge(pe_done, PE.after("yT"))
            per = lambda c: prm[:, :, c:c + 1].broadcast_to([P, NPAIR, NS])
            do("b0", V.tensor_tensor(b_[:, :, :], yp[:, 0:NPAIR * NS].rearrange("p (t b) -> p t b", b=NS), per(C_LG), ALU.mult))
            do("b1", V.tensor_tensor(b_[:, :, :], b_[:, :, :], per(C_LB), ALU.add))
            do("b2", V.tensor_tensor(b_[:, :, :], b_[:, :, :], bonus[:, :, :], ALU.add))
            do("b3", V.tensor_tensor(b_[:, :, :], b_[:, :, :], gate[:, :, :], ALU.mult))


def merge(nc, A):
    with ExitStack() as ctx:
        sb = lambda n, s: ctx.enter_context(nc.sbuf_tensor(n, s, F32))
        sem = lambda n: ctx.enter_context(nc.semaphore(n))
        src = [sb("m_aT", [P, KT, NT]), sb("m_bT", [P, KT, NT])]
        w = [[sb(f"m_w{j}{x}", [P, KT, P]) for x in range(2)] for j in range(2)]
        g = [[sb(f"m_g{j}{x}", [P, NT]) for x in range(2)] for j in range(2)]
        m = [sb(f"m_m{j}", [P, NT]) for j in range(2)]
        zero = sb("m_zero", [P, NPAD - NT])
        ps = [ctx.enter_context(nc.psum_tensor(f"m_ps{x}", [P, 3, 512], F32)) for x in range(2)]
        src_in = [sem("m_a_in"), sem("m_b_in")]
        w_in = [[sem(f"m_w_in{j}{x}") for x in range(2)] for j in range(2)]
        g_in = [sem(f"m_g_in{j}") for j in range(2)]
        m_out = [sem(f"m_m_out{j}") for j in range(2)]
        zeroed, pad_out = sem("m_zeroed"), sem("m_pad_out")
        pe_done, act_done, dve_done = sem("m_pe_done"), sem("m_act_done"), sem("m_dve_done")
        PE = Steps("a0", "b0", "a1", "b1")
        AC = Steps("ga0", "gb0", "ga1", "gb1")
        DV = Steps("ma0", "mb0", "m0", "ma1", "mb1", "m1")
        block = ctx.enter_context(nc.Block())

        @block.sync
        def _(sp):
            for x, name in enumerate(("aT", "bT")):
                for k in range(KT):
                    sp.dma_start(src[x][:, k, :], A[name][k]).then_inc(src_in[x], 16)
            with sp.Fori(0, KT // 2) as i:
                for j in range(2):
                    sp.wait_ge(pe_done, PE.n * i)
                    for x, name in enumerate(("wba_tiles", "wbr_tiles")):
                        sp.dma_start(w[j][x][:, :, :], A[name][2 * i + j]).then_inc(w_in[j][x], 16)
                    sp.wait_ge(dve_done, DV.n * i)
                    for x, t in enumerate((T_GA, T_GB)):
                        sp.dma_start(g[j][x][:, :], A["zT"][2 * i + j + t]).then_inc(g_in[j], 16)

        @block.tensor
        def _(pe):
            with pe.Fori(0, KT // 2) as i:
                for j in range(2):
                    for x in range(2):
                        pe.wait_ge(src_in[x], 16 * KT)
                        pe.wait_ge(w_in[j][x], 16 * i + 16)
                        if j == 0:
                            pe.wait_ge(dve_done, DV.n * i)
                        else:
                            pe.wait_ge(dve_done, DV.after(("ma0", "mb0")[x], i))
                        for c in range(3):
                            for k in range(KT):
                                mm = pe.matmul(ps[x][:, c, 0:TG], w[j][x][:, k, :], src[x][:, k, c * TG:(c + 1) * TG],
                                               start=(k == 0), stop=(k == KT - 1))
                        mm.then_inc(pe_done, 1)

        @block.scalar
        def _(act):
            with act.Fori(0, KT // 2) as i:
                for j in range(2):
                    act.wait_ge(g_in[j], 32 * i + 32)
                    for x in range(2):
                        act.activation(g[j][x][:, :], g[j][x][:, :], ACT.Sigmoid).then_inc(act_done, 1)

        @block.vector
        def _(dve):
            nc.vector.memset(zero[:, :], 0.0).then_inc(zeroed, 1)
            with dve.Fori(0, KT // 2) as i:
                def do(name, ins):
                    ins.then_inc(dve_done, 1)
                    dve.wait_ge(dve_done, DV.after(name, i))

                for j in range(2):
                    dve.wait_ge(m_out[j], 16 * i)
                    for x, n in enumerate("ab"):
                        dve.wait_ge(act_done, AC.after(f"g{n}{j}", i))
                        dve.wait_ge(pe_done, PE.after(f"{n}{j}", i))
                        do(f"m{n}{j}", nc.vector.tensor_tensor(grouped(g[j][x][:, :]), ps[x][:, :, 0:TG], grouped(g[j][x][:, :]), ALU.mult))
                    do(f"m{j}", nc.vector.tensor_tensor(m[j][:, :], g[j][0][:, :], g[j][1][:, :], ALU.add))

        @block.gpsimd
        def _(pool):
            pool.wait_ge(zeroed, 1)
            for k in range(KT):
                pool.dma_start(A["mT"][k, :, NT:], zero[:, :]).then_inc(pad_out, 16)
            with pool.Fori(0, KT // 2) as i:
                for j in range(2):
                    pool.wait_ge(dve_done, DV.after(f"m{j}", i))
                    pool.dma_start(A["mT"][2 * i + j, :, 0:NT], m[j][:, :]).then_inc(m_out[j], 16)
            pool.wait_ge(pad_out, 16 * KT)
            for j in range(2):
                pool.wait_ge(m_out[j], 16 * (KT // 2))


PH, NKEY, TOPK = 8, 128, 16
SLOTS = PH * TOPK
CAND = [(i, TOPK // (i + 1)) for i in range(TOPK)]
NCAND = sum(n for _, n in CAND)
LOW = -3.0e38


def peer(nc, A):
    RING = 16
    USES = 2 * SLOTS // RING
    ON_DVE = 4
    NV = SLOTS // ON_DVE
    with ExitStack() as ctx:
        ident = A["sb_ident"]
        sb = lambda n, s, d=F32: ctx.enter_context(nc.sbuf_tensor(n, s, d))
        sem = lambda n: ctx.enter_context(nc.semaphore(n))
        psum = lambda n, w: ctx.enter_context(nc.psum_tensor(n, [P, w], F32))
        wo, wq = sb("f_wo", [P, KT, DM]), sb("f_wq", [P, KT, DM])
        keys = sb("f_keys", [P, PH, NKEY])
        ln = sb("f_ln", [P, 4, DM])
        ring = sb("f_ring", [P, RING, DM])
        mTb, xb = sb("f_mTb", [P, KT, P]), sb("f_xb", [P, DM])
        h = [sb(f"f_h{j}", [P, DM]) for j in range(2)]
        hT = sb("f_hT", [P, KT, P])
        scs = sb("f_scs", [P, 2, PH, NKEY])
        st, ag, rs = sb("f_st", [P, 2, 6]), sb("f_ag", [P, 2]), sb("f_rs", [P, 1])
        st2, ag2, rs2 = sb("f_st2", [P, 2, 6]), sb("f_ag2", [P, 2]), sb("f_rs2", [P, 1])
        s2 = sb("f_s2", [P, NKEY])
        sv, si, sif = sb("f_sv", [P, 2, PH, TOPK]), sb("f_si", [P, 2, PH, TOPK], U32), sb("f_sif", [P, 2, PH, TOPK])
        cand, cidx, iota = sb("f_cand", [P, PH, NCAND]), sb("f_cidx", [P, PH, NCAND]), sb("f_iota", [P, NCAND])
        c2 = sb("f_c2", [P, NCAND])
        fv, fi, fif = sb("f_fv", [P, PH, TOPK]), sb("f_fi", [P, PH, TOPK], U32), sb("f_fif", [P, PH, TOPK])
        eq = sb("f_eq", [P, TOPK, NCAND])
        ef = sb("f_ef", [P, PH, TOPK])
        eidx = [sb(f"f_eidx{j}", [P, SLOTS], U32) for j in range(2)]
        gate = [sb(f"f_gate{j}", [P, PH, TOPK]) for j in range(2)]
        gs = sb("f_gs", [P, PH])
        dots, wts = sb("f_dots", [P, SLOTS]), sb("f_wts", [P, SLOTS])
        diag = [sb(f"f_diag{r}", [P, P]) for r in range(4)]
        yacc = sb("f_yacc", [P, DM])
        flag = sb("f_flag", [1, 1])
        wexp = sb("f_wexp", [P, NS, NS])
        fps, sps, yps = psum("f_fps", 1024), psum("f_sps", 2048), psum("f_yps", 1024)
        const_in, ld_m, ld_x = sem("f_const_in"), sem("f_ld_m"), sem("f_ld_x")
        (mixed, h0_done, var_done, std_done, h_done, hT_psum, hT_done, q_psum, q_done, sc_psum, sc_done, topk_done,
         idx_done, fv_done, fe_done) = (sem("f_" + n) for n in (
             "mixed", "h0_done", "var_done", "std_done", "h_done", "hT_psum", "hT_done", "q_psum", "q_done", "sc_psum",
             "sc_done", "topk_done", "idx_done", "fv_done", "fe_done"))
        gelu_done, w_done, y_read, var2_done, std2_done, y_done = (sem("f_" + n) for n in (
            "gelu_done", "w_done", "y_read", "var2_done", "std2_done", "y_done"))
        y_out = sem("f_y_out")
        got = [sem(f"f_got{r}") for r in range(RING)]
        used = [sem(f"f_used{r}") for r in range(RING)]
        diag_done, link = sem("f_diag_done"), sem("f_link")
        (d_ready, d_by_slot, d_idx, d_select, d_spread, d_gelu, d_w, d_sum, d_var, d_std, d_done, d_out) = (sem("f_d_" + n) for n in (
            "ready", "by_slot", "idx", "select", "spread", "gelu", "w", "sum", "var", "std", "done", "out"))
        block = ctx.enter_context(nc.Block())
        on_pe = [s for s in range(SLOTS) if s % ON_DVE != ON_DVE - 1]

        @block.sync
        def _(sp):
            for k in range(KT):
                sp.dma_start(wo[:, k, :], A["w_out"][k]).then_inc(const_in, 16)

            def load(f):
                sp.wait_ge(mixed, f)
                sp.dma_start(mTb[:, :, :], A["mT"][:, :, bass.ds(f * P, P)].rearrange("t p c -> p t c")).then_inc(ld_m, 16)
                sp.wait_ge(h0_done, f)
                sp.dma_start(xb[:, :], A["x_pad"][f]).then_inc(ld_x, 16)

            load(0)
            for k in range(KT):
                sp.dma_start(wq[:, k, :], A["peer_q"][k]).then_inc(const_in, 16)
            for d, s in ((keys[:, :, :], A["keysT"]), (ln[:, :, :], A["ln"]), (iota[:, :], A["iota"])):
                sp.dma_start(d, s).then_inc(const_in, 16)
            with sp.Fori(0, NB // 2) as i:
                for j in range(2):
                    b = 2 * i + j
                    load(b + 1)
                    sp.wait_ge(y_done, b + 1)
                    sp.dma_start(A["y"][bass.ds(b * P, P), :], yacc[:, :]).then_inc(y_out, 16)
            sp.wait_ge(y_out, 16 * NB)
            sp.wait_ge(d_done, 1)
            sp.dma_start(A["y"][NP:NT, :], yacc[0:NS, :]).then_inc(d_out, 16)
            sp.wait_ge(d_out, 16)

        @block.gpsimd
        def _(pool):
            with pool.Fori(0, NB // 2) as i:
                for j in range(2):
                    b = 2 * i + j
                    pool.wait_ge(idx_done, b + 1)
                    for n in range(2 * SLOTS):
                        table, s, r = ("peer_u", "peer_v")[n // SLOTS], n % SLOTS, n % RING
                        pool.wait_ge(used[r], USES * b + n // RING)
                        stand_alone(pool, A)
                        pool.indirect_dma_start(out=ring[:, r, :], out_offset=None, in_=A[table],
                                                in_offset=bass.IndirectOffsetOnAxis(ap=eidx[j][:, s:s + 1], axis=0)).then_inc(got[r], 16)
            pool.wait_ge(d_idx, 1)
            for n in range(2 * NS):
                pool.wait_ge(used[n], USES * NB)
                pool.indirect_dma_start(out=ring[:, n, :], out_offset=None, in_=A[("peer_u", "peer_v")[n // NS]],
                                        in_offset=bass.IndirectOffsetOnAxis(ap=fi[:, 0, n % NS:n % NS + 1], axis=0)).then_inc(got[n], 16)

        @block.tensor
        def _(pe):
            def front(f):
                pe.wait_ge(ld_m, 16 * f + 16)
                pe.wait_ge(q_done, f)
                for c in range(2):
                    for k in range(KT):
                        mm = pe.matmul(fps[:, c * 512:(c + 1) * 512], mTb[:, k, :], wo[:, k, c * 512:(c + 1) * 512],
                                       start=(k == 0), stop=(k == KT - 1))
                mm.then_inc(mixed, 1)

            def front2(f, j):
                pe.wait_ge(h_done, f + 1)
                for k in range(KT):
                    mm = pe.transpose(fps[:, k * P:(k + 1) * P], h[j][:, k * P:(k + 1) * P], ident[:, :])
                mm.then_inc(hT_psum, 1)
                pe.wait_ge(hT_done, f + 1)
                for x in range(PH):
                    for k in range(KT):
                        mm = pe.matmul(fps[:, x * P:(x + 1) * P], wq[:, k, x * P:(x + 1) * P], hT[:, k, :],
                                       start=(k == 0), stop=(k == KT - 1))
                mm.then_inc(q_psum, 1)
                pe.wait_ge(q_done, f + 1)
                pe.wait_ge(sc_done, 2 * f)
                for x in range(PH):
                    for c in range(2):
                        mm = pe.matmul(sps[:, (c * PH + x) * NKEY:(c * PH + x + 1) * NKEY], hT[c * HD:(c + 1) * HD, x, :],
                                       keys[c * HD:(c + 1) * HD, x, :], start=True, stop=True)
                mm.then_inc(sc_psum, 1)

            pe.wait_ge(const_in, 16 * KT)
            front(0)
            pe.wait_ge(const_in, 16 * (2 * KT + 3))
            front2(0, 0)
            with pe.Fori(0, NB // 2) as i:
                for j in range(2):
                    b = 2 * i + j
                    front(b + 1)
                    front2(b + 1, 1 - j)
                    pe.wait_ge(y_read, b)
                    for m, s in enumerate(on_pe):
                        n = SLOTS + s
                        pe.wait_ge(diag_done, len(on_pe) * b + m + 1)
                        pe.wait_ge(got[n % RING], 16 * (USES * b + n // RING + 1))
                        for c in range(2):
                            mm = pe.matmul(yps[:, c * 512:(c + 1) * 512], diag[m % 4][:, :], ring[:, n % RING, c * 512:(c + 1) * 512],
                                           start=(m == 0), stop=(m == len(on_pe) - 1))
                        mm.then_inc(used[n % RING], 1)
            pe.wait_ge(d_ready, 1)
            pe.transpose(fps[:, 0:NS], ef[0:NS, :, :].rearrange("p a b -> p (a b)"), ident[0:NS, 0:NS])
            pe.transpose(fps[:, 512:512 + NS], gate[0][0:NS, :, :].rearrange("p a b -> p (a b)"), ident[0:NS, 0:NS]).then_inc(d_by_slot, 1)
            pe.wait_ge(d_select, 1)
            for t in range(NS):
                if t >= 2:
                    pe.wait_ge(used[t - 2], USES * NB + 1)
                for c in range(2):
                    mm = pe.matmul(sps[:, (t % 2) * DM + c * 512:(t % 2) * DM + (c + 1) * 512], scs[0:NS, 0, t, :],
                                   h[0][0:NS, c * 512:(c + 1) * 512], start=True, stop=True)
                mm.then_inc(d_spread, 1)
            pe.wait_ge(d_w, 1)
            for t in range(NS):
                pe.wait_ge(got[NS + t], 16 * (USES * NB + 1))
                for c in range(2):
                    mm = pe.matmul(yps[0:NS, c * 512:(c + 1) * 512], wexp[:, t, :], ring[:, NS + t, c * 512:(c + 1) * 512], start=(t == 0), stop=(t == NS - 1))
            mm.then_inc(d_sum, 1)

        @block.scalar
        def _(act):
            def front(f):
                act.wait_ge(var_done, f + 1)
                act.activation(rs[:, :], rs[:, :], ACT.Sqrt).then_inc(std_done, 1)
                act.wait_ge(hT_psum, f + 1)
                act.wait_ge(sc_psum, f)
                act.activation(hT[:, :, :].rearrange("p a b -> p (a b)"), fps[:, :], ACT.Copy).then_inc(hT_done, 1)
                act.wait_ge(q_psum, f + 1)
                act.activation(hT[:, :, :].rearrange("p a b -> p (a b)"), fps[:, :], ACT.Copy).then_inc(q_done, 1)
                act.wait_ge(sc_psum, f + 1)
                act.wait_ge(topk_done, f)
                for c in range(2):
                    act.activation(scs[:, c, :, :].rearrange("p a b -> p (a b)"), sps[:, c * 1024:(c + 1) * 1024], ACT.Copy).then_inc(sc_done, 1)

            def soften(f, j):
                act.wait_ge(fv_done, f + 1)
                act.activation(gate[j][:, :, :], gate[j][:, :, :], ACT.Exp).then_inc(fe_done, 1)

            front(0)
            soften(0, 0)
            with act.Fori(0, NB // 2) as i:
                for j in range(2):
                    b = 2 * i + j
                    front(b + 1)
                    for r in range(RING):
                        act.wait_ge(used[r], USES * b + USES // 2)
                    act.activation(dots[:, :], dots[:, :], ACT.Gelu).then_inc(gelu_done, 1)
                    act.wait_ge(w_done, b + 1)
                    for m, s in enumerate(on_pe):
                        if m < 4:
                            act.wait_ge(y_read, b)
                        else:
                            n = SLOTS + on_pe[m - 4]
                            act.wait_ge(used[n % RING], USES * b + n // RING + 1)
                        act.activation(diag[m % 4][:, :], ident[:, :], ACT.Copy, scale=wts[:, s:s + 1]).then_inc(diag_done, 1)
                    soften(b + 1, 1 - j)
                    act.wait_ge(var2_done, b + 1)
                    act.activation(rs2[:, :], rs2[:, :], ACT.Sqrt).then_inc(std2_done, 1)
            act.wait_ge(used[NS - 1], USES * NB + 1)
            act.activation(dots[:, 0:NS], dots[:, 0:NS], ACT.Gelu).then_inc(d_gelu, 1)
            act.wait_ge(d_var, 1)
            act.activation(rs2[0:NS, :], rs2[0:NS, :], ACT.Sqrt).then_inc(d_std, 1)

        @block.vector
        def _(dve):
            V = nc.vector
            N_TAIL = 7
            count = [0]

            def chain(base):
                count[0] = 0

                def lnk(ins):
                    count[0] += 1
                    ins.then_inc(link, 1)
                    dve.wait_ge(link, base + count[0])
                return lnk

            def mark(ins, s, v):
                ins.then_inc(s, 1)
                dve.wait_ge(s, v)

            def moments(lnk, x, st, ag, rows=P):
                for c in range(2):
                    lnk(V.bn_stats(st[0:rows, c, :], x[0:rows, c * 512:(c + 1) * 512]))
                stand_alone(dve, A)
                lnk(V.bn_aggr(ag[0:rows, :], st[0:rows, :, :].rearrange("p a b -> p (a b)")))

            def front_a(f, j, lnk):
                dve.wait_ge(mixed, f + 1)
                dve.wait_ge(ld_x, 16 * f + 16)
                mark(V.scalar_tensor_tensor(h[j][:, :], xb[:, :], ALPHA, fps[:, :], ALU.mult, ALU.add), h0_done, f + 1)
                moments(lnk, h[j], st, ag)
                mark(V.tensor_scalar(rs[:, :], ag[:, 1:2], LN_EPS, None, ALU.add), var_done, f + 1)

            def front_b(f, j, lnk):
                dve.wait_ge(std_done, f + 1)
                lnk(V.reciprocal(rs[:, :], rs[:, :]))
                lnk(V.tensor_scalar(h[j][:, :], h[j][:, :], ag[:, 0:1], rs[:, 0:1], ALU.subtract, ALU.mult))
                lnk(V.tensor_tensor(h[j][:, :], h[j][:, :], ln[:, 0, :], ALU.mult))
                mark(V.tensor_tensor(h[j][:, :], h[j][:, :], ln[:, 1, :], ALU.add), h_done, f + 1)

            def best16(lnk, src, copy, val, idx, last=None):
                stand_alone(dve, A)
                lnk(V.max(val[:, 0:8], src))
                stand_alone(dve, A)
                V.max_index(idx[:, 0:8], val[:, 0:8], src).then_inc(link, 1)
                count[0] += 1
                lnk(V.match_replace(copy, val[:, 0:8], src, LOW))
                stand_alone(dve, A)
                lnk(V.max(val[:, 8:16], copy))
                stand_alone(dve, A)
                (last or lnk)(V.max_index(idx[:, 8:16], val[:, 8:16], copy))

            def rows(f, n, lnk):
                c, x = n // PH, n % PH
                dve.wait_ge(sc_done, 2 * f + 2)
                last = (lambda ins: mark(ins, topk_done, f + 1)) if n == 2 * PH - 1 else None
                best16(lnk, scs[:, c, x, :], s2[:, :], sv[:, c, x, :], si[:, c, x, :], last)

            def sums(lnk, out, v):
                o = 0
                for a, n in CAND[:TOPK // 2]:
                    lnk(V.tensor_tensor(out[:, :, o:o + n], v[:, 1, :, 0:n], v[:, 0, :, a:a + 1].broadcast_to([P, PH, n]), ALU.add))
                    o += n
                lnk(V.tensor_tensor(out[:, :, o:], v[:, 0, :, TOPK // 2:], v[:, 1, :, 0:1].broadcast_to([P, PH, TOPK // 2]), ALU.add))

            def candidates(lnk):
                lnk(V.tensor_copy(sif[:, :, :, :], si[:, :, :, :]))
                lnk(V.tensor_scalar(sif[:, 0, :, :], sif[:, 0, :, :], float(NKEY), None, ALU.mult))
                sums(lnk, cand, sv)

            def best(x, lnk):
                best16(lnk, cand[:, x, :], c2[:, :], fv[:, x, :], fi[:, x, :])

            def expert_of(x, lnk):
                if x == 0:
                    lnk(V.tensor_copy(fif[:, :, :], fi[:, :, :]))
                lnk(V.tensor_tensor(eq[:, :, :], iota[:, :].unsqueeze(1).broadcast_to([P, TOPK, NCAND]),
                                    fif[:, x, :].unsqueeze(2).broadcast_to([P, TOPK, NCAND]), ALU.is_equal))
                lnk(V.tensor_tensor(eq[:, :, :], eq[:, :, :], cidx[:, x, :].unsqueeze(1).broadcast_to([P, TOPK, NCAND]), ALU.mult))
                lnk(V.tensor_reduce(ef[:, x, :], eq[:, :, :], AX_X, ALU.add))

            def finish(f, j):
                mark(V.tensor_copy(eidx[j][:, :], ef[:, :, :].rearrange("p a b -> p (a b)")), idx_done, f + 1)
                mark(V.tensor_tensor(gate[j][:, :, :], fv[:, :, :], fv[:, :, 0:1].broadcast_to([P, PH, TOPK]), ALU.subtract), fv_done, f + 1)

            def gates(f, j, lnk):
                dve.wait_ge(fe_done, f + 1)
                lnk(V.tensor_reduce(gs[:, :], gate[j][:, :, :], AX_X, ALU.add))
                lnk(V.reciprocal(gs[:, :], gs[:, :]))
                lnk(V.tensor_tensor(gate[j][:, :, :], gate[j][:, :, :], gs[:, :].unsqueeze(2).broadcast_to([P, PH, TOPK]), ALU.mult))

            def second_norm(lnk, rows, var_s, std_s, done_s, v):
                moments(lnk, yacc, st2, ag2, rows)
                mark(V.tensor_scalar(rs2[0:rows, :], ag2[0:rows, 1:2], LN_EPS, None, ALU.add), var_s, v)
                dve.wait_ge(std_s, v)
                lnk(V.reciprocal(rs2[0:rows, :], rs2[0:rows, :]))
                lnk(V.tensor_scalar(yacc[0:rows, :], yacc[0:rows, :], ag2[0:rows, 0:1], rs2[0:rows, 0:1], ALU.subtract, ALU.mult))
                lnk(V.tensor_tensor(yacc[0:rows, :], yacc[0:rows, :], ln[0:rows, 2, :], ALU.mult))
                mark(V.tensor_tensor(yacc[0:rows, :], yacc[0:rows, :], ln[0:rows, 3, :], ALU.add), done_s, v)

            dve.wait_ge(const_in, 16 * (2 * KT + 3))
            lnk = chain(0)
            front_a(0, 0, lnk)
            front_b(0, 0, lnk)
            for n in range(2 * PH):
                rows(0, n, lnk)
            candidates(lnk)
            sums(lnk, cidx, sif)
            for x in range(PH):
                best(x, lnk)
            for x in range(PH):
                expert_of(x, lnk)
            finish(0, 0)
            gates(0, 0, lnk)
            n_front = count[0]
            n_turn = n_front + N_TAIL
            with dve.Fori(0, NB // 2) as i:
                for j in range(2):
                    b = 2 * i + j
                    f = b + 1
                    lnk = chain(n_front + n_turn * b)
                    for s in range(SLOTS):
                        r = s % RING
                        dve.wait_ge(got[r], 16 * (USES * b + s // RING + 1))
                        V.tensor_tensor_reduce(ring[:, r, :], ring[:, r, :], h[j][:, :], 1.0, 0.0, ALU.mult, ALU.add,
                                               dots[:, s:s + 1]).then_inc(used[r], 1)
                        if s == 24:
                            front_a(f, 1 - j, lnk)
                        if s == 32:
                            front_b(f, 1 - j, lnk)
                    dve.wait_ge(gelu_done, b + 1)
                    mark(V.tensor_tensor(wts[:, :], dots[:, :], gate[j][:, :, :].rearrange("p a b -> p (a b)"), ALU.mult), w_done, b + 1)
                    dve.wait_ge(y_out, 16 * b)
                    lnk(V.tensor_scalar(yacc[:, :], h[j][:, :], ALPHA, None, ALU.mult))
                    for m in range(NV):
                        s = ON_DVE * m + ON_DVE - 1
                        n = SLOTS + s
                        dve.wait_ge(got[n % RING], 16 * (USES * b + n // RING + 1))
                        mark(V.scalar_tensor_tensor(yacc[:, :], ring[:, n % RING, :], wts[:, s:s + 1], yacc[:, :], ALU.mult, ALU.add),
                             used[n % RING], USES * b + n // RING + 1)
                        if m < 8:
                            rows(f, 2 * m, lnk)
                            rows(f, 2 * m + 1, lnk)
                        elif m == 8:
                            candidates(lnk)
                        elif m == 9:
                            sums(lnk, cidx, sif)
                        elif m < 14:
                            for x in range(2):
                                best(2 * (m - 10) + x, lnk)
                        elif m < 18:
                            for x in range(2):
                                expert_of(2 * (m - 14) + x, lnk)
                        elif m == 18:
                            finish(f, 1 - j)
                    dve.wait_ge(used[(SLOTS + on_pe[-1]) % RING], USES * b + USES)
                    mark(V.tensor_tensor(yacc[:, :], yacc[:, :], yps[:, :], ALU.add), y_read, b + 1)
                    second_norm(lnk, P, var2_done, std2_done, y_done, b + 1)
                    gates(f, 1 - j, lnk)
                    assert count[0] == n_turn

            lnk = chain(n_front + n_turn * NB)
            lnk(V.memset(wexp[:, :, :], 0.0))
            mark(V.tensor_copy(scs[0:NS, 0, :, :], ident[0:NS, 0:NS].unsqueeze(2).broadcast_to([NS, NS, NKEY])), d_select, 1)
            mark(V.memset(flag[:, :], 0.0), d_ready, 1)
            dve.wait_ge(d_by_slot, 1)
            mark(V.tensor_copy(fi[:, 0, 0:NS], fps[:, 0:NS]), d_idx, 1)
            lnk(V.tensor_copy(fif[:, 0, 0:NS], fps[:, 512:512 + NS]))
            for t in range(NS):
                dve.wait_ge(got[t], 16 * (USES * NB + 1))
                dve.wait_ge(d_spread, t + 1)
                V.tensor_tensor_reduce(ring[:, t, :], ring[:, t, :], sps[:, (t % 2) * DM:(t % 2 + 1) * DM], 1.0, 0.0, ALU.mult, ALU.add,
                                       dots[:, t:t + 1]).then_inc(used[t], 1)
            dve.wait_ge(d_gelu, 1)
            mark(V.tensor_tensor(wexp[:, :, :].rearrange("p a b -> p (a b)")[:, 0:NS * NS:NS + 1], dots[:, 0:NS], fif[:, 0, 0:NS], ALU.mult), d_w, 1)
            dve.wait_ge(y_out, 16 * NB)
            dve.wait_ge(d_sum, 1)
            lnk(V.scalar_tensor_tensor(yacc[0:NS, :], h[0][0:NS, :], ALPHA, yps[0:NS, :], ALU.mult, ALU.add))
            second_norm(lnk, NS, d_var, d_std, d_done, 1)


def program(nc, A, phases=99):
    with ExitStack() as ctx:
        A["passed"] = ctx.enter_context(nc.semaphore("c_passed"))
        A["sb_ident"] = ctx.enter_context(nc.sbuf_tensor("c_ident", [P, P], F32))
        A["sb_bd"] = ctx.enter_context(nc.sbuf_tensor("c_bd", [P, P], F32))
        A["sb_eye2"] = ctx.enter_context(nc.sbuf_tensor("c_eye2", [P, HD], F32))
        with ExitStack() as c1:
            A["sb_xT"] = c1.enter_context(nc.sbuf_tensor("c_xT", [P, KT, NT], F32))
            project_plain(nc, A, None)
            if phases > 1:
                project_pairs(nc, A, None)
        if phases > 2:
            scan_pairs(nc, A)
        if phases > 3:
            attend(nc, A)
        if phases > 4:
            decode(nc, A)
        if phases > 5:
            merge(nc, A)
        if phases > 6:
            peer(nc, A)


def scratch(nc, A):
    for name, shape in (("zT", (N_TILES, P, NT)), ("zn", (NS + 1, N_TILES, P)), ("rw", (NPAIR, N_RW, P, NP)),
                        ("gate", (NPAIR, P, NT)), ("bonus", (NPAIR, P, NT)), ("dend", (NPAIR, P, NC)),
                        ("decn", (NS, NPAIR, 2, 6, HD)), ("yd", (NS, DM)), ("bT", (NPAIR, P, NT)),
                        ("aT", (KT, P, NT)), ("tab", (NH, P, 3 * WIN)), ("mT", (KT, P, NPAD))):
        A[name] = nc.dram_tensor("s_" + name, shape, F32).ap()


def bucket(rel):
    half = 16
    n = np.maximum(rel, 0)
    nf = np.maximum(n, half).astype(np.float32)
    large = half + (np.log(nf / np.float32(half)) / np.float32(math.log(128 / half)) * np.float32(half)).astype(np.int32)
    return np.where(n < half, n, np.minimum(large, 2 * half - 1))


def layouts(x):
    f = lambda n: np.asarray(x[n], np.float32)
    xall = np.concatenate([f("x_prompt")[0], f("x_sample")[:, 0]], 0)
    w = f("w_in")[0]
    q0, k0, v0 = 0, NH * HD, NH * HD + NKV * HD
    r0 = v0 + NKV * HD
    l0 = r0 + 3 * DM
    g0 = l0 + 2 * HD + P
    heads = [(2 * (t // 4) + h) * 4 + t % 4 for t in range(KT) for h in range(2)]
    cols = [h * HD + i for h in heads for i in range(HD)]
    cols += list(range(k0, r0)) + list(range(l0, g0)) + list(range(g0, g0 + 2 * DM))
    pair = []
    for p in range(NPAIR):
        for base in (DM, 0, 2 * DM):
            pair += list(range(base + p * P, base + (p + 1) * P))
    cols = np.array(cols + [r0 + c for c in pair])
    feats = np.array([3 * DM + i for i in range(2 * P)] + pair)
    tiles = lambda m: np.ascontiguousarray(m.reshape(KT, P, -1, P).transpose(2, 1, 0, 3))
    mu = f("rwkv_mu")[0]
    per = lambda v: v.reshape(NPAIR, P).T
    prm = np.stack([per(mu[DM:2 * DM]), per(mu[0:DM]), per(mu[2 * DM:3 * DM])] +
                   [per(f(n)[0]) for n in ("rwkv_w0", "rwkv_a0", "rwkv_k_k", "rwkv_k_a", "rwkv_r_k",
                                           "rwkv_lnx_g", "rwkv_lnx_b")], 2)
    upwa = np.concatenate([f("rwkv_w_up")[0], f("rwkv_a_up")[0]], 0).reshape(P, NPAIR, P)
    upg = f("rwkv_g_up")[0].reshape(P, NPAIR, P)
    d = {
        "xT": xall.T.reshape(KT, P, NT).transpose(1, 0, 2),
        "x_all": xall,
        "w_tiles": tiles(w[:, cols]),
        "shT": f("state_shift")[0].T[feats].reshape(-1, P, NS).transpose(1, 0, 2),
        "prm": prm,
        "mu_lora": mu[3 * DM:].reshape(2, P).T,
        "up": np.stack([upwa, upg], 2).transpose(1, 0, 2, 3),
        "ident": np.eye(P, dtype=np.float32),
        "bd": np.kron(np.eye(2), np.ones((HD, HD))).astype(np.float32),
    }
    d["eye2"] = np.tile(np.eye(HD, dtype=np.float32), (2, 1))
    i, j = np.arange(CL)[:, None], np.arange(CL)[None, :]
    ms = [-1.0 * (j < i), -1.0 * (j > i), 1.0 * (j > i), -1.0 * (j >= i), 1.0 * (j >= i)]
    d["masks"] = np.tile(np.stack(ms, 1), (2, 1, 1)).astype(np.float32)
    order = [heads[2 * (2 * u + t) + h] for u in range(KT // 2) for h in range(2) for t in range(2)]
    d["rel_bias"] = f("rel_bias")[:, order]
    d["sinks"] = np.tile(f("attn_sinks")[0][order], (P, 1))
    d["pen"] = np.tile(np.where(np.arange(NB) == 0, MASKED, 0.0).astype(np.float32), (P, 1))
    by_tile = [heads[2 * t + h] for t in range(KT) for h in range(2)]
    d["rel_bias_d"] = np.concatenate([np.tile(f("rel_bias")[:, by_tile], (1, NS)), np.ones((1, NS * NH), np.float32)], 0)
    d["sinks_d"] = np.tile(f("attn_sinks")[0][by_tile], NS)[:, None]
    ck, cv = f("cache_win_k")[0], f("cache_win_v")[0]
    d["cache_k"], d["cache_v"] = ck.reshape(NS, WIN, -1), cv.reshape(NS, WIN, -1)
    d["kc"] = ck.reshape(NS, WIN, 2, P).transpose(3, 0, 2, 1)
    d["vc"] = cv.reshape(NS, WIN, -1).transpose(1, 0, 2)
    d["state"] = f("state_wkv")[0].reshape(NS * NH, HD * HD)
    d["wba_tiles"] = tiles(f("w_branch_attn")[0][[h * HD + i for h in by_tile for i in range(HD)]])
    d["wbr_tiles"] = tiles(f("w_branch_rwkv")[0])
    d["w_out"] = f("w_out")[0].reshape(KT, P, DM)
    d["peer_q"] = f("peer_q")[0].reshape(KT, P, DM)
    d["keysT"] = f("peer_keys")[0].transpose(1, 3, 0, 2).reshape(P, PH, NKEY)
    d["ln"] = np.tile(np.stack([f(n)[0] for n in ("ln1_g", "ln1_b", "ln2_g", "ln2_b")]), (P, 1, 1))
    d["iota"] = np.tile(np.arange(NCAND, dtype=np.float32), (P, 1))
    d["x_pad"] = np.concatenate([xall, np.zeros((NPAD - NT, DM), np.float32)], 0).reshape(NB + 1, P, DM)
    d["peer_u"], d["peer_v"] = f("peer_u")[0], f("peer_v")[0]
    del d["x_all"]
    rel = 2 * WIN - 1 - np.arange(3 * WIN)
    ok = (rel >= 0) & (rel <= WIN)
    oneh = np.zeros((REL_ROWS, 3 * WIN), np.float32)
    oneh[bucket(rel)[ok], np.arange(3 * WIN)[ok]] = HD ** 0.5
    oneh[REL_ROWS - 1, ~ok] = MASKED
    d["onehot"] = oneh
    return {k: np.ascontiguousarray(v) for k, v in d.items()}


_OUTS = [("y", (NT, DM)), ("win_k_p", (WIN, NKV * HD)), ("win_v_p", (WIN, NKV * HD)), ("wkv_p", (NPAIR, P, HD)),
         ("shift", (NS + 1, 3 * DM + 2 * P)), ("win_k_s", (NS, WIN, NKV * HD)), ("win_v_s", (NS, WIN, NKV * HD)),
         ("wkv_s", (NS * NH, HD * HD))]


def kernel(**inputs):
    import concourse.bacc as _bacc
    from concourse.bass_utils import run_bass_kernel_spmd as _run

    nc = _bacc.Bacc("TRN2", target_bir_lowering=False, num_devices=1)
    arrays = layouts(inputs)
    A = {n: nc.dram_tensor(n, a.shape, mybir.dt.from_np(a.dtype), kind="ExternalInput").ap() for n, a in arrays.items()}
    for n, shape in _OUTS:
        A[n] = nc.dram_tensor(n, shape, F32, kind="ExternalOutput").ap()
    scratch(nc, A)
    program(nc, A)
    g = _run(nc, [arrays], core_ids=[0]).results[0]
    win = (1, -1, WIN, NKV, HD)
    return (g["y"][:NP].reshape(1, NP, DM), g["y"][NP:].reshape(NS, 1, DM),
            g["win_k_p"].reshape(win), g["win_v_p"].reshape(win), g["wkv_p"].reshape(1, 1, NH, HD, HD), g["shift"][0:1].reshape(1, 1, -1),
            g["win_k_s"].reshape(win), g["win_v_s"].reshape(win), g["wkv_s"].reshape(1, NS, NH, HD, HD), g["shift"][1:].reshape(1, NS, -1))
```

```python
import math
from contextlib import ExitStack, contextmanager

import numpy as np
import concourse.bass as bass
from concourse import mybir

F32 = mybir.dt.float32
U32 = mybir.dt.uint32
ALU = mybir.AluOpType
ACT = mybir.ActivationFunctionType
AX_X = mybir.AxisListType.X

P = 128
DM = 1024
KT = DM // P
NP = 1024
NS = 8
NT = NP + NS
TG = NT // 3
NH = 16
NKV = 4
NPAD = NP + P
HD = 64
WIN = 128
NB = NP // WIN
NPAIR = NH // 2
CL = 64
NC = NP // CL
LN_EPS = 1e-5
GN_EPS = 64e-5
ALPHA = 2.0 ** 0.25
REL_ROWS = 33
MASKED = -1e30
DECAY_C = float(np.exp(-0.5))

T_Q, T_K, T_V, T_XWA, T_XG, T_GA, T_GB, T_PAIR = 0, 8, 10, 12, 13, 14, 22, 30
N_PLAIN = T_PAIR
N_TILES = T_PAIR + 3 * NPAIR
Q_PAIR_K, Q_PAIR_R, Q_PAIR_V = 0, 1, 2

(C_MUK, C_MUR, C_MUV, C_W0, C_A0, C_KK, C_KA, C_RK, C_LG, C_LB) = range(10)
NPRM = 10

(R_ALPHA, R_BETA, R_KAPPA, R_RHO, R_BETAE, R_KAPPAE, R_V) = range(7)
N_RW = 7


class Steps:

    def __init__(self, *names):
        self.at = {n: i + 1 for i, n in enumerate(names)}
        self.n = len(names)
        assert len(self.at) == self.n

    def after(self, name, turn=0):
        return turn * self.n + self.at[name]


@contextmanager
def signals(nc):
    made = []

    def sem(name):
        made.append(nc.alloc_semaphore(name))
        return made[-1]

    yield sem
    nc.clear_and_free_semaphores(made)
    nc.all_engine_barrier()


def stand_alone(engine, A):
    engine.sem_inc(A["passed"], 1)


def grouped(ap):
    return ap.rearrange("p (a b) -> p a b", a=3)


def project_plain(nc, A):
    UN = 6
    with ExitStack() as ctx:
        xT, ident = A["sb_xT"], A["sb_ident"]
        w = [ctx.enter_context(nc.sbuf_tensor(f"pw{j}", [P, KT, P], F32)) for j in range(2)]
        z = [ctx.enter_context(nc.sbuf_tensor(f"pz{j}", [P, NT], F32)) for j in range(2)]
        zn = [ctx.enter_context(nc.sbuf_tensor(f"pzn{j}", [NS + 1, P], F32)) for j in range(2)]
        zp = [ctx.enter_context(nc.psum_tensor(f"pzp{j}", [P, 3, 512], F32)) for j in range(2)]
        tp = [ctx.enter_context(nc.psum_tensor(f"ptp{j}", [P, 512], F32)) for j in range(2)]
        sem = ctx.enter_context(signals(nc))
        const_in = sem("p_const_in")
        two = lambda n: [sem(f"p_{n}{j}") for j in range(2)]
        w_in, z_out, zn_out = two("w_in"), two("z_out"), two("zn_out")
        z_psum, z_sbuf, t_psum, t_sbuf = two("z_psum"), two("z_sbuf"), two("t_psum"), two("t_sbuf")
        block = ctx.enter_context(nc.Block())
        TURNS = N_PLAIN // UN
        use = lambda i, u: (UN // 2) * i + u // 2

        @block.sync
        def _(sp):
            sp.dma_start(ident[:, :], A["ident"]).then_inc(const_in, 16)
            sp.dma_start(A["sb_bd"][:, :], A["bd"]).then_inc(const_in, 16)
            sp.dma_start(A["sb_eye2"][:, :], A["eye2"]).then_inc(const_in, 16)
            for k in range(KT):
                sp.dma_start(xT[:, k, :], A["xT"][:, k, :]).then_inc(const_in, 16)
            with sp.Fori(0, TURNS) as i:
                for u in range(UN):
                    sp.wait_ge(z_psum[u % 2], use(i, u))
                    sp.dma_start(w[u % 2][:, :, :], A["w_tiles"][UN * i + u]).then_inc(w_in[u % 2], 16)

        @block.tensor
        def _(pe):
            pe.wait_ge(const_in, 16 * (KT + 3))
            with pe.Fori(0, TURNS) as i:
                def natural(u):
                    j = u % 2
                    pe.wait_ge(z_sbuf[j], use(i, u) + 1)
                    pe.wait_ge(t_sbuf[j], use(i, u))
                    pe.transpose(tp[j][0:NS + 1, 0:P], z[j][:, NP - 1:NT], ident[:, :]).then_inc(t_psum[j], 1)

                for u in range(UN):
                    j = u % 2
                    pe.wait_ge(w_in[j], 16 * use(i, u) + 16)
                    pe.wait_ge(z_sbuf[j], use(i, u))
                    for g in range(3):
                        for k in range(KT):
                            mm = pe.matmul(zp[j][:, g, 0:TG], w[j][:, k, :], xT[:, k, g * TG:(g + 1) * TG],
                                           start=(k == 0), stop=(k == KT - 1))
                    mm.then_inc(z_psum[j], 1)
                    if u:
                        natural(u - 1)
                natural(UN - 1)

        @block.scalar
        def _(act):
            with act.Fori(0, TURNS) as i:
                def natural(u):
                    j = u % 2
                    act.wait_ge(t_psum[j], use(i, u) + 1)
                    act.wait_ge(zn_out[j], 16 * use(i, u))
                    act.activation(zn[j][:, :], tp[j][0:NS + 1, 0:P], ACT.Copy).then_inc(t_sbuf[j], 1)
                    act.wait_ge(t_sbuf[j], use(i, u) + 1)
                    act.dma_start(A["zn"][:, UN * i + u, :], zn[j][:, :]).then_inc(zn_out[j], 16)

                for u in range(UN):
                    j = u % 2
                    act.wait_ge(z_psum[j], use(i, u) + 1)
                    act.wait_ge(z_out[j], 16 * use(i, u))
                    act.wait_ge(t_psum[j], use(i, u))
                    act.activation(grouped(z[j][:, :]), zp[j][:, :, 0:TG], ACT.Copy).then_inc(z_sbuf[j], 1)
                    act.wait_ge(z_sbuf[j], use(i, u) + 1)
                    act.dma_start(A["zT"][UN * i + u], z[j][:, :]).then_inc(z_out[j], 16)
                    if u:
                        natural(u - 1)
                natural(UN - 1)
            for j in range(2):
                act.wait_ge(z_out[j], 16 * (N_PLAIN // 2))
                act.wait_ge(zn_out[j], 16 * (N_PLAIN // 2))


def project_pairs(nc, A):
    PE = Steps("w", "a", "g", "r", "ss", "v", "bonus", "raw_t", "dec_t")
    AC = Steps("w", "a", "g", "r", "D", "Dprev", "Dinv", "wdec", "norm", "v", "raw_t", "dec_t0", "dec_t1")
    DV = Steps("prm", "k_d", "k_ds", "k_f", "kkr", "sq", "lw", "scan", "lprev", "a", "ka1", "kp",
               "r_d", "r_ds", "r_f", "rkr", "rk", "ssm", "rinv", "kk", "kka", "v_d", "v_ds", "v_f",
               "alpha", "beta", "kappa", "rho", "dend", "betae", "kappae")
    N_PRE = 14
    with ExitStack() as ctx:
        xT, ident, bd = A["sb_xT"], A["sb_ident"], A["sb_bd"]
        sb = lambda n, s: ctx.enter_context(nc.sbuf_tensor(n, s, F32))
        sem = ctx.enter_context(signals(nc))
        w = [sb(f"qw{j}", [P, KT, P]) for j in range(3)]
        up = sb("q_up", [P, 2, P])
        z = [sb(f"qz{q}", [P, 1 + NT]) for q in range(3)]
        lora = [sb(f"q_lora{j}", [P, NT]) for j in range(2)]
        prm = sb("q_prm", [P, NPAIR, NPRM])
        sh = sb("q_sh", [P, 2 + 3 * NPAIR, NS])
        mul_ = sb("q_mulora", [P, 2])
        pc = sb("q_pc", [P, NPRM])
        hc = sb("q_hc", [P, NPAIR, 2])
        tmp = sb("q_tmp", [P, NT])
        fk, fr, fv = sb("q_fk", [P, NT]), sb("q_fr", [P, NT]), sb("q_fv", [P, NT])
        kkr, sq, tw, ta = sb("q_kkr", [P, NT]), sb("q_sq", [P, NT]), sb("q_tw", [P, NT]), sb("q_ta", [P, NT])
        kk, kka, kp, rk = sb("q_kk", [P, NT]), sb("q_kka", [P, NT]), sb("q_kp", [P, NT]), sb("q_rk", [P, NT])
        lcum, lprev = sb("q_lcum", [P, NP]), sb("q_lprev", [P, NP])
        D, Dp, Di = sb("q_D", [P, NP]), sb("q_Dp", [P, NP]), sb("q_Di", [P, NP])
        wdec = sb("q_wdec", [P, NS])
        dend = sb("q_dend", [P, NC])
        reset = sb("q_reset", [P, NP])
        gate, bonus = sb("q_gate", [P, NT]), sb("q_bonus", [P, NT])
        out = [sb(f"q_out{n}", [P, NP]) for n in range(6)]
        rawn = sb("q_rawn", [NS + 1, 3 * P])
        decn = sb("q_decn", [NS, 6 * P])
        zp = [ctx.enter_context(nc.psum_tensor(f"qzp{j}", [P, 3, 512], F32)) for j in range(2)]
        tp = [ctx.enter_context(nc.psum_tensor(f"qtp{j}", [P, 512], F32)) for j in range(2)]
        const_in, lora_in = sem("q_const_in"), sem("q_lora_in")
        w_in = [sem(f"q_w_in{j}") for j in range(3)]
        up_in = sem("q_up_in")
        pe_done, act_done, dve_done = sem("q_pe_done"), sem("q_act_done"), sem("q_dve_done")
        k_psum, k_sbuf, bonus_done = sem("q_k_psum"), sem("q_k_sbuf"), sem("q_bonus_done")
        pre_dve, pre_act = sem("q_pre_dve"), sem("q_pre_act")
        rw_out = [sem(f"q_rw_out{n}") for n in range(N_RW)]
        g_out, b_out, d_out = sem("q_g_out"), sem("q_b_out"), sem("q_d_out")
        raw_out, dec_out = sem("q_raw_out"), sem("q_dec_out")
        block = ctx.enter_context(nc.Block())
        PROMPT, DEC = slice(0, NP), slice(NP, NT)
        chunks = lambda ap: ap.rearrange("p (c l) -> p c l", l=CL)
        each = lambda ap: ap.unsqueeze(2).broadcast_to([P, NC, CL])

        @block.sync
        def _(sp):
            for d, s in ((z[0][:, 1:], A["zT"][T_XWA]), (z[1][:, 1:], A["zT"][T_XG])):
                sp.dma_start(d, s).then_inc(lora_in, 16)
            for d, s in ((prm[:, :, :], A["prm"]), (sh[:, :, :], A["shT"]), (mul_[:, :], A["mu_lora"])):
                sp.dma_start(d, s).then_inc(const_in, 16)
            def load(q, p):
                sp.dma_start(w[q][:, :, :], A["w_tiles"][T_PAIR + 3 * p + q]).then_inc(w_in[q], 16)

            def load_up(p):
                sp.dma_start(up[:, :, :], A["up"][p]).then_inc(up_in, 16)

            load(0, 0)
            load_up(0)
            load(1, 0)
            load(2, 0)
            with sp.Fori(0, NPAIR - 1) as p:
                sp.wait_ge(k_psum, p + 1)
                stand_alone(sp, A)
                load(0, p + 1)
                sp.wait_ge(pe_done, PE.after("g", p))
                stand_alone(sp, A)
                load_up(p + 1)
                for q, n in ((1, "r"), (2, "v")):
                    sp.wait_ge(pe_done, PE.after(n, p))
                    stand_alone(sp, A)
                    load(q, p + 1)

        @block.tensor
        def _(pe):
            def project(q, s, done):
                for g in range(3):
                    for k in range(KT):
                        mm = pe.matmul(zp[s][:, g, 0:TG], w[q][:, k, :], xT[:, k, g * TG:(g + 1) * TG],
                                       start=(k == 0), stop=(k == KT - 1))
                mm.then_inc(done, 1)

            def small(s, lhsT, rhs):
                for g in range(3):
                    mm = pe.matmul(zp[s][:, g, 0:TG], lhsT, rhs[:, g * TG:(g + 1) * TG], start=True, stop=True)
                mm.then_inc(pe_done, 1)

            pe.wait_ge(pre_act, 2)
            pe.wait_ge(pre_dve, N_PRE)
            def pair(p, more):
                pe.wait_ge(up_in, 16 * p + 16)
                pe.wait_ge(bonus_done, p)
                small(1, up[0:HD, 0, :], lora[0][0:HD, :])
                pe.wait_ge(k_sbuf, p + 1)
                small(0, up[HD:P, 0, :], lora[0][HD:P, :])
                pe.wait_ge(act_done, AC.after("w", p))
                small(1, up[:, 1, :], lora[1][:, :])
                pe.wait_ge(w_in[1], 16 * p + 16)
                pe.wait_ge(act_done, AC.after("a", p))
                project(Q_PAIR_R, 0, pe_done)
                pe.wait_ge(act_done, AC.after("g", p))
                pe.wait_ge(dve_done, DV.after("sq", p))
                small(1, bd[:, :], sq[:, :])
                pe.wait_ge(w_in[2], 16 * p + 16)
                pe.wait_ge(act_done, AC.after("r", p))
                project(Q_PAIR_V, 0, pe_done)
                pe.wait_ge(dve_done, DV.after("ssm", p))
                small(1, bd[:, :], rk[:, :])
                pe.wait_ge(act_done, AC.after("v", p))
                for q in range(3):
                    t = pe.transpose(tp[0][0:NS + 1, q * P:(q + 1) * P], z[q][:, NP:1 + NT], ident[:, :])
                t.then_inc(pe_done, 1)
                if more:
                    pe.wait_ge(w_in[0], 16 * p + 32)
                    project(Q_PAIR_K, 0, k_psum)
                pe.wait_ge(act_done, AC.after("raw_t", p))
                pe.wait_ge(dve_done, DV.after("v_f", p))
                for n, src in enumerate((fr[:, DEC], wdec[:, :], kp[:, DEC], fv[:, DEC], kk[:, DEC], kka[:, DEC])):
                    t = pe.transpose(tp[n // 4][0:NS, (n % 4) * P:(n % 4 + 1) * P], src, ident[:, :])
                t.then_inc(pe_done, 1)

            pe.wait_ge(w_in[0], 16)
            project(Q_PAIR_K, 0, k_psum)
            with pe.Fori(0, NPAIR - 1) as p:
                pair(p, True)
            pair(NPAIR - 1, False)

        @block.scalar
        def _(act):
            act.wait_ge(pre_dve, N_PRE - 3)
            act.activation(lora[0][0:HD, :], z[0][0:HD, 1:], ACT.Tanh).then_inc(pre_act, 1)
            act.activation(lora[1][:, :], z[1][:, 1:], ACT.Tanh, scale=0.5).then_inc(pre_act, 1)
            act.wait_ge(pre_dve, N_PRE)
            def k_evac(p):
                act.wait_ge(k_psum, p + 1)
                act.activation(grouped(z[0][:, 1:]), zp[0][:, :, 0:TG], ACT.Copy).then_inc(k_sbuf, 1)

            def pair(p, more):
                half = lambda n: hc[:, bass.ds(p, 1), n:n + 1].rearrange("p a b -> p (a b)")
                act.wait_ge(pe_done, PE.after("w", p))
                act.activation(grouped(tw[:, :]), zp[1][:, :, 0:TG], ACT.Tanh, bias=half(0), scale=0.5).then_inc(act_done, 1)
                act.wait_ge(pe_done, PE.after("a", p))
                act.activation(grouped(ta[:, :]), zp[0][:, :, 0:TG], ACT.Tanh, bias=half(1), scale=0.5).then_inc(act_done, 1)
                act.wait_ge(pe_done, PE.after("g", p))
                act.wait_ge(g_out, 16 * p)
                act.activation(grouped(gate[:, :]), zp[1][:, :, 0:TG], ACT.Copy).then_inc(act_done, 1)
                act.wait_ge(pe_done, PE.after("r", p))
                act.activation(grouped(z[1][:, 1:]), zp[0][:, :, 0:TG], ACT.Copy).then_inc(act_done, 1)
                act.wait_ge(dve_done, DV.after("lprev", p))
                act.activation(D[:, :], lcum[:, :], ACT.Exp).then_inc(act_done, 1)
                act.activation(Dp[:, :], lprev[:, :], ACT.Exp).then_inc(act_done, 1)
                act.activation(Di[:, :], lcum[:, :], ACT.Exp, scale=-1.0).then_inc(act_done, 1)
                act.activation(wdec[:, :], tw[:, DEC], ACT.Exp).then_inc(act_done, 1)
                act.wait_ge(dve_done, DV.after("ssm", p))
                act.activation(sq[:, :], sq[:, :], ACT.Sqrt).then_inc(act_done, 1)
                act.wait_ge(pe_done, PE.after("v", p))
                act.activation(grouped(z[2][:, 1:]), zp[0][:, :, 0:TG], ACT.Copy).then_inc(act_done, 1)
                act.wait_ge(pe_done, PE.after("raw_t", p))
                act.wait_ge(raw_out, 16 * p)
                act.activation(rawn[:, :], tp[0][0:NS + 1, 0:3 * P], ACT.Copy).then_inc(act_done, 1)
                act.wait_ge(act_done, AC.after("raw_t", p))
                act.dma_start(A["zn"][:, bass.ds(T_PAIR + 3 * p, 3), :],
                              rawn[:, :].rearrange("b (q f) -> b q f", q=3)).then_inc(raw_out, 16)
                if more:
                    k_evac(p + 1)
                act.wait_ge(pe_done, PE.after("dec_t", p))
                act.wait_ge(dec_out, 32 * p)
                act.activation(decn[:, 0:4 * P], tp[0][0:NS, :], ACT.Copy).then_inc(act_done, 1)
                act.activation(decn[:, 4 * P:], tp[1][0:NS, 0:2 * P], ACT.Copy).then_inc(act_done, 1)
                act.wait_ge(act_done, AC.after("dec_t1", p))
                for h in range(2):
                    act.dma_start(A["decn"][:, p, h],
                                  decn[:, :].rearrange("b (q h d) -> b q h d", h=2, d=HD)[:, :, h, :]).then_inc(dec_out, 16)

            k_evac(0)
            with act.Fori(0, NPAIR - 1) as p:
                pair(p, True)
            pair(NPAIR - 1, False)
            act.wait_ge(raw_out, 16 * NPAIR)
            act.wait_ge(dec_out, 32 * NPAIR)

        @block.vector
        def _(dve):
            steps = iter(range(1, N_PRE + 1))

            def pre(ins):
                ins.then_inc(pre_dve, 1)
                dve.wait_ge(pre_dve, next(steps))

            for q in range(3):
                pre(nc.vector.memset(z[q][:, 0:1], 0.0))
            pre(nc.vector.memset(reset[:, :], 1.0))
            pre(nc.vector.memset(reset[:, 0:NP:CL], 0.0))
            dve.wait_ge(lora_in, 32)
            dve.wait_ge(const_in, 48)
            for j, t in ((0, tmp), (1, fk)):
                pre(nc.vector.tensor_tensor(t[:, PROMPT], z[j][:, 0:NP], z[j][:, 1:1 + NP], ALU.subtract))
                pre(nc.vector.tensor_tensor(t[:, DEC], sh[:, j, :], z[j][:, 1 + NP:], ALU.subtract))
                pre(nc.vector.scalar_tensor_tensor(z[j][:, 1:], t[:, :], mul_[:, j:j + 1], z[j][:, 1:], ALU.mult, ALU.add))
            dve.wait_ge(pre_act, 2)
            pre(nc.vector.tensor_copy(lora[0][HD:P, :], z[0][HD:P, 1:]))
            pre(nc.vector.tensor_scalar(lora[1][:, :], lora[1][:, :], 0.5, 0.5, ALU.mult, ALU.add))

            pre(nc.vector.tensor_scalar(hc[:, :, :], prm[:, :, C_W0:C_A0 + 1], 0.5, None, ALU.mult))

            with dve.Fori(0, NPAIR) as p:
                def do(name, ins):
                    ins.then_inc(dve_done, 1)
                    dve.wait_ge(dve_done, DV.after(name, p))

                def mixed(q, f, n, mu):
                    do(n + "_d", nc.vector.tensor_tensor(tmp[:, PROMPT], z[q][:, 0:NP], z[q][:, 1:1 + NP], ALU.subtract))
                    do(n + "_ds", nc.vector.tensor_tensor(tmp[:, DEC], sh[:, bass.ds(2 + 3 * p + q, 1), :].rearrange("p a b -> p (a b)"),
                                                          z[q][:, 1 + NP:], ALU.subtract))
                    do(n + "_f", nc.vector.scalar_tensor_tensor(f[:, :], tmp[:, :], pc[:, mu:mu + 1], z[q][:, 1:], ALU.mult, ALU.add))

                do("prm", nc.vector.tensor_copy(pc[:, :], prm[:, bass.ds(p, 1), :].rearrange("p a b -> p (a b)")))
                dve.wait_ge(k_sbuf, p + 1)
                mixed(0, fk, "k", C_MUK)
                do("kkr", nc.vector.tensor_scalar(kkr[:, :], fk[:, :], pc[:, C_KK:C_KK + 1], None, ALU.mult))
                do("sq", nc.vector.tensor_tensor(sq[:, :], kkr[:, :], kkr[:, :], ALU.mult))
                dve.wait_ge(act_done, AC.after("w", p))
                do("lw", nc.vector.tensor_scalar(tw[:, :], tw[:, :], -0.5 * DECAY_C, -0.5 * DECAY_C, ALU.mult, ALU.add))
                do("scan", nc.vector.tensor_tensor_scan(lcum[:, :], reset[:, :], tw[:, PROMPT], 0.0, ALU.mult, ALU.add))
                do("lprev", nc.vector.tensor_tensor(lprev[:, :], lcum[:, :], tw[:, PROMPT], ALU.subtract))
                dve.wait_ge(act_done, AC.after("a", p))
                do("a", nc.vector.tensor_scalar(ta[:, :], ta[:, :], 0.5, 0.5, ALU.mult, ALU.add))
                do("ka1", nc.vector.tensor_scalar(kp[:, :], ta[:, :], -1.0, pc[:, C_KA:C_KA + 1], ALU.add, ALU.mult))
                do("kp", nc.vector.scalar_tensor_tensor(kp[:, :], kp[:, :], 1.0, fk[:, :], ALU.add, ALU.mult))
                dve.wait_ge(act_done, AC.after("r", p))
                mixed(1, fr, "r", C_MUR)
                do("rkr", nc.vector.tensor_scalar(rk[:, :], kp[:, :], pc[:, C_RK:C_RK + 1], None, ALU.mult))
                do("rk", nc.vector.tensor_tensor(rk[:, :], rk[:, :], fr[:, :], ALU.mult))
                dve.wait_ge(pe_done, PE.after("ss", p))
                do("ssm", nc.vector.tensor_scalar(grouped(sq[:, :]), zp[1][:, :, 0:TG], 1e-24, None, ALU.max))
                dve.wait_ge(act_done, AC.after("norm", p))
                do("rinv", nc.vector.reciprocal(sq[:, :], sq[:, :]))
                do("kk", nc.vector.tensor_tensor(kk[:, :], kkr[:, :], sq[:, :], ALU.mult))
                do("kka", nc.vector.tensor_tensor(kka[:, :], kk[:, :], ta[:, :], ALU.mult))
                dve.wait_ge(act_done, AC.after("v", p))
                for n in range(N_RW):
                    dve.wait_ge(rw_out[n], 16 * p)
                dve.wait_ge(b_out, 16 * p)
                dve.wait_ge(d_out, 16 * p)
                mixed(2, fv, "v", C_MUV)
                dve.wait_ge(pe_done, PE.after("bonus", p))
                nc.vector.tensor_tensor(grouped(bonus[:, :]), zp[1][:, :, 0:TG], grouped(fv[:, :]), ALU.mult).then_inc(bonus_done, 1)
                for name, n, x, d in (("alpha", R_ALPHA, kk, Dp), ("beta", R_BETA, kka, Di),
                                      ("kappa", R_KAPPA, kp, Di), ("rho", R_RHO, fr, D)):
                    do(name, nc.vector.tensor_tensor(out[n][:, :], x[:, PROMPT], d[:, :], ALU.mult))
                do("dend", nc.vector.tensor_copy(dend[:, :], D[:, CL - 1:NP:CL]))
                for name, n, x in (("betae", R_BETAE, R_BETA), ("kappae", R_KAPPAE, R_KAPPA)):
                    do(name, nc.vector.tensor_tensor(chunks(out[n][:, :]), chunks(out[x][:, :]), each(dend[:, :]), ALU.mult))

        @block.gpsimd
        def _(pool):
            with pool.Fori(0, NPAIR) as p:
                pool.wait_ge(act_done, AC.after("g", p))
                stand_alone(pool, A)
                pool.dma_start(A["gate"][p], gate[:, :]).then_inc(g_out, 16)
                pool.wait_ge(dve_done, DV.after("v_f", p))
                stand_alone(pool, A)
                pool.dma_start(A["rw"][p, R_V], fv[:, PROMPT]).then_inc(rw_out[R_V], 16)
                pool.wait_ge(bonus_done, p + 1)
                stand_alone(pool, A)
                pool.dma_start(A["bonus"][p], bonus[:, :]).then_inc(b_out, 16)
                for name, n in (("alpha", R_ALPHA), ("beta", R_BETA), ("kappa", R_KAPPA), ("rho", R_RHO),
                                ("betae", R_BETAE), ("kappae", R_KAPPAE)):
                    pool.wait_ge(dve_done, DV.after(name, p))
                    stand_alone(pool, A)
                    pool.dma_start(A["rw"][p, n], out[n][:, :]).then_inc(rw_out[n], 16)
                    if name == "rho":
                        pool.wait_ge(dve_done, DV.after("dend", p))
                        stand_alone(pool, A)
                        pool.dma_start(A["dend"][p], dend[:, :]).then_inc(d_out, 16)
            for s in (*rw_out, g_out, b_out, d_out):
                pool.wait_ge(s, 16 * NPAIR)


def scan_pairs(nc, A):
    LEVELS = 5
    HT = NP // 2
    prep = [("ab", "D"), ("abT", "D"), ("akT", "D")]
    fill = {1: "vn", 2: "bn", 3: "kn", 4: "an", 5: "rbT"}
    for l in range(1, LEVELS + 1):
        prep.append((f"P{l}", "A"))
        if l < LEVELS:
            prep.append((f"PT{l}", "A"))
        prep += [(fill[l], "D" if fill[l] == "rbT" else "A"), (f"X{l}", "D")]
    prep += [("rkT", "D"), ("Z", "A"), ("GT", "A"), ("H", "A")]
    order = [n for n, _ in prep]
    on_act = dict((n, e == "A") for n, e in prep)
    slot_of = {n: i % 2 for i, n in enumerate(order)}
    assert len(order) % 2 == 0 and len(order) <= 2 * NC
    MID = NC // 2
    chain = [x for c in range(NC) for x in ((f"u{c}", "Y0", f"s{c}") if c == MID else (f"u{c}", f"s{c}"))] + ["Y1", "fin"]
    PP, PC, PT_ = Steps(*order), Steps(*chain), Steps("mean0", "var0", "mean1", "var1")
    AP, AC, AT = Steps(*[n for n in order if on_act[n]]), Steps("Y0", "Y1", "fin"), Steps("std0", "std1")
    DP = Steps("ab", "abT", "X0", "akT", "X1", "X2", "X3", "X4", "rbT", "X5", "rkT")
    DC = Steps(*[f"{x}{c}" for c in range(NC) for x in "us"])
    DT = Steps(*[f"{n}{g}" for g in range(2) for n in ("yc", "sqy", "tv", "ri", "yn", "ya", "yb")])
    TAIL1 = {1: "mean", 3: "var", 4: "ri", 5: "scale", 6: "gate"}
    TAIL0 = {MID + 2: "mean", MID + 4: "var", MID + 5: "ri", MID + 6: "scale", MID + 7: "gate"}
    with ExitStack() as ctx:
        ident, bd = A["sb_ident"], A["sb_bd"]
        sb = lambda n, s: ctx.enter_context(nc.sbuf_tensor(n, s, F32))
        two = lambda n, s: [sb(f"{n}{j}", s) for j in range(2)]
        psum = lambda n, w: ctx.enter_context(nc.psum_tensor(n, [P, w], F32))
        sem = ctx.enter_context(signals(nc))
        rw = two("r_in", [P, N_RW, NP])
        dend = two("r_dend", [P, NC])
        gate, bonus = sb("r_gate", [P, NP]), sb("r_bonus", [P, NP])
        prm = sb("r_prm", [P, NPAIR, NPRM])
        masks = sb("r_masks", [P, 5, CL])
        Pn, Pt = two("r_P", [P, NP]), two("r_PT", [P, NP])
        X, akT, an, Z = (sb("r_" + n, [P, NP]) for n in ("X", "akT", "an", "Z"))
        rbT, rkT, vn, bn, kn, GT, H = (two("r_" + n, [P, NP]) for n in ("rbT", "rkT", "vn", "bn", "kn", "GT", "H"))
        U = sb("r_U", [P, NP])
        ST = sb("r_ST", [P, (NC + 1) * HD])
        ysb, sqy = sb("r_y", [P, NP]), sb("r_sqy", [P, HT])
        fin = sb("r_fin", [P, HD])
        ps = [psum(f"r_ps{j}", NP) for j in range(2)]
        ups, sps, yps, tps = psum("r_ups", HT), psum("r_sps", HT), psum("r_yps", HT), psum("r_tps", HT)
        const_in = sem("r_const_in")
        rw_in, rho_in = [sem(f"r_rw_in{j}") for j in range(2)], [sem(f"r_rho_in{j}") for j in range(2)]
        gb_in, zeroed, fin_out, y_out = sem("r_gb_in"), sem("r_zeroed"), sem("r_fin_out"), sem("r_y_out")
        pe_prep, pe_chain, pe_tail = sem("r_pe_prep"), sem("r_pe_chain"), sem("r_pe_tail")
        act_prep, act_chain, act_tail = sem("r_act_prep"), sem("r_act_chain"), sem("r_act_tail")
        dve_prep, dve_chain, dve_tail = sem("r_dve_prep"), sem("r_dve_chain"), sem("r_dve_tail")
        block = ctx.enter_context(nc.Block())
        chunks = lambda ap: ap.rearrange("p (c l) -> p c l", l=CL)
        col = lambda c: slice(c * CL, (c + 1) * CL)
        bank = lambda c: col(c % MID)
        half = lambda h: slice(h * HD, (h + 1) * HD)
        tok = lambda g: slice(g * HT, (g + 1) * HT)
        EARLY = [n for n in range(N_RW) if n != R_RHO]

        def turns(engine, turn):
            turn(0, 0, False, True)
            with engine.Fori(0, NPAIR // 2 - 1) as i:
                turn(2 * i + 1, 1, True, True)
                turn(2 * i + 2, 0, True, True)
            turn(NPAIR - 1, (NPAIR - 1) % 2, True, False)

        @block.sync
        def _(sp):
            def load_early(p, j):
                for n in EARLY:
                    sp.dma_start(rw[j][:, n, :], A["rw"][p, n]).then_inc(rw_in[j], 16)

            def load_late(p, j):
                sp.dma_start(rw[j][:, R_RHO, :], A["rw"][p, R_RHO]).then_inc(rho_in[j], 16)
                sp.dma_start(dend[j][:, :], A["dend"][p]).then_inc(rho_in[j], 16)

            for p in range(2):
                load_early(p, p)
                if p == 0:
                    for d, s in ((masks[:, :, :], A["masks"]), (prm[:, :, :], A["prm"])):
                        sp.dma_start(d, s).then_inc(const_in, 16)
                load_late(p, p)
            with sp.Fori(0, NPAIR // 2 - 1) as i:
                for j in range(2):
                    p = 2 * i + j
                    sp.wait_ge(pe_prep, PP.after("rkT", p))
                    stand_alone(sp, A)
                    load_early(p + 2, j)
                    sp.wait_ge(pe_chain, PC.after("fin", p))
                    stand_alone(sp, A)
                    load_late(p + 2, j)

        @block.tensor
        def _(pe):
            def need(p, *names):
                for done, S in ((act_prep, AP), (dve_prep, DP), (act_chain, AC), (dve_chain, DC), (dve_tail, DT)):
                    mine = [n for n in names if n in S.at]
                    if mine:
                        pe.wait_ge(done, S.after(max(mine, key=S.at.get), p))
                stand_alone(pe, A)

            def prep_batch(g, p, j):
                name = order[g]
                r = [rw[j][:, n, :] for n in range(N_RW)]
                if name == "ab":
                    pe.wait_ge(rw_in[j], 8 * len(EARLY) * (p + 2 - j))
                if name == "rbT":
                    pe.wait_ge(rho_in[j], 16 * (p + 2 - j))
                if g < 2:
                    pe.wait_ge(act_prep, AP.n * p)
                    pe.wait_ge(dve_prep, DP.n * p)
                l = int(name[-1]) if name[-1].isdigit() else 0
                a, b = (l - 1) % 2, l % 2
                got = ("ab", "abT") if l == 1 else (f"P{l - 1}", f"PT{l - 1}")
                lhsT, rhs, inputs = {
                    "ab": (r[R_ALPHA], r[R_BETA], ()), "abT": (r[R_BETA], r[R_ALPHA], ()), "akT": (r[R_KAPPA], r[R_ALPHA], ()),
                    f"P{l}": (Pt[a], Pn[a], got), f"PT{l}": (Pn[a], Pt[a], got), f"X{l}": (Pn[b], X, (f"P{l}", f"X{l - 1}")),
                    "vn": (r[R_V], None, ()), "bn": (r[R_BETAE], None, ()), "kn": (r[R_KAPPAE], None, ()), "an": (r[R_ALPHA], None, ()),
                    "rbT": (r[R_BETA], r[R_RHO], ()), "rkT": (r[R_KAPPA], r[R_RHO], ()),
                    "Z": (akT, vn[j], ("akT", "vn")), "GT": (an, X, ("an", "X5")), "H": (X, Z, ("Z", "X5"))}[name]
                need(p, *([order[g - 2]] if g >= 2 else []), *inputs)
                for c in range(NC):
                    for h in range(2):
                        mm = pe.matmul(ps[slot_of[name]][half(h), col(c)], lhsT[half(h), col(c)],
                                       ident[half(h), half(h)] if rhs is None else rhs[half(h), col(c)],
                                       start=True, stop=True)
                mm.then_inc(pe_prep, 1)

            def y_chunk(c, p, j):
                for h in range(2):
                    out = yps[half(h), bank(c)]
                    pe.matmul(out, ST[half(h), col(c)], rw[j][half(h), R_RHO, col(c)], start=True, stop=False)
                    pe.matmul(out, U[half(h), col(c)], rbT[j][half(h), col(c)], start=False, stop=False)
                    mm = pe.matmul(out, vn[j][half(h), col(c)], rkT[j][half(h), col(c)], start=False, stop=True)
                return mm

            def tail(step, g, p):
                if step == "mean":
                    if g:
                        need(p, "tv0", "Y1")
                    else:
                        pe.wait_ge(dve_tail, DT.n * p)
                        need(p, "Y0")
                    pe.matmul(tps[:, :], bd[:, :], ysb[:, tok(g)], start=True, stop=True).then_inc(pe_tail, 1)
                if step == "var":
                    need(p, f"sqy{g}")
                    pe.matmul(tps[:, :], bd[:, :], sqy[:, :], start=True, stop=True).then_inc(pe_tail, 1)

            def turn(p, j, tail_open, more):
                pe.wait_ge(act_chain, AC.n * p)
                need(p, "GT", "H", "rkT")
                for c in range(NC):
                    if c:
                        need(p, f"s{c - 1}")
                    for h in range(2):
                        mm = pe.matmul(ups[half(h), bank(c)], GT[j][half(h), col(c)], ST[half(h), col(c)], start=True, stop=True)
                    mm.then_inc(pe_chain, 1)
                    if c == MID:
                        y_chunk(c - 1, p, j).then_inc(pe_chain, 1)
                    elif c:
                        if c == MID + 1:
                            need(p, "Y0")
                        y_chunk(c - 1, p, j)
                    if more and 2 * c < len(order):
                        prep_batch(2 * c, p + 1, 1 - j)
                    for h in range(2):
                        pe.matmul(sps[half(h), bank(c)], kn[j][half(h), col(c)], vn[j][half(h), col(c)], start=True, stop=False)
                    need(p, f"u{c}")
                    for h in range(2):
                        mm = pe.matmul(sps[half(h), bank(c)], bn[j][half(h), col(c)], U[half(h), col(c)], start=False, stop=True)
                    mm.then_inc(pe_chain, 1)
                    if more and 2 * c + 1 < len(order):
                        prep_batch(2 * c + 1, p + 1, 1 - j)
                    if c in TAIL1 and tail_open:
                        tail(TAIL1[c], 1, p - 1)
                    if c in TAIL0:
                        tail(TAIL0[c], 0, p)
                need(p, f"s{NC - 1}")
                y_chunk(NC - 1, p, j).then_inc(pe_chain, 1)
                for h in range(2):
                    mm = pe.matmul(ups[half(h), 0:HD], ST[half(h), col(NC)], ident[half(h), half(h)], start=True, stop=True)
                mm.then_inc(pe_chain, 1)

            pe.wait_ge(zeroed, 1)
            for g in range(len(order)):
                prep_batch(g, 0, 0)
            turns(pe, turn)
            tail("mean", 1, NPAIR - 1)
            tail("var", 1, NPAIR - 1)

        @block.scalar
        def _(act):
            def prep_batch(g, p, j):
                name = order[g]
                if not on_act[name]:
                    return
                to = {"vn": vn[j], "bn": bn[j], "kn": kn[j], "an": an, "Z": Z, "GT": GT[j], "H": H[j]}
                dst = to[name] if name in to else (Pt if name[1] == "T" else Pn)[int(name[-1]) % 2]
                act.wait_ge(pe_prep, PP.after(name, p))
                act.activation(dst[:, :], ps[slot_of[name]][:, :], ACT.Copy,
                               scale=-1.0 if name == "bn" else 1.0).then_inc(act_prep, 1)

            def y_half(g, p):
                act.wait_ge(pe_chain, PC.after(f"Y{g}", p))
                act.wait_ge(y_out, 16 * p)
                act.activation(ysb[:, tok(g)], yps[:, :], ACT.Copy).then_inc(act_chain, 1)

            def tail(step, g, p):
                if step == "var":
                    act.wait_ge(dve_tail, DT.after(f"tv{g}", p))
                    act.activation(sqy[:, :], sqy[:, :], ACT.Sqrt).then_inc(act_tail, 1)

            def turn(p, j, tail_open, more):
                for c in range(NC):
                    if c == MID:
                        y_half(0, p)
                    for g in (2 * c, 2 * c + 1):
                        if more and g < len(order):
                            prep_batch(g, p + 1, 1 - j)
                    if c in TAIL1 and tail_open:
                        tail(TAIL1[c], 1, p - 1)
                    if c in TAIL0:
                        tail(TAIL0[c], 0, p)
                y_half(1, p)
                act.wait_ge(pe_chain, PC.after("fin", p))
                act.wait_ge(fin_out, 16 * p)
                act.activation(fin[:, :], ups[:, 0:HD], ACT.Copy).then_inc(act_chain, 1)
                act.wait_ge(act_chain, AC.after("fin", p))
                act.dma_start(A["wkv_p"][bass.ds(p, 1)].rearrange("a p k -> (a p) k"), fin[:, :]).then_inc(fin_out, 16)

            for g in range(len(order)):
                prep_batch(g, 0, 0)
            turns(act, turn)
            tail("var", 1, NPAIR - 1)
            act.wait_ge(fin_out, 16 * NPAIR)

        @block.vector
        def _(dve):
            V = nc.vector
            mask = lambda n: masks[:, n, :].unsqueeze(1).broadcast_to([P, NC, CL])

            def done(sem_, S, name, p, ins):
                ins.then_inc(sem_, 1)
                dve.wait_ge(sem_, S.after(name, p))

            def prep_batch(g, p, j):
                name = order[g]
                if on_act[name]:
                    return
                dve.wait_ge(pe_prep, PP.after(name, p))
                src = ps[slot_of[name]]
                if name[0] == "X":
                    done(dve_prep, DP, name, p, V.tensor_tensor(X[:, :], src[:, :], X[:, :], ALU.add))
                    return
                dst, m = {"ab": (Pn[0], 0), "abT": (Pt[0], 1), "akT": (akT, 2), "rbT": (rbT[j], 3), "rkT": (rkT[j], 4)}[name]
                done(dve_prep, DP, name, p, V.tensor_tensor(chunks(dst[:, :]), chunks(src[:, :]), mask(m), ALU.mult))
                if name == "abT":
                    done(dve_prep, DP, "X0", p, V.tensor_tensor(chunks(X[:, :]), chunks(Pt[0][:, :]),
                                                                A["sb_eye2"][:, :].unsqueeze(1).broadcast_to([P, NC, CL]), ALU.add))

            def tail(step, g, p):
                do = lambda name, ins: done(dve_tail, DT, f"{name}{g}", p, ins)
                y, of_pair = ysb[:, tok(g)], lambda c: prm[:, bass.ds(p, 1), c:c + 1].rearrange("p a b -> p (a b)")
                if step == "mean":
                    dve.wait_ge(pe_tail, PT_.after(f"mean{g}", p))
                    do("yc", V.scalar_tensor_tensor(y, tps[:, :], -1.0 / HD, y, ALU.mult, ALU.add))
                    do("sqy", V.tensor_tensor(sqy[:, :], y, y, ALU.mult))
                if step == "var":
                    dve.wait_ge(pe_tail, PT_.after(f"var{g}", p))
                    do("tv", V.tensor_scalar(sqy[:, :], tps[:, :], 1.0 / HD, GN_EPS, ALU.mult, ALU.add))
                if step == "ri":
                    dve.wait_ge(act_tail, AT.after(f"std{g}", p))
                    do("ri", V.reciprocal(sqy[:, :], sqy[:, :]))
                if step == "scale":
                    dve.wait_ge(gb_in, 32 * (p + 1))
                    do("yn", V.scalar_tensor_tensor(y, y, of_pair(C_LG), sqy[:, :], ALU.mult, ALU.mult))
                    do("ya", V.scalar_tensor_tensor(y, y, of_pair(C_LB), bonus[:, tok(g)], ALU.add, ALU.add))
                if step == "gate":
                    do("yb", V.tensor_tensor(y, y, gate[:, tok(g)], ALU.mult))

            def turn(p, j, tail_open, more):
                dve.wait_ge(act_prep, AP.after("H", p))
                dve.wait_ge(rho_in[j], 16 * (p + 2 - j))
                for c in range(NC):
                    dve.wait_ge(pe_chain, PC.after(f"u{c}", p))
                    done(dve_chain, DC, f"u{c}", p, V.tensor_tensor(U[:, col(c)], ups[:, bank(c)], H[j][:, col(c)], ALU.add))
                    if more and 2 * c < len(order):
                        prep_batch(2 * c, p + 1, 1 - j)
                    dve.wait_ge(pe_chain, PC.after(f"s{c}", p))
                    done(dve_chain, DC, f"s{c}", p, V.scalar_tensor_tensor(ST[:, col(c + 1)], ST[:, col(c)], dend[j][:, c:c + 1],
                                                                           sps[:, bank(c)], ALU.mult, ALU.add))
                    if more and 2 * c + 1 < len(order):
                        prep_batch(2 * c + 1, p + 1, 1 - j)
                    if c in TAIL1 and tail_open:
                        tail(TAIL1[c], 1, p - 1)
                    if c in TAIL0:
                        tail(TAIL0[c], 0, p)

            dve.wait_ge(const_in, 32)
            V.memset(ST[:, 0:HD], 0.0).then_inc(zeroed, 1)
            dve.wait_ge(zeroed, 1)
            for g in range(len(order)):
                prep_batch(g, 0, 0)
            turns(dve, turn)
            for step in TAIL1.values():
                tail(step, 1, NPAIR - 1)

        @block.gpsimd
        def _(pool):
            def load(p):
                pool.dma_start(gate[:, :], A["gate"][p, :, 0:NP]).then_inc(gb_in, 16)
                pool.dma_start(bonus[:, :], A["bonus"][p, :, 0:NP]).then_inc(gb_in, 16)

            def store(p):
                pool.wait_ge(dve_tail, DT.after("yb1", p))
                stand_alone(pool, A)
                pool.dma_start(A["bT"][p, :, 0:NP], ysb[:, :]).then_inc(y_out, 16)

            load(0)
            with pool.Fori(0, NPAIR - 1) as p:
                store(p)
                load(p + 1)
            store(NPAIR - 1)
            pool.wait_ge(y_out, 16 * NPAIR)


def attend(nc, A):
    UN = 4
    UNITS = NH // UN
    NBUF = 4
    STEPS_ = NBUF * UNITS

    def staged(front, mid, tail):
        out = []
        for s in range(STEPS_ + 2):
            for stage, d in ((front, 0), (mid, 1), (tail, 2)):
                if 0 <= s - d < STEPS_:
                    out += [x + str(s - d) for x in stage]
        return out

    PE = Steps(*staged(("sc",), ("pt", "pv"), ("at",)))
    DV = Steps(*staged(("s1_", "s2_", "mx", "ms", "nm", "sd"), ("den", "rec", "on"), ()))
    ac = []
    for s in range(STEPS_ + 2):
        if 0 <= s - 1 < STEPS_:
            ac.append(f"cp{s - 1}")
        if s < STEPS_:
            ac += [f"e{x}_{s}" for x in range(UN)] + [f"es{s}"]
        if 0 <= s - 2:
            ac.append(f"ac{s - 2}")
    AC = Steps(*ac)
    with ExitStack() as ctx:
        ident = A["sb_ident"]
        sb = lambda n, s: ctx.enter_context(nc.sbuf_tensor(n, s, F32))
        sem = ctx.enter_context(signals(nc))
        relb, oneh = sb("a_relb", [REL_ROWS, NH]), sb("a_oneh", [REL_ROWS, 3 * WIN])
        tab = sb("a_tab", [NH, 3 * WIN])
        bias = sb("a_bias", [P, NH, 2 * WIN])
        sinks, sink8 = sb("a_sinks", [P, NH]), sb("a_sink8", [P, NH])
        pen = sb("a_pen", [P, NB])
        q = [sb(f"a_q{j}", [P, KT, 2, WIN]) for j in range(NBUF)]
        kT, vT = sb("a_kT", [P, 2, WIN + NP]), sb("a_vT", [P, 2, NP])
        kb = [sb(f"a_kb{j}", [P, 2, 2 * WIN]) for j in range(NBUF)]
        vnat = sb("a_vnat", [P, NB + 1, NKV * HD])
        knat = sb("a_knat", [P, NKV * HD])
        Sx = [sb(f"a_S{j}", [P, UN, 2 * WIN]) for j in range(2)]
        PTs = [sb(f"a_PT{j}", [P, UN, 2, WIN]) for j in range(2)]
        on = [sb(f"a_on{j}", [P, UN * HD]) for j in range(2)]
        aT = A["sb_aT"]
        mx, ms, nm, sd, es, sums, den = (sb("a_" + n, [P, STEPS_, UN]) for n in ("mx", "ms", "nm", "sd", "es", "sums", "den"))
        scp = [ctx.enter_context(nc.psum_tensor(f"a_scp{j}", [P, UN, 2 * WIN], F32)) for j in range(2)]
        ptp = ctx.enter_context(nc.psum_tensor("a_ptp", [P, UN, 2, WIN], F32))
        outp = ctx.enter_context(nc.psum_tensor("a_outp", [P, 1, UN * HD], F32))
        atp = ctx.enter_context(nc.psum_tensor("a_atp", [P, 1, 2, WIN], F32))
        const_in, tab_out, bias_in, kv_in = sem("a_const_in"), sem("a_tab_out"), sem("a_bias_in"), sem("a_kv_in")
        q_in = [sem(f"a_q_in{j}") for j in range(NBUF)]
        win_out, kb_ready, ahead_in = sem("a_win_out"), sem("a_kb_ready"), sem("a_ahead_in")
        pre_pe, pre_act, pre_dve = sem("a_pre_pe"), sem("a_pre_act"), sem("a_pre_dve")
        pe_done, act_done, dve_done = sem("a_pe_done"), sem("a_act_done"), sem("a_dve_done")
        block = ctx.enter_context(nc.Block())

        @block.sync
        def _(sp):
            for d, s in ((relb[0:REL_ROWS - 1, :], A["rel_bias"]), (oneh[:, :], A["onehot"]), (sinks[:, :], A["sinks"]), (pen[:, :], A["pen"])):
                sp.dma_start(d, s).then_inc(const_in, 16)
            for t in range(2):
                sp.dma_start(kT[:, t, WIN:], A["zT"][T_K + t, :, 0:NP]).then_inc(kv_in, 16)
                sp.dma_start(vT[:, t, :], A["zT"][T_V + t, :, 0:NP]).then_inc(kv_in, 16)
            sp.wait_ge(pre_act, 1)
            sp.dma_start(A["tab"], tab[:, :].unsqueeze(1).broadcast_to([NH, P, 3 * WIN])).then_inc(tab_out, 16)
            sp.wait_ge(tab_out, 16)
            for h in range(NH):
                src = bass.AP(A["tab"].tensor, h * P * 3 * WIN + WIN - 1, [[3 * WIN - 1, P], [1, 2 * WIN]])
                sp.dma_start(bias[:, h, :], src).then_inc(bias_in, 16)
            with sp.Fori(0, NB // NBUF) as i:
                for j in range(NBUF):
                    sp.wait_ge(pe_done, PE.n * i)
                    for h in range(2):
                        o = slice(h * HD, (h + 1) * HD)
                        sp.dma_start(q[j][o, :, h, :], A["zT"][T_Q:T_Q + KT, o, bass.ds((NBUF * i + j) * WIN, WIN)]
                                     .rearrange("t p c -> p t c")).then_inc(q_in[j], 16)
            sp.wait_ge(pre_act, 2 + NB)
            sp.dma_start(A["win_k_p"], knat[:, :]).then_inc(win_out, 16)
            sp.dma_start(A["win_v_p"], vnat[:, NB, :]).then_inc(win_out, 16)
            sp.wait_ge(win_out, 32)

        @block.tensor
        def _(pe):
            pe.wait_ge(const_in, 64)
            pe.wait_ge(pre_dve, 1)
            pe.matmul(scp[0][0:NH, :, :].rearrange("p a b -> p (a b)")[:, 0:3 * WIN],
                      relb[:, :], oneh[:, :], start=True, stop=True).then_inc(pre_pe, 1)
            pe.wait_ge(kv_in, 64)
            for b in range(NB):
                if b >= 2:
                    pe.wait_ge(pre_act, b)
                for t in range(2):
                    mm = pe.transpose(ptp[:, 2 * (b % 2), t, :], vT[:, t, b * WIN:(b + 1) * WIN], ident[:, :])
                mm.then_inc(pre_pe, 1)
            pe.wait_ge(pre_act, NB)
            for t in range(2):
                mm = pe.transpose(ptp[:, 0, t, :], kT[:, t, NP:], ident[:, :])
            mm.then_inc(pre_pe, 1)
            pe.wait_ge(pre_act, 2 + NB)
            pe.wait_ge(pre_dve, 4 + 2 * NBUF)
            with pe.Fori(0, NB // NBUF) as i:
                for s in range(STEPS_ + 2):
                    if s < STEPS_:
                        j, u = s // UNITS, s % UNITS
                        if u == 0:
                            pe.wait_ge(q_in[j], 32 * i + 32)
                            pe.wait_ge(kb_ready, NBUF * i + j + 1)
                        if s >= 2:
                            pe.wait_ge(dve_done, DV.after(f"s2_{s - 2}", i))
                        else:
                            pe.wait_ge(dve_done, DV.n * i)
                            pe.wait_ge(act_done, AC.n * i)
                        for x in range(UN):
                            t, h = 2 * u + x % 2, x // 2
                            mm = pe.matmul(scp[s % 2][:, x, :], q[j][:, t, h, :],
                                           kb[j][:, u // 2, :], start=True, stop=True)
                        mm.then_inc(pe_done, 1)
                    m = s - 1
                    if 0 <= m < STEPS_:
                        j, u = m // UNITS, m % UNITS
                        pe.wait_ge(act_done, AC.after(f"e{UN - 1}_{m}", i))
                        if m:
                            pe.wait_ge(act_done, AC.after(f"cp{m - 1}", i))
                        for x in range(UN):
                            for b in range(2):
                                mm = pe.transpose(ptp[:, x, b, :], Sx[m % 2][:, x, b * WIN:(b + 1) * WIN], ident[:, :])
                        mm.then_inc(pe_done, 1)
                        pe.wait_ge(act_done, AC.after(f"cp{m}", i))
                        if m >= 1:
                            pe.wait_ge(dve_done, DV.after(f"on{m - 1}", i))
                        for x in range(UN):
                            kv = 2 * (u // 2) + x // 2
                            c = 2 * (x % 2) + x // 2
                            for b in range(2):
                                mm = pe.matmul(outp[:, 0, c * HD:(c + 1) * HD], PTs[m % 2][:, x, b, :],
                                               vnat[:, bass.ds(NBUF * i + j + b, 1), kv * HD:(kv + 1) * HD].rearrange("p a b -> p (a b)"),
                                               start=(b == 0), stop=(b == 1))
                        mm.then_inc(pe_done, 1)
                    m = s - 2
                    if m >= 0:
                        pe.wait_ge(dve_done, DV.after(f"on{m}", i))
                        if m >= 1:
                            pe.wait_ge(act_done, AC.after(f"ac{m - 1}", i))
                        for x in range(2):
                            mm = pe.transpose(atp[:, 0, x, :], on[m % 2][:, x * P:(x + 1) * P], ident[:, :])
                        mm.then_inc(pe_done, 1)

        @block.scalar
        def _(act):
            act.wait_ge(pre_pe, 1)
            act.activation(tab[:, :], scp[0][0:NH, :, :].rearrange("p a b -> p (a b)")[:, 0:3 * WIN], ACT.Copy).then_inc(pre_act, 1)
            for b in range(NB):
                act.wait_ge(pre_pe, 2 + b)
                act.activation(vnat[:, b + 1, :], ptp[:, 2 * (b % 2), :, :].rearrange("p a b -> p (a b)"), ACT.Copy).then_inc(pre_act, 1)
            act.wait_ge(pre_pe, 2 + NB)
            act.activation(knat[:, :], ptp[:, 0, :, :].rearrange("p a b -> p (a b)"), ACT.Copy).then_inc(pre_act, 1)
            with act.Fori(0, NB // NBUF) as i:
                for s in range(STEPS_ + 2):
                    m = s - 1
                    if 0 <= m < STEPS_:
                        act.wait_ge(pe_done, PE.after(f"pt{m}", i))
                        if m >= 2:
                            act.wait_ge(pe_done, PE.after(f"pv{m - 2}", i))
                        act.activation(PTs[m % 2][:, :, :, :], ptp[:, :, :, :], ACT.Copy).then_inc(act_done, 1)
                    if s < STEPS_:
                        act.wait_ge(dve_done, DV.after(f"sd{s}", i))
                        for x in range(UN):
                            act.activation(Sx[s % 2][:, x, :], Sx[s % 2][:, x, :], ACT.Exp, bias=nm[:, s, x:x + 1],
                                           scale=HD ** -0.5, accum_out=sums[:, s, x:x + 1]).then_inc(act_done, 1)
                        act.activation(es[:, s, :], sd[:, s, :], ACT.Exp).then_inc(act_done, 1)
                    m = s - 2
                    if m >= 0:
                        j, u = m // UNITS, m % UNITS
                        act.wait_ge(pe_done, PE.after(f"at{m}", i))
                        act.activation(aT[:, 2 * u:2 * u + 2, bass.ds((NBUF * i + j) * WIN, WIN)], atp[:, 0, :, :], ACT.Copy).then_inc(act_done, 1)

        @block.vector
        def _(dve):
            nc.vector.memset(relb[REL_ROWS - 1:REL_ROWS, :], 1.0).then_inc(pre_dve, 1)
            nc.vector.memset(kT[:, :, 0:WIN], 0.0).then_inc(pre_dve, 1)
            nc.vector.memset(vnat[:, 0, :], 0.0).then_inc(pre_dve, 1)
            for j in range(NBUF):
                for h in range(2):
                    nc.vector.memset(q[j][(1 - h) * HD:(2 - h) * HD, :, h, :], 0.0).then_inc(pre_dve, 1)
            dve.wait_ge(const_in, 64)
            nc.vector.tensor_scalar(sink8[:, :], sinks[:, :], HD ** 0.5, None, ALU.mult).then_inc(pre_dve, 1)
            dve.wait_ge(pre_dve, 4 + 2 * NBUF)
            dve.wait_ge(bias_in, 16 * NH)
            with dve.Fori(0, NB // NBUF) as i:
                def do(name, ins):
                    ins.then_inc(dve_done, 1)
                    dve.wait_ge(dve_done, DV.after(name, i))

                for s in range(STEPS_ + 1):
                    if s < STEPS_:
                        j, u = s // UNITS, s % UNITS
                        hs = slice(u * UN, (u + 1) * UN)
                        dve.wait_ge(pe_done, PE.after(f"sc{s}", i))
                        if s >= 2:
                            dve.wait_ge(pe_done, PE.after(f"pt{s - 2}", i))
                        do(f"s1_{s}", nc.vector.scalar_tensor_tensor(Sx[s % 2][:, :, 0:WIN], scp[s % 2][:, :, 0:WIN], pen[:, bass.ds(NBUF * i + j, 1)],
                                                                     bias[:, hs, 0:WIN], ALU.add, ALU.add))
                        do(f"s2_{s}", nc.vector.tensor_tensor(Sx[s % 2][:, :, WIN:], scp[s % 2][:, :, WIN:], bias[:, hs, WIN:], ALU.add))
                        do(f"mx{s}", nc.vector.tensor_reduce(mx[:, s, :], Sx[s % 2][:, :, :], AX_X, ALU.max))
                        do(f"ms{s}", nc.vector.tensor_tensor(ms[:, s, :], mx[:, s, :], sink8[:, hs], ALU.max))
                        do(f"nm{s}", nc.vector.tensor_scalar(nm[:, s, :], ms[:, s, :], -(HD ** -0.5), None, ALU.mult))
                        do(f"sd{s}", nc.vector.tensor_tensor(sd[:, s, :], sinks[:, hs], nm[:, s, :], ALU.add))
                    m = s - 1
                    if 0 <= m:
                        dve.wait_ge(act_done, AC.after(f"es{m}", i))
                        do(f"den{m}", nc.vector.tensor_tensor(den[:, m, :], sums[:, m, :], es[:, m, :], ALU.add))
                        do(f"rec{m}", nc.vector.reciprocal(den[:, m, :], den[:, m, :]))
                        dve.wait_ge(pe_done, PE.after(f"pv{m}", i))
                        if m >= 2:
                            dve.wait_ge(pe_done, PE.after(f"at{m - 2}", i))
                        do(f"on{m}", nc.vector.tensor_tensor(on[m % 2][:, :].rearrange("p (t h d) -> p t h d", t=2, h=2),
                                                             outp[:, 0, :].rearrange("p (t h d) -> p t h d", t=2, h=2),
                                                             den[:, m, :].rearrange("p (h t) -> p t h", h=2).unsqueeze(3).broadcast_to([P, 2, 2, HD]),
                                                             ALU.mult))

        @block.gpsimd
        def _(pool):
            for d, s in ([(A["sb_bT"][:, k, 0:NP], A["bT"][k]) for k in range(KT)] +
                         [(A["sb_S"][:, :, :].rearrange("p v k -> p (v k)"), A["state"]), (A["sb_kc"][:, :, :, :], A["kc"]),
                          (A["sb_vc"][:, :, :], A["vc"])]):
                pool.dma_start(d, s).then_inc(ahead_in, 16)
            pool.wait_ge(kv_in, 64)
            pool.wait_ge(pre_dve, 4 + 2 * NBUF)
            with pool.Fori(0, NB // NBUF) as i:
                pool.wait_ge(pe_done, PE.n * i)
                for j in range(NBUF):
                    nc.gpsimd.tensor_copy(kb[j][:, :, :], kT[:, :, bass.ds((NBUF * i + j) * WIN, 2 * WIN)]).then_inc(kb_ready, 1)
            pool.wait_ge(ahead_in, 16 * (KT + 3))


def decode(nc, A):
    BH = NS * NH
    J = WIN + 1
    R_, W_, K_, V_, KK_, KKA_ = range(6)
    DV = Steps("t0", "sa", "Sw", "t1", "S1", "t2", "S2", "ones", "sink8", "sT0", "sT1", "qk", "self", "s_own", "s_raw", "s",
               "mx", "ms", "nm", "sd", "den", "rec", "p", "t3", "y",
               "mu", "mun", "yc", "y2", "var", "tv", "ri", "yn", "b0", "b1", "b2", "b3")
    with ExitStack() as ctx:
        ident = A["sb_ident"]
        sb = lambda n, s: ctx.enter_context(nc.sbuf_tensor(n, s, F32))
        sem = ctx.enter_context(signals(nc))
        bank = lambda n: ctx.enter_context(nc.psum_tensor(n, [P, 512], F32))
        relb, oneh = sb("d_relb", [REL_ROWS, BH]), sb("d_oneh", [REL_ROWS, 3 * WIN])
        sinks, sink8 = sb("d_sinks", [P, 1]), sb("d_sink8", [P, 1])
        qT = sb("d_qT", [P, KT, NS])
        kc, vc, S = A["sb_kc"], A["sb_vc"], A["sb_S"]
        qn, kn = sb("d_qn", [P, HD]), sb("d_kn", [P, HD])
        vrow, prow = sb("d_vrow", [1, NS, NKV * HD]), sb("d_prow", [1, BH])
        sT, s = sb("d_sT", [P, BH]), sb("d_s", [P, J])
        pT = sb("d_pT", [P, BH])
        small = sb("d_small", [P, 16])
        vec = sb("d_vec", [P, 6, HD])
        tmp = sb("d_tmp", [P, HD, HD])
        sa, y, y2 = sb("d_sa", [P, HD]), sb("d_y", [P, HD]), sb("d_y2", [P, HD])
        yrow = sb("d_yrow", [NS, DM])
        prm = sb("d_prm", [P, NPAIR, NPRM])
        gate, bonus, b_ = sb("d_gate", [P, NPAIR, NS]), sb("d_bonus", [P, NPAIR, NS]), A["sb_bT"][:, :, NP:]
        sc0, sc1, bp, tp, pp, op, rp, yp = (bank("d_ps" + n) for n in ("sc0", "sc1", "bp", "tp", "pp", "op", "rp", "yp"))
        att_in, own_in, rwkv_in, y_out, y_in = (sem("d_" + n) for n in ("att_in", "own_in", "rwkv_in", "y_out", "y_in"))
        caches_out = sem("d_caches_out")
        pe_done, act_done, dve_done = sem("d_pe_done"), sem("d_act_done"), sem("d_dve_done")
        PE = Steps("bias", "sc", "tp", "pT", "prow", "o", "yT")
        AC = Steps("p", "es", "pT", "prow", "oT", "std")
        block = ctx.enter_context(nc.Block())
        mx, ms, nm, sd, es, sums, den, own, mu, var = (small[:, i:i + 1] for i in range(10))

        @block.sync
        def _(sp):
            for d, s_ in ((relb[:, :], A["rel_bias_d"]), (oneh[:, :], A["onehot"]), (sinks[:, :], A["sinks_d"]),
                          (qT[:, :, :], A["zT"][T_Q:T_Q + KT, :, NP:].rearrange("t p b -> p t b"))):
                sp.dma_start(d, s_).then_inc(att_in, 16)
            zn = A["zn"]
            for b in range(NS):
                rows = slice(b * NH, (b + 1) * NH)
                sp.dma_start(qn[rows, :], zn[1 + b, T_Q:T_Q + KT, :].rearrange("t (h d) -> (t h) d", h=2)).then_inc(own_in, 16)
                for g in range(2):
                    for t in range(4):
                        r = b * NH + g * 8 + t * 2
                        sp.dma_start(kn[r:r + 2, :], zn[1 + b, T_K + g, :].rearrange("(h d) -> h d", h=2)).then_inc(own_in, 16)
                sp.dma_start(vrow[0:1, b, :], zn[1 + b:2 + b, T_V:T_V + 2, :].rearrange("a t f -> a (t f)")).then_inc(own_in, 16)
            sp.wait_ge(dve_done, DV.after("yn"))
            sp.dma_start(A["yd"].rearrange("b (h d) -> (b h) d", d=HD), y[:, :]).then_inc(y_out, 16)
            sp.wait_ge(y_out, 16)
            sp.dma_start(yrow[:, :], A["yd"]).then_inc(y_in, 16)

        @block.gpsimd
        def _(pool):
            zn = A["zn"]
            for cache, out, t in ((A["cache_k"], A["win_k_s"], T_K), (A["cache_v"], A["win_v_s"], T_V)):
                pool.dma_start(out[:, 0:WIN - 1, :], cache[:, 1:, :]).then_inc(caches_out, 16)
                pool.dma_start(out[:, WIN - 1, :], zn[1:, t:t + 2, :].rearrange("b t f -> b (t f)")).then_inc(caches_out, 16)
            for n, q in enumerate((Q_PAIR_R, Q_PAIR_K, Q_PAIR_V)):
                pool.dma_start(A["shift"][:, n * DM:(n + 1) * DM].rearrange("b (p f) -> b p f", f=P),
                               zn[:, T_PAIR + q:N_TILES:3, :]).then_inc(caches_out, 16)
            pool.dma_start(A["shift"][:, 3 * DM:].rearrange("b (t f) -> b t f", f=P), zn[:, T_XWA:T_XG + 1, :]).then_inc(caches_out, 16)
            pool.wait_ge(dve_done, DV.after("S2"))
            pool.dma_start(A["wkv_s"], S[:, :, :].rearrange("p v k -> p (v k)")).then_inc(caches_out, 16)
            pool.wait_ge(caches_out, 16 * 9)

        @block.tensor
        def _(pe):
            pe.wait_ge(att_in, 16 * 4)
            pe.matmul(bp[:, 0:J], relb[:, :], oneh[:, WIN - 1:2 * WIN], start=True, stop=True).then_inc(pe_done, 1)
            for b in range(NS):
                for g in range(2):
                    for h, dst in ((0, sc0), (1, sc1)):
                        o = slice(h * HD, (h + 1) * HD)
                        mm = pe.matmul(dst[:, b * KT + 4 * g:b * KT + 4 * g + 4], kc[o, b, g, :],
                                       qT[o, 4 * g:4 * g + 4, b], start=True, stop=True)
            mm.then_inc(pe_done, 1)
            pe.wait_ge(dve_done, DV.after("sT1"))
            pe.transpose(tp[:, 0:WIN], sT[:, :], ident[:, :]).then_inc(pe_done, 1)
            pe.wait_ge(dve_done, DV.after("p"))
            pe.transpose(pp[:, 0:BH], s[:, 0:WIN], ident[:, :]).then_inc(pe_done, 1)
            pe.transpose(rp[0:1, 0:BH], s[:, WIN:J], ident[:, :]).then_inc(pe_done, 1)
            pe.wait_ge(act_done, AC.after("prow"))
            pe.wait_ge(own_in, 16 * 10 * NS)
            for b in range(NS):
                for g in range(2):
                    for h in range(2):
                        kv = 2 * g + h
                        dst = op[h * HD:(h + 1) * HD, 0:KT * NS].rearrange("p (t b) -> p t b", b=NS)[:, 4 * g:4 * g + 4, b]
                        c = b * NH + 8 * g + h
                        pe.matmul(dst, vc[:, b, kv * HD:(kv + 1) * HD], pT[:, c:c + 7:2], start=True, stop=False)
                        mm = pe.matmul(dst, vrow[0:1, b, kv * HD:(kv + 1) * HD], prow[0:1, c:c + 7:2], start=False, stop=True)
            mm.then_inc(pe_done, 1)
            pe.wait_ge(y_in, 16)
            for t in range(NPAIR):
                mm = pe.transpose(yp[:, t * NS:(t + 1) * NS], yrow[:, t * P:(t + 1) * P], ident[0:NS, 0:NS])
            mm.then_inc(pe_done, 1)

        @block.scalar
        def _(act):
            act.dma_start(vec[:, :, :], A["decn"].rearrange("b p h q d -> (b p h) q d")).then_inc(rwkv_in, 16)
            for d, s_ in ((prm[:, :, :], A["prm"]), (gate[:, :, :], A["gate"][:, :, NP:].rearrange("t p b -> p t b")),
                          (bonus[:, :, :], A["bonus"][:, :, NP:].rearrange("t p b -> p t b"))):
                act.dma_start(d, s_).then_inc(rwkv_in, 16)
            act.wait_ge(dve_done, DV.after("sd"))
            act.activation(s[:, :], s[:, :], ACT.Exp, bias=nm, scale=HD ** -0.5, accum_out=sums).then_inc(act_done, 1)
            act.activation(es, sd, ACT.Exp).then_inc(act_done, 1)
            act.wait_ge(pe_done, PE.after("pT"))
            act.activation(pT[:, :], pp[:, 0:BH], ACT.Copy).then_inc(act_done, 1)
            act.wait_ge(pe_done, PE.after("prow"))
            act.activation(prow[:, :], rp[0:1, 0:BH], ACT.Copy).then_inc(act_done, 1)
            act.wait_ge(pe_done, PE.after("o"))
            act.activation(A["sb_aT"][:, :, NP:], op[:, 0:KT * NS].rearrange("p (t b) -> p t b", b=NS), ACT.Copy).then_inc(act_done, 1)
            act.wait_ge(dve_done, DV.after("tv"))
            act.activation(var, var, ACT.Sqrt).then_inc(act_done, 1)

        @block.vector
        def _(dve):
            V = nc.vector

            def do(name, ins):
                ins.then_inc(dve_done, 1)
                dve.wait_ge(dve_done, DV.after(name))

            over_v = lambda n: vec[:, n, :].unsqueeze(1).broadcast_to([P, HD, HD])
            over_k = lambda ap: ap.unsqueeze(2).broadcast_to([P, HD, HD])
            dve.wait_ge(rwkv_in, 64)
            do("t0", V.tensor_tensor(tmp[:, :, :], S[:, :, :], over_v(KK_), ALU.mult))
            do("sa", V.tensor_reduce(sa[:, :], tmp[:, :, :], AX_X, ALU.add))
            do("Sw", V.tensor_tensor(S[:, :, :], S[:, :, :], over_v(W_), ALU.mult))
            do("t1", V.tensor_tensor(tmp[:, :, :], over_k(sa[:, :]), over_v(KKA_), ALU.mult))
            do("S1", V.tensor_tensor(S[:, :, :], S[:, :, :], tmp[:, :, :], ALU.subtract))
            do("t2", V.tensor_tensor(tmp[:, :, :], over_k(vec[:, V_, :]), over_v(K_), ALU.mult))
            do("S2", V.tensor_tensor(S[:, :, :], S[:, :, :], tmp[:, :, :], ALU.add))
            dve.wait_ge(att_in, 16 * 4)
            do("ones", V.memset(small[:, :], 0.0))
            do("sink8", V.tensor_scalar(sink8[:, :], sinks[:, :], HD ** 0.5, None, ALU.mult))
            dve.wait_ge(pe_done, PE.after("sc"))
            for h, src in ((0, sc0), (1, sc1)):
                do(f"sT{h}", V.tensor_copy(sT[:, h:BH:2], src[:, 0:BH // 2]))
            dve.wait_ge(own_in, 16 * 10 * NS)
            do("qk", V.tensor_tensor(qn[:, :], qn[:, :], kn[:, :], ALU.mult))
            do("self", V.tensor_reduce(own, qn[:, :], AX_X, ALU.add))
            dve.wait_ge(pe_done, PE.after("tp"))
            do("s_own", V.tensor_copy(s[:, WIN:J], own))
            do("s_raw", V.tensor_copy(s[:, 0:WIN], tp[:, 0:WIN]))
            do("s", V.tensor_tensor(s[:, :], s[:, :], bp[:, 0:J], ALU.add))
            do("mx", V.tensor_reduce(mx, s[:, :], AX_X, ALU.max))
            do("ms", V.tensor_tensor(ms, mx, sink8[:, :], ALU.max))
            do("nm", V.tensor_scalar(nm, ms, -(HD ** -0.5), None, ALU.mult))
            do("sd", V.tensor_tensor(sd, sinks[:, :], nm, ALU.add))
            dve.wait_ge(act_done, AC.after("es"))
            do("den", V.tensor_tensor(den, sums, es, ALU.add))
            do("rec", V.reciprocal(den, den))
            do("p", V.tensor_scalar(s[:, :], s[:, :], den, None, ALU.mult))
            do("t3", V.tensor_tensor(tmp[:, :, :], S[:, :, :], over_v(R_), ALU.mult))
            do("y", V.tensor_reduce(y[:, :], tmp[:, :, :], AX_X, ALU.add))
            do("mu", V.tensor_reduce(mu, y[:, :], AX_X, ALU.add))
            do("mun", V.tensor_scalar(mu, mu, -1.0 / HD, None, ALU.mult))
            do("yc", V.tensor_scalar(y[:, :], y[:, :], mu, None, ALU.add))
            do("y2", V.tensor_tensor(y2[:, :], y[:, :], y[:, :], ALU.mult))
            do("var", V.tensor_reduce(var, y2[:, :], AX_X, ALU.add))
            do("tv", V.tensor_scalar(var, var, 1.0 / HD, GN_EPS, ALU.mult, ALU.add))
            dve.wait_ge(act_done, AC.after("std"))
            do("ri", V.reciprocal(var, var))
            do("yn", V.tensor_scalar(y[:, :], y[:, :], var, None, ALU.mult))
            dve.wait_ge(pe_done, PE.after("yT"))
            per = lambda c: prm[:, :, c:c + 1].broadcast_to([P, NPAIR, NS])
            do("b0", V.tensor_tensor(b_, yp[:, 0:NPAIR * NS].rearrange("p (t b) -> p t b", b=NS), per(C_LG), ALU.mult))
            do("b1", V.tensor_tensor(b_, b_, per(C_LB), ALU.add))
            do("b2", V.tensor_tensor(b_, b_, bonus[:, :, :], ALU.add))
            do("b3", V.tensor_tensor(b_, b_, gate[:, :, :], ALU.mult))


def merge(nc, A):
    with ExitStack() as ctx:
        sb = lambda n, s: ctx.enter_context(nc.sbuf_tensor(n, s, F32))
        sem = ctx.enter_context(signals(nc))
        src = [A["sb_aT"], A["sb_bT"]]
        w = [[sb(f"m_w{j}{x}", [P, KT, P]) for x in range(2)] for j in range(2)]
        g = [[sb(f"m_g{j}{x}", [P, NT]) for x in range(2)] for j in range(2)]
        m = [sb(f"m_m{j}", [P, NT]) for j in range(2)]
        zero = sb("m_zero", [P, NPAD - NT])
        ps = [ctx.enter_context(nc.psum_tensor(f"m_ps{x}", [P, 3, 512], F32)) for x in range(2)]
        each = lambda n: [[sem(f"m_{n}{j}{x}") for x in range(2)] for j in range(2)]
        w_in, product, opened, gated = each("w_in"), each("product"), each("opened"), each("gated")
        g_in, summed, m_out = ([sem(f"m_{n}{j}") for j in range(2)] for n in ("g_in", "summed", "m_out"))
        zeroed, pad_out = sem("m_zeroed"), sem("m_pad_out")
        block = ctx.enter_context(nc.Block())

        @block.sync
        def _(sp):
            with sp.Fori(0, KT // 2) as i:
                for j in range(2):
                    for x, name in enumerate(("wba_tiles", "wbr_tiles")):
                        sp.wait_ge(product[j][x], i)
                        sp.dma_start(w[j][x][:, :, :], A[name][2 * i + j]).then_inc(w_in[j][x], 16)
                    sp.wait_ge(summed[j], i)
                    for x, t in enumerate((T_GA, T_GB)):
                        sp.dma_start(g[j][x][:, :], A["zT"][2 * i + j + t]).then_inc(g_in[j], 16)

        @block.tensor
        def _(pe):
            with pe.Fori(0, KT // 2) as i:
                for j in range(2):
                    for x in range(2):
                        pe.wait_ge(w_in[j][x], 16 * i + 16)
                        pe.wait_ge(gated[1 - j][x], i + j)
                        for c in range(3):
                            for k in range(KT):
                                mm = pe.matmul(ps[x][:, c, 0:TG], w[j][x][:, k, :], src[x][:, k, c * TG:(c + 1) * TG],
                                               start=(k == 0), stop=(k == KT - 1))
                        mm.then_inc(product[j][x], 1)

        @block.scalar
        def _(act):
            with act.Fori(0, KT // 2) as i:
                for j in range(2):
                    act.wait_ge(g_in[j], 32 * i + 32)
                    for x in range(2):
                        act.activation(g[j][x][:, :], g[j][x][:, :], ACT.Sigmoid).then_inc(opened[j][x], 1)

        @block.vector
        def _(dve):
            nc.vector.memset(zero[:, :], 0.0).then_inc(zeroed, 1)
            with dve.Fori(0, KT // 2) as i:
                for j in range(2):
                    for x in range(2):
                        dve.wait_ge(opened[j][x], i + 1)
                        dve.wait_ge(product[j][x], i + 1)
                        nc.vector.tensor_tensor(grouped(g[j][x][:, :]), ps[x][:, :, 0:TG], grouped(g[j][x][:, :]),
                                                ALU.mult).then_inc(gated[j][x], 1)
                        dve.wait_ge(gated[j][x], i + 1)
                    dve.wait_ge(m_out[j], 16 * i)
                    nc.vector.tensor_tensor(m[j][:, :], g[j][0][:, :], g[j][1][:, :], ALU.add).then_inc(summed[j], 1)

        @block.gpsimd
        def _(pool):
            pool.wait_ge(zeroed, 1)
            for k in range(KT):
                pool.dma_start(A["mT"][k, :, NT:], zero[:, :]).then_inc(pad_out, 16)
            with pool.Fori(0, KT // 2) as i:
                for j in range(2):
                    pool.wait_ge(summed[j], i + 1)
                    stand_alone(pool, A)
                    pool.dma_start(A["mT"][2 * i + j, :, 0:NT], m[j][:, :]).then_inc(m_out[j], 16)
            pool.wait_ge(pad_out, 16 * KT)
            for j in range(2):
                pool.wait_ge(m_out[j], 16 * (KT // 2))


PH, NKEY, TOPK = 8, 128, 16
SLOTS = PH * TOPK
CAND = [(i, TOPK // (i + 1)) for i in range(TOPK)]
NCAND = sum(n for _, n in CAND)
LOW = -3.0e38


def peer(nc, A):
    RING = 16
    USES = 2 * SLOTS // RING
    ON_DVE = 4
    NV = SLOTS // ON_DVE
    with ExitStack() as ctx:
        ident = A["sb_ident"]
        sb = lambda n, s, d=F32: ctx.enter_context(nc.sbuf_tensor(n, s, d))
        sem = ctx.enter_context(signals(nc))
        psum = lambda n, w: ctx.enter_context(nc.psum_tensor(n, [P, w], F32))
        wo, wq = sb("f_wo", [P, KT, DM]), sb("f_wq", [P, KT, DM])
        keys = sb("f_keys", [P, PH, NKEY])
        ln = sb("f_ln", [P, 4, DM])
        ring = sb("f_ring", [P, RING, DM])
        mTb, xb = sb("f_mTb", [P, KT, P]), sb("f_xb", [P, DM])
        h = [sb(f"f_h{j}", [P, DM]) for j in range(2)]
        hT = sb("f_hT", [P, KT, P])
        scs = sb("f_scs", [P, 2, PH, NKEY])
        st, ag, rs = sb("f_st", [P, 2, 6]), sb("f_ag", [P, 2]), sb("f_rs", [P, 1])
        st2, ag2, rs2 = sb("f_st2", [P, 2, 6]), sb("f_ag2", [P, 2]), sb("f_rs2", [P, 1])
        s2 = sb("f_s2", [P, NKEY])
        sv, si, sif = sb("f_sv", [P, 2, PH, TOPK]), sb("f_si", [P, 2, PH, TOPK], U32), sb("f_sif", [P, 2, PH, TOPK])
        cand, cidx, iota = sb("f_cand", [P, PH, NCAND]), sb("f_cidx", [P, PH, NCAND]), sb("f_iota", [P, NCAND])
        c2 = sb("f_c2", [P, NCAND])
        fv, fi, fif = sb("f_fv", [P, PH, TOPK]), sb("f_fi", [P, PH, TOPK], U32), sb("f_fif", [P, PH, TOPK])
        eq = sb("f_eq", [P, TOPK, NCAND])
        ef = sb("f_ef", [P, PH, TOPK])
        eidx = [sb(f"f_eidx{j}", [P, SLOTS], U32) for j in range(2)]
        gate = [sb(f"f_gate{j}", [P, PH, TOPK]) for j in range(2)]
        gs = sb("f_gs", [P, PH])
        dots, wts = sb("f_dots", [P, SLOTS]), sb("f_wts", [P, SLOTS])
        diag = [sb(f"f_diag{r}", [P, P]) for r in range(4)]
        yacc = sb("f_yacc", [P, DM])
        flag = sb("f_flag", [1, 1])
        wexp = sb("f_wexp", [P, NS, NS])
        fps, sps, yps = psum("f_fps", 1024), psum("f_sps", 2048), psum("f_yps", 1024)
        const_in, wo_in, ln_in, ld_m, ld_x = sem("f_const_in"), sem("f_wo_in"), sem("f_ln_in"), sem("f_ld_m"), sem("f_ld_x")
        (mixed, h0_done, var_done, std_done, h_done, hT_psum, hT_done, q_psum, q_done, sc_psum, sc_done, topk_done,
         idx_done, fv_done, fe_done) = (sem("f_" + n) for n in (
             "mixed", "h0_done", "var_done", "std_done", "h_done", "hT_psum", "hT_done", "q_psum", "q_done", "sc_psum",
             "sc_done", "topk_done", "idx_done", "fv_done", "fe_done"))
        gelu_done, w_done, y_read, var2_done, std2_done, y_done = (sem("f_" + n) for n in (
            "gelu_done", "w_done", "y_read", "var2_done", "std2_done", "y_done"))
        y_out = sem("f_y_out")
        got = [sem(f"f_got{r}") for r in range(RING)]
        used = [sem(f"f_used{r}") for r in range(RING)]
        diag_done, link = sem("f_diag_done"), sem("f_link")
        (d_ready, d_by_slot, d_idx, d_select, d_spread, d_gelu, d_w, d_sum, d_var, d_std, d_done, d_out) = (sem("f_d_" + n) for n in (
            "ready", "by_slot", "idx", "select", "spread", "gelu", "w", "sum", "var", "std", "done", "out"))
        block = ctx.enter_context(nc.Block())
        on_pe = [s for s in range(SLOTS) if s % ON_DVE != ON_DVE - 1]

        @block.sync
        def _(sp):
            def load(f):
                sp.wait_ge(mixed, f)
                sp.dma_start(mTb[:, :, :], A["mT"][:, :, bass.ds(f * P, P)].rearrange("t p c -> p t c")).then_inc(ld_m, 16)
                sp.wait_ge(h0_done, f)
                sp.dma_start(xb[:, :], A["x_pad"][f]).then_inc(ld_x, 16)

            for k in range(KT):
                sp.dma_start(wo[:, k, :], A["w_out"][k]).then_inc(wo_in, 16)
            load(0)
            sp.dma_start(ln[:, :, :], A["ln"]).then_inc(ln_in, 16)
            for k in range(KT):
                sp.dma_start(wq[:, k, :], A["peer_q"][k]).then_inc(const_in, 16)
            for d, s in ((keys[:, :, :], A["keysT"]), (iota[:, :], A["iota"])):
                sp.dma_start(d, s).then_inc(const_in, 16)
            with sp.Fori(0, NB // 2) as i:
                for j in range(2):
                    b = 2 * i + j
                    load(b + 1)
                    sp.wait_ge(y_done, b + 1)
                    sp.dma_start(A["y"][bass.ds(b * P, P), :], yacc[:, :]).then_inc(y_out, 16)
            sp.wait_ge(y_out, 16 * NB)
            sp.wait_ge(d_done, 1)
            sp.dma_start(A["y"][NP:NT, :], yacc[0:NS, :]).then_inc(d_out, 16)
            sp.wait_ge(d_out, 16)

        @block.gpsimd
        def _(pool):
            with pool.Fori(0, NB // 2) as i:
                for j in range(2):
                    b = 2 * i + j
                    pool.wait_ge(idx_done, b + 1)
                    for n in range(2 * SLOTS):
                        table, s, r = ("peer_u", "peer_v")[n // SLOTS], n % SLOTS, n % RING
                        pool.wait_ge(used[r], USES * b + n // RING)
                        stand_alone(pool, A)
                        pool.indirect_dma_start(out=ring[:, r, :], out_offset=None, in_=A[table],
                                                in_offset=bass.IndirectOffsetOnAxis(ap=eidx[j][:, s:s + 1], axis=0)).then_inc(got[r], 16)
            pool.wait_ge(d_idx, 1)
            for n in range(2 * NS):
                pool.wait_ge(used[n], USES * NB)
                pool.indirect_dma_start(out=ring[:, n, :], out_offset=None, in_=A[("peer_u", "peer_v")[n // NS]],
                                        in_offset=bass.IndirectOffsetOnAxis(ap=fi[:, 0, n % NS:n % NS + 1], axis=0)).then_inc(got[n], 16)

        @block.tensor
        def _(pe):
            def front(f):
                pe.wait_ge(ld_m, 16 * f + 16)
                pe.wait_ge(q_done, f)
                for c in range(2):
                    for k in range(KT):
                        mm = pe.matmul(fps[:, c * 512:(c + 1) * 512], mTb[:, k, :], wo[:, k, c * 512:(c + 1) * 512],
                                       start=(k == 0), stop=(k == KT - 1))
                mm.then_inc(mixed, 1)

            def front2(f, j):
                pe.wait_ge(h_done, f + 1)
                for k in range(KT):
                    mm = pe.transpose(fps[:, k * P:(k + 1) * P], h[j][:, k * P:(k + 1) * P], ident[:, :])
                mm.then_inc(hT_psum, 1)
                pe.wait_ge(hT_done, f + 1)
                for x in range(PH):
                    for k in range(KT):
                        mm = pe.matmul(fps[:, x * P:(x + 1) * P], wq[:, k, x * P:(x + 1) * P], hT[:, k, :],
                                       start=(k == 0), stop=(k == KT - 1))
                mm.then_inc(q_psum, 1)
                pe.wait_ge(q_done, f + 1)
                pe.wait_ge(sc_done, 2 * f)
                for x in range(PH):
                    for c in range(2):
                        mm = pe.matmul(sps[:, (c * PH + x) * NKEY:(c * PH + x + 1) * NKEY], hT[c * HD:(c + 1) * HD, x, :],
                                       keys[c * HD:(c + 1) * HD, x, :], start=True, stop=True)
                mm.then_inc(sc_psum, 1)

            pe.wait_ge(wo_in, 16 * KT)
            front(0)
            pe.wait_ge(const_in, 16 * (KT + 2))
            front2(0, 0)
            with pe.Fori(0, NB // 2) as i:
                for j in range(2):
                    b = 2 * i + j
                    front(b + 1)
                    front2(b + 1, 1 - j)
                    pe.wait_ge(y_read, b)
                    for m, s in enumerate(on_pe):
                        n = SLOTS + s
                        pe.wait_ge(diag_done, len(on_pe) * b + m + 1)
                        pe.wait_ge(got[n % RING], 16 * (USES * b + n // RING + 1))
                        for c in range(2):
                            mm = pe.matmul(yps[:, c * 512:(c + 1) * 512], diag[m % 4][:, :], ring[:, n % RING, c * 512:(c + 1) * 512],
                                           start=(m == 0), stop=(m == len(on_pe) - 1))
                        mm.then_inc(used[n % RING], 1)
            pe.wait_ge(d_ready, 1)
            pe.transpose(fps[:, 0:NS], ef[0:NS, :, :].rearrange("p a b -> p (a b)"), ident[0:NS, 0:NS])
            pe.transpose(fps[:, 512:512 + NS], gate[0][0:NS, :, :].rearrange("p a b -> p (a b)"), ident[0:NS, 0:NS]).then_inc(d_by_slot, 1)
            pe.wait_ge(d_select, 1)
            for t in range(NS):
                if t >= 2:
                    pe.wait_ge(used[t - 2], USES * NB + 1)
                for c in range(2):
                    mm = pe.matmul(sps[:, (t % 2) * DM + c * 512:(t % 2) * DM + (c + 1) * 512], scs[0:NS, 0, t, :],
                                   h[0][0:NS, c * 512:(c + 1) * 512], start=True, stop=True)
                mm.then_inc(d_spread, 1)
            pe.wait_ge(d_w, 1)
            for t in range(NS):
                pe.wait_ge(got[NS + t], 16 * (USES * NB + 1))
                for c in range(2):
                    mm = pe.matmul(yps[0:NS, c * 512:(c + 1) * 512], wexp[:, t, :], ring[:, NS + t, c * 512:(c + 1) * 512], start=(t == 0), stop=(t == NS - 1))
            mm.then_inc(d_sum, 1)

        @block.scalar
        def _(act):
            def front(f):
                act.wait_ge(var_done, f + 1)
                act.activation(rs[:, :], rs[:, :], ACT.Sqrt).then_inc(std_done, 1)
                act.wait_ge(hT_psum, f + 1)
                act.wait_ge(sc_psum, f)
                act.activation(hT[:, :, :].rearrange("p a b -> p (a b)"), fps[:, :], ACT.Copy).then_inc(hT_done, 1)
                act.wait_ge(q_psum, f + 1)
                act.activation(hT[:, :, :].rearrange("p a b -> p (a b)"), fps[:, :], ACT.Copy).then_inc(q_done, 1)
                act.wait_ge(sc_psum, f + 1)
                act.wait_ge(topk_done, f)
                for c in range(2):
                    act.activation(scs[:, c, :, :].rearrange("p a b -> p (a b)"), sps[:, c * 1024:(c + 1) * 1024], ACT.Copy).then_inc(sc_done, 1)

            def soften(f, j):
                act.wait_ge(fv_done, f + 1)
                act.activation(gate[j][:, :, :], gate[j][:, :, :], ACT.Exp).then_inc(fe_done, 1)

            front(0)
            soften(0, 0)
            with act.Fori(0, NB // 2) as i:
                for j in range(2):
                    b = 2 * i + j
                    front(b + 1)
                    for r in range(RING):
                        act.wait_ge(used[r], USES * b + USES // 2)
                    act.activation(dots[:, :], dots[:, :], ACT.Gelu).then_inc(gelu_done, 1)
                    act.wait_ge(w_done, b + 1)
                    for m, s in enumerate(on_pe):
                        if m < 4:
                            act.wait_ge(y_read, b)
                        else:
                            n = SLOTS + on_pe[m - 4]
                            act.wait_ge(used[n % RING], USES * b + n // RING + 1)
                        act.activation(diag[m % 4][:, :], ident[:, :], ACT.Copy, scale=wts[:, s:s + 1]).then_inc(diag_done, 1)
                    soften(b + 1, 1 - j)
                    act.wait_ge(var2_done, b + 1)
                    act.activation(rs2[:, :], rs2[:, :], ACT.Sqrt).then_inc(std2_done, 1)
            act.wait_ge(used[NS - 1], USES * NB + 1)
            act.activation(dots[:, 0:NS], dots[:, 0:NS], ACT.Gelu).then_inc(d_gelu, 1)
            act.wait_ge(d_var, 1)
            act.activation(rs2[0:NS, :], rs2[0:NS, :], ACT.Sqrt).then_inc(d_std, 1)

        @block.vector
        def _(dve):
            V = nc.vector
            N_TAIL = 7
            count = [0]

            def chain(base):
                count[0] = 0

                def lnk(ins):
                    count[0] += 1
                    ins.then_inc(link, 1)
                    dve.wait_ge(link, base + count[0])
                return lnk

            def mark(ins, s, v):
                ins.then_inc(s, 1)
                dve.wait_ge(s, v)

            def moments(lnk, x, st, ag, rows=P):
                for c in range(2):
                    lnk(V.bn_stats(st[0:rows, c, :], x[0:rows, c * 512:(c + 1) * 512]))
                stand_alone(dve, A)
                lnk(V.bn_aggr(ag[0:rows, :], st[0:rows, :, :].rearrange("p a b -> p (a b)")))

            def front_a(f, j, lnk):
                dve.wait_ge(mixed, f + 1)
                dve.wait_ge(ld_x, 16 * f + 16)
                mark(V.scalar_tensor_tensor(h[j][:, :], xb[:, :], ALPHA, fps[:, :], ALU.mult, ALU.add), h0_done, f + 1)
                moments(lnk, h[j], st, ag)
                mark(V.tensor_scalar(rs[:, :], ag[:, 1:2], LN_EPS, None, ALU.add), var_done, f + 1)

            def front_b(f, j, lnk):
                dve.wait_ge(std_done, f + 1)
                lnk(V.reciprocal(rs[:, :], rs[:, :]))
                lnk(V.tensor_scalar(h[j][:, :], h[j][:, :], ag[:, 0:1], rs[:, 0:1], ALU.subtract, ALU.mult))
                lnk(V.tensor_tensor(h[j][:, :], h[j][:, :], ln[:, 0, :], ALU.mult))
                mark(V.tensor_tensor(h[j][:, :], h[j][:, :], ln[:, 1, :], ALU.add), h_done, f + 1)

            def best16(lnk, src, copy, val, idx, last=None):
                stand_alone(dve, A)
                lnk(V.max(val[:, 0:8], src))
                stand_alone(dve, A)
                V.max_index(idx[:, 0:8], val[:, 0:8], src).then_inc(link, 1)
                count[0] += 1
                lnk(V.match_replace(copy, val[:, 0:8], src, LOW))
                stand_alone(dve, A)
                lnk(V.max(val[:, 8:16], copy))
                stand_alone(dve, A)
                (last or lnk)(V.max_index(idx[:, 8:16], val[:, 8:16], copy))

            def rows(f, n, lnk):
                c, x = n // PH, n % PH
                dve.wait_ge(sc_done, 2 * f + 2)
                last = (lambda ins: mark(ins, topk_done, f + 1)) if n == 2 * PH - 1 else None
                best16(lnk, scs[:, c, x, :], s2[:, :], sv[:, c, x, :], si[:, c, x, :], last)

            def sums(lnk, out, v):
                o = 0
                for a, n in CAND[:TOPK // 2]:
                    lnk(V.tensor_tensor(out[:, :, o:o + n], v[:, 1, :, 0:n], v[:, 0, :, a:a + 1].broadcast_to([P, PH, n]), ALU.add))
                    o += n
                lnk(V.tensor_tensor(out[:, :, o:], v[:, 0, :, TOPK // 2:], v[:, 1, :, 0:1].broadcast_to([P, PH, TOPK // 2]), ALU.add))

            def candidates(lnk):
                lnk(V.tensor_copy(sif[:, :, :, :], si[:, :, :, :]))
                lnk(V.tensor_scalar(sif[:, 0, :, :], sif[:, 0, :, :], float(NKEY), None, ALU.mult))
                sums(lnk, cand, sv)

            def best(x, lnk):
                best16(lnk, cand[:, x, :], c2[:, :], fv[:, x, :], fi[:, x, :])

            def expert_of(x, lnk):
                if x == 0:
                    lnk(V.tensor_copy(fif[:, :, :], fi[:, :, :]))
                lnk(V.tensor_tensor(eq[:, :, :], iota[:, :].unsqueeze(1).broadcast_to([P, TOPK, NCAND]),
                                    fif[:, x, :].unsqueeze(2).broadcast_to([P, TOPK, NCAND]), ALU.is_equal))
                lnk(V.tensor_tensor(eq[:, :, :], eq[:, :, :], cidx[:, x, :].unsqueeze(1).broadcast_to([P, TOPK, NCAND]), ALU.mult))
                lnk(V.tensor_reduce(ef[:, x, :], eq[:, :, :], AX_X, ALU.add))

            def finish(f, j):
                mark(V.tensor_copy(eidx[j][:, :], ef[:, :, :].rearrange("p a b -> p (a b)")), idx_done, f + 1)
                mark(V.tensor_tensor(gate[j][:, :, :], fv[:, :, :], fv[:, :, 0:1].broadcast_to([P, PH, TOPK]), ALU.subtract), fv_done, f + 1)

            def gates(f, j, lnk):
                dve.wait_ge(fe_done, f + 1)
                lnk(V.tensor_reduce(gs[:, :], gate[j][:, :, :], AX_X, ALU.add))
                lnk(V.reciprocal(gs[:, :], gs[:, :]))
                lnk(V.tensor_tensor(gate[j][:, :, :], gate[j][:, :, :], gs[:, :].unsqueeze(2).broadcast_to([P, PH, TOPK]), ALU.mult))

            def second_norm(lnk, rows, var_s, std_s, done_s, v):
                moments(lnk, yacc, st2, ag2, rows)
                mark(V.tensor_scalar(rs2[0:rows, :], ag2[0:rows, 1:2], LN_EPS, None, ALU.add), var_s, v)
                dve.wait_ge(std_s, v)
                lnk(V.reciprocal(rs2[0:rows, :], rs2[0:rows, :]))
                lnk(V.tensor_scalar(yacc[0:rows, :], yacc[0:rows, :], ag2[0:rows, 0:1], rs2[0:rows, 0:1], ALU.subtract, ALU.mult))
                lnk(V.tensor_tensor(yacc[0:rows, :], yacc[0:rows, :], ln[0:rows, 2, :], ALU.mult))
                mark(V.tensor_tensor(yacc[0:rows, :], yacc[0:rows, :], ln[0:rows, 3, :], ALU.add), done_s, v)

            lnk = chain(0)
            front_a(0, 0, lnk)
            dve.wait_ge(ln_in, 16)
            front_b(0, 0, lnk)
            dve.wait_ge(const_in, 16 * (KT + 2))
            for n in range(2 * PH):
                rows(0, n, lnk)
            candidates(lnk)
            sums(lnk, cidx, sif)
            for x in range(PH):
                best(x, lnk)
            for x in range(PH):
                expert_of(x, lnk)
            finish(0, 0)
            gates(0, 0, lnk)
            n_front = count[0]
            n_turn = n_front + N_TAIL
            with dve.Fori(0, NB // 2) as i:
                for j in range(2):
                    b = 2 * i + j
                    f = b + 1
                    lnk = chain(n_front + n_turn * b)
                    for s in range(SLOTS):
                        r = s % RING
                        dve.wait_ge(got[r], 16 * (USES * b + s // RING + 1))
                        V.tensor_tensor_reduce(ring[:, r, :], ring[:, r, :], h[j][:, :], 1.0, 0.0, ALU.mult, ALU.add,
                                               dots[:, s:s + 1]).then_inc(used[r], 1)
                        if s == 24:
                            front_a(f, 1 - j, lnk)
                        if s == 32:
                            front_b(f, 1 - j, lnk)
                    dve.wait_ge(gelu_done, b + 1)
                    mark(V.tensor_tensor(wts[:, :], dots[:, :], gate[j][:, :, :].rearrange("p a b -> p (a b)"), ALU.mult), w_done, b + 1)
                    dve.wait_ge(y_out, 16 * b)
                    lnk(V.tensor_scalar(yacc[:, :], h[j][:, :], ALPHA, None, ALU.mult))
                    for m in range(NV):
                        s = ON_DVE * m + ON_DVE - 1
                        n = SLOTS + s
                        dve.wait_ge(got[n % RING], 16 * (USES * b + n // RING + 1))
                        mark(V.scalar_tensor_tensor(yacc[:, :], ring[:, n % RING, :], wts[:, s:s + 1], yacc[:, :], ALU.mult, ALU.add),
                             used[n % RING], USES * b + n // RING + 1)
                        if m < 8:
                            rows(f, 2 * m, lnk)
                            rows(f, 2 * m + 1, lnk)
                        elif m == 8:
                            candidates(lnk)
                        elif m == 9:
                            sums(lnk, cidx, sif)
                        elif m < 14:
                            for x in range(2):
                                best(2 * (m - 10) + x, lnk)
                        elif m < 18:
                            for x in range(2):
                                expert_of(2 * (m - 14) + x, lnk)
                        elif m == 18:
                            finish(f, 1 - j)
                    dve.wait_ge(used[(SLOTS + on_pe[-1]) % RING], USES * b + USES)
                    mark(V.tensor_tensor(yacc[:, :], yacc[:, :], yps[:, :], ALU.add), y_read, b + 1)
                    second_norm(lnk, P, var2_done, std2_done, y_done, b + 1)
                    gates(f, 1 - j, lnk)
                    assert count[0] == n_turn

            lnk = chain(n_front + n_turn * NB)
            lnk(V.memset(wexp[:, :, :], 0.0))
            mark(V.tensor_copy(scs[0:NS, 0, :, :], ident[0:NS, 0:NS].unsqueeze(2).broadcast_to([NS, NS, NKEY])), d_select, 1)
            mark(V.memset(flag[:, :], 0.0), d_ready, 1)
            dve.wait_ge(d_by_slot, 1)
            mark(V.tensor_copy(fi[:, 0, 0:NS], fps[:, 0:NS]), d_idx, 1)
            lnk(V.tensor_copy(fif[:, 0, 0:NS], fps[:, 512:512 + NS]))
            for t in range(NS):
                dve.wait_ge(got[t], 16 * (USES * NB + 1))
                dve.wait_ge(d_spread, t + 1)
                V.tensor_tensor_reduce(ring[:, t, :], ring[:, t, :], sps[:, (t % 2) * DM:(t % 2 + 1) * DM], 1.0, 0.0, ALU.mult, ALU.add,
                                       dots[:, t:t + 1]).then_inc(used[t], 1)
            dve.wait_ge(d_gelu, 1)
            mark(V.tensor_tensor(wexp[:, :, :].rearrange("p a b -> p (a b)")[:, 0:NS * NS:NS + 1], dots[:, 0:NS], fif[:, 0, 0:NS], ALU.mult), d_w, 1)
            dve.wait_ge(y_out, 16 * NB)
            dve.wait_ge(d_sum, 1)
            lnk(V.scalar_tensor_tensor(yacc[0:NS, :], h[0][0:NS, :], ALPHA, yps[0:NS, :], ALU.mult, ALU.add))
            second_norm(lnk, NS, d_var, d_std, d_done, 1)


def program(nc, A, phases=99):
    with ExitStack() as ctx:
        A["passed"] = ctx.enter_context(nc.semaphore("c_passed"))
        A["sb_ident"] = ctx.enter_context(nc.sbuf_tensor("c_ident", [P, P], F32))
        A["sb_bd"] = ctx.enter_context(nc.sbuf_tensor("c_bd", [P, P], F32))
        A["sb_eye2"] = ctx.enter_context(nc.sbuf_tensor("c_eye2", [P, HD], F32))
        with ExitStack() as c1:
            A["sb_xT"] = c1.enter_context(nc.sbuf_tensor("c_xT", [P, KT, NT], F32))
            project_plain(nc, A)
            if phases > 1:
                project_pairs(nc, A)
        if phases > 2:
            scan_pairs(nc, A)
        with ExitStack() as c2:
            held = lambda n, s: c2.enter_context(nc.sbuf_tensor(n, s, F32))
            A["sb_aT"], A["sb_bT"] = held("c_aT", [P, KT, NT]), held("c_bT", [P, KT, NT])
            with ExitStack() as c3:
                held = lambda n, s: c3.enter_context(nc.sbuf_tensor(n, s, F32))
                A["sb_S"] = held("c_S", [P, HD, HD])
                A["sb_kc"], A["sb_vc"] = held("c_kc", [P, NS, 2, WIN]), held("c_vc", [P, NS, NKV * HD])
                if phases > 3:
                    attend(nc, A)
                if phases > 4:
                    decode(nc, A)
            if phases > 5:
                merge(nc, A)
        if phases > 6:
            peer(nc, A)


def scratch(nc, A):
    for name, shape in (("zT", (N_TILES, P, NT)), ("zn", (NS + 1, N_TILES, P)), ("rw", (NPAIR, N_RW, P, NP)),
                        ("gate", (NPAIR, P, NT)), ("bonus", (NPAIR, P, NT)), ("dend", (NPAIR, P, NC)),
                        ("decn", (NS, NPAIR, 2, 6, HD)), ("yd", (NS, DM)), ("bT", (NPAIR, P, NP)),
                        ("tab", (NH, P, 3 * WIN)), ("mT", (KT, P, NPAD))):
        A[name] = nc.dram_tensor("s_" + name, shape, F32).ap()


def bucket(rel):
    half = 16
    n = np.maximum(rel, 0)
    nf = np.maximum(n, half).astype(np.float32)
    large = half + (np.log(nf / np.float32(half)) / np.float32(math.log(128 / half)) * np.float32(half)).astype(np.int32)
    return np.where(n < half, n, np.minimum(large, 2 * half - 1))


def layouts(x):
    f = lambda n: np.asarray(x[n], np.float32)
    xall = np.concatenate([f("x_prompt")[0], f("x_sample")[:, 0]], 0)
    w = f("w_in")[0]
    q0, k0, v0 = 0, NH * HD, NH * HD + NKV * HD
    r0 = v0 + NKV * HD
    l0 = r0 + 3 * DM
    g0 = l0 + 2 * HD + P
    heads = [(2 * (t // 4) + h) * 4 + t % 4 for t in range(KT) for h in range(2)]
    cols = [h * HD + i for h in heads for i in range(HD)]
    cols += list(range(k0, r0)) + list(range(l0, g0)) + list(range(g0, g0 + 2 * DM))
    pair = []
    for p in range(NPAIR):
        for base in (DM, 0, 2 * DM):
            pair += list(range(base + p * P, base + (p + 1) * P))
    cols = np.array(cols + [r0 + c for c in pair])
    feats = np.array([3 * DM + i for i in range(2 * P)] + pair)
    tiles = lambda m: np.ascontiguousarray(m.reshape(KT, P, -1, P).transpose(2, 1, 0, 3))
    mu = f("rwkv_mu")[0]
    per = lambda v: v.reshape(NPAIR, P).T
    prm = np.stack([per(mu[DM:2 * DM]), per(mu[0:DM]), per(mu[2 * DM:3 * DM])] +
                   [per(f(n)[0]) for n in ("rwkv_w0", "rwkv_a0", "rwkv_k_k", "rwkv_k_a", "rwkv_r_k",
                                           "rwkv_lnx_g", "rwkv_lnx_b")], 2)
    upwa = np.concatenate([f("rwkv_w_up")[0], f("rwkv_a_up")[0]], 0).reshape(P, NPAIR, P)
    upg = f("rwkv_g_up")[0].reshape(P, NPAIR, P)
    d = {
        "xT": xall.T.reshape(KT, P, NT).transpose(1, 0, 2),
        "w_tiles": tiles(w[:, cols]),
        "shT": f("state_shift")[0].T[feats].reshape(-1, P, NS).transpose(1, 0, 2),
        "prm": prm,
        "mu_lora": mu[3 * DM:].reshape(2, P).T,
        "up": np.stack([upwa, upg], 2).transpose(1, 0, 2, 3),
        "ident": np.eye(P, dtype=np.float32),
        "bd": np.kron(np.eye(2), np.ones((HD, HD))).astype(np.float32),
    }
    d["eye2"] = np.tile(np.eye(HD, dtype=np.float32), (2, 1))
    i, j = np.arange(CL)[:, None], np.arange(CL)[None, :]
    ms = [-1.0 * (j < i), -1.0 * (j > i), 1.0 * (j > i), -1.0 * (j >= i), 1.0 * (j >= i)]
    d["masks"] = np.tile(np.stack(ms, 1), (2, 1, 1)).astype(np.float32)
    order = [heads[2 * (2 * u + t) + h] for u in range(KT // 2) for h in range(2) for t in range(2)]
    d["rel_bias"] = f("rel_bias")[:, order]
    d["sinks"] = np.tile(f("attn_sinks")[0][order], (P, 1))
    d["pen"] = np.tile(np.where(np.arange(NB) == 0, MASKED, 0.0).astype(np.float32), (P, 1))
    by_tile = [heads[2 * t + h] for t in range(KT) for h in range(2)]
    d["rel_bias_d"] = np.concatenate([np.tile(f("rel_bias")[:, by_tile], (1, NS)), np.ones((1, NS * NH), np.float32)], 0)
    d["sinks_d"] = np.tile(f("attn_sinks")[0][by_tile], NS)[:, None]
    ck, cv = f("cache_win_k")[0], f("cache_win_v")[0]
    d["cache_k"], d["cache_v"] = ck.reshape(NS, WIN, -1), cv.reshape(NS, WIN, -1)
    d["kc"] = ck.reshape(NS, WIN, 2, P).transpose(3, 0, 2, 1)
    d["vc"] = cv.reshape(NS, WIN, -1).transpose(1, 0, 2)
    d["state"] = f("state_wkv")[0].reshape(NS * NH, HD * HD)
    d["wba_tiles"] = tiles(f("w_branch_attn")[0][[h * HD + i for h in by_tile for i in range(HD)]])
    d["wbr_tiles"] = tiles(f("w_branch_rwkv")[0])
    d["w_out"] = f("w_out")[0].reshape(KT, P, DM)
    d["peer_q"] = f("peer_q")[0].reshape(KT, P, DM)
    d["keysT"] = f("peer_keys")[0].transpose(1, 3, 0, 2).reshape(P, PH, NKEY)
    d["ln"] = np.tile(np.stack([f(n)[0] for n in ("ln1_g", "ln1_b", "ln2_g", "ln2_b")]), (P, 1, 1))
    d["iota"] = np.tile(np.arange(NCAND, dtype=np.float32), (P, 1))
    d["x_pad"] = np.concatenate([xall, np.zeros((NPAD - NT, DM), np.float32)], 0).reshape(NB + 1, P, DM)
    d["peer_u"], d["peer_v"] = f("peer_u")[0], f("peer_v")[0]
    rel = 2 * WIN - 1 - np.arange(3 * WIN)
    ok = (rel >= 0) & (rel <= WIN)
    oneh = np.zeros((REL_ROWS, 3 * WIN), np.float32)
    oneh[bucket(rel)[ok], np.arange(3 * WIN)[ok]] = HD ** 0.5
    oneh[REL_ROWS - 1, ~ok] = MASKED
    d["onehot"] = oneh
    return {k: np.ascontiguousarray(v) for k, v in d.items()}


_OUTS = [("y", (NT, DM)), ("win_k_p", (WIN, NKV * HD)), ("win_v_p", (WIN, NKV * HD)), ("wkv_p", (NPAIR, P, HD)),
         ("shift", (NS + 1, 3 * DM + 2 * P)), ("win_k_s", (NS, WIN, NKV * HD)), ("win_v_s", (NS, WIN, NKV * HD)),
         ("wkv_s", (NS * NH, HD * HD))]


def kernel(**inputs):
    import concourse.bacc as _bacc
    from concourse.bass_utils import run_bass_kernel_spmd as _run

    nc = _bacc.Bacc("TRN2", target_bir_lowering=False, num_devices=1)
    arrays = layouts(inputs)
    A = {n: nc.dram_tensor(n, a.shape, mybir.dt.from_np(a.dtype), kind="ExternalInput").ap() for n, a in arrays.items()}
    for n, shape in _OUTS:
        A[n] = nc.dram_tensor(n, shape, F32, kind="ExternalOutput").ap()
    scratch(nc, A)
    program(nc, A)
    g = _run(nc, [arrays], core_ids=[0]).results[0]
    win = (1, -1, WIN, NKV, HD)
    return (g["y"][:NP].reshape(1, NP, DM), g["y"][NP:].reshape(NS, 1, DM),
            g["win_k_p"].reshape(win), g["win_v_p"].reshape(win), g["wkv_p"].reshape(1, 1, NH, HD, HD), g["shift"][0:1].reshape(1, 1, -1),
            g["win_k_s"].reshape(win), g["win_v_s"].reshape(win), g["wkv_s"].reshape(1, NS, NH, HD, HD), g["shift"][1:].reshape(1, NS, -1))
```
